# Optimizing a Trainium2 kernel written in Bass

```python
import math
import jax
import jax.numpy as jnp
from jax import lax
import numpy as np
import jax, jax.numpy as jnp

D_MODEL = 1024
BATCH = 1
SEQ = 256
DEPTH = 1

MEM_LEN = 256
MIX_W = 512
N_BRANCH = 3
CONV_K = 3
SB_HEADS = 8
SB_HEAD_DIM = MIX_W // SB_HEADS
SB_BLOCK = 128
RWKV_HEADS = 8
RWKV_HEAD = MIX_W // RWKV_HEADS
DECAY_LORA = 64
ICLR_LORA = 64
GATE_LORA = 128
VRES_LORA = 32
DECAY_SCALE = math.exp(-0.5)
CA_HEADS = 4
CA_HEAD_DIM = D_MODEL // CA_HEADS
FFN_DIM = 2816
FFN_CONV_K = 3
RMS_EPS = 1e-6
GN_EPS = 64e-5

CONV_COLS = 3 * MIX_W
SB_COLS = 3 * MIX_W
GATE_COLS = N_BRANCH * D_MODEL
RWKV_COLS = 3 * MIX_W + DECAY_LORA + ICLR_LORA + GATE_LORA
COMB_COLS = CONV_COLS + SB_COLS + GATE_COLS + RWKV_COLS
OFF_SB = CONV_COLS
OFF_GATE = OFF_SB + SB_COLS
OFF_RWKV = OFF_GATE + GATE_COLS


def rms_norm(x, g):
    xf = x.astype(jnp.float32)
    y = xf * lax.rsqrt(jnp.mean(xf * xf, axis=-1, keepdims=True) + RMS_EPS)
    return (y * g.astype(jnp.float32)).astype(x.dtype)

def causal_dwconv(x, w):
    c = x.shape[-1]
    return lax.conv_general_dilated(
        x, w[:, None, :].astype(x.dtype), window_strides=(1,),
        padding=[(w.shape[0] - 1, 0)], dimension_numbers=("NWC", "WIO", "NWC"),
        feature_group_count=c)

def stick_breaking_attention(q, k, v):
    s_len, dh = q.shape[2], q.shape[3]
    scale = dh ** -0.5
    outs = []
    for i in range(s_len // SB_BLOCK):
        start, end = i * SB_BLOCK, (i + 1) * SB_BLOCK
        q_blk = q[:, :, start:end]
        k_blk, v_blk = k[:, :, :end], v[:, :, :end]
        z = jnp.einsum("bhqd,bhkd->bhqk", q_blk, k_blk).astype(jnp.float32) * scale
        q_pos = start + jnp.arange(SB_BLOCK)
        k_pos = jnp.arange(end)
        mask = k_pos[None, :] < q_pos[:, None]
        log_not = jnp.where(mask, jax.nn.log_sigmoid(-z), 0.0)
        suffix = lax.cumsum(log_not, axis=3, reverse=True) - log_not
        log_w = jax.nn.log_sigmoid(z) + suffix
        att = jnp.where(mask, jnp.exp(log_w), 0.0)
        outs.append(jnp.einsum("bhqk,bhkd->bhqd", att.astype(v.dtype), v_blk))
    return jnp.concatenate(outs, axis=2)

def rwkv7_time_mix(p, mu, w0, w_lora, a0, a_lora, g_lora, k_k, k_a, r_k, lnx_w, lnx_b,
                   v_first, v0, v_lora):
    b, s, _ = p.shape
    f32 = jnp.float32
    p = p.astype(f32)
    prev = jnp.pad(p, ((0, 0), (1, 0), (0, 0)))[:, :-1]
    p = p + mu.astype(f32) * (prev - p)
    w_ = MIX_W
    r, k, v = p[..., :w_], p[..., w_:2 * w_], p[..., 2 * w_:3 * w_]
    o = 3 * w_
    xw = p[..., o:o + DECAY_LORA]; o += DECAY_LORA
    xa = p[..., o:o + ICLR_LORA]; o += ICLR_LORA
    xg = p[..., o:o + GATE_LORA]; o += GATE_LORA
    log_decay = -DECAY_SCALE * jax.nn.sigmoid(w0 + jnp.tanh(xw) @ w_lora)
    a = jax.nn.sigmoid(a0 + xa @ a_lora)
    if v0 is None:
        v_first = v
    else:
        xv = p[..., o:o + VRES_LORA]
        v = v + (v_first - v) * jax.nn.sigmoid(v0 + xv @ v_lora)
    g = jax.nn.sigmoid(xg) @ g_lora

    def heads(t):
        return t.reshape(b, s, RWKV_HEADS, RWKV_HEAD)

    kk = heads(k * k_k)
    kk = kk / jnp.maximum(jnp.linalg.norm(kk, axis=-1, keepdims=True), 1e-12)
    k = k * (1.0 + (a - 1.0) * k_a)
    rh, kh, vh, ah, wh = heads(r), heads(k), heads(v), heads(a), heads(jnp.exp(log_decay))

    def step(state, inp):
        r_t, w_t, k_t, v_t, kk_t, a_t = inp
        sa = jnp.einsum("bhvk,bhk->bhv", state, kk_t)
        state = (state * w_t[:, :, None, :]
                 - sa[..., None] * (kk_t * a_t)[:, :, None, :]
                 + v_t[..., None] * k_t[:, :, None, :])
        return state, jnp.einsum("bhvk,bhk->bhv", state, r_t)

    xs = tuple(jnp.moveaxis(t, 1, 0) for t in (rh, wh, kh, vh, kk, ah))
    state0 = jnp.zeros((b, RWKV_HEADS, RWKV_HEAD, RWKV_HEAD), f32)
    _, out = lax.scan(step, state0, xs)
    out = jnp.moveaxis(out, 0, 1)
    mean = jnp.mean(out, axis=-1, keepdims=True)
    var = jnp.mean(jnp.square(out - mean), axis=-1, keepdims=True)
    out = ((out - mean) * lax.rsqrt(var + GN_EPS)).reshape(b, s, w_) * lnx_w + lnx_b
    bonus = (jnp.sum(rh * kh * r_k, axis=-1, keepdims=True) * vh).reshape(b, s, w_)
    return (out + bonus) * g, v_first

def hybrid_token_mixer(xn, w_comb, conv_w, mu_rwkv, w0, w_lora, a0, a_lora, g_lora, k_k, k_a,
                       r_k, lnx_w, lnx_b, branch_proj, gate_b, w_mix_out, v_first, vres):
    b, s, _ = xn.shape
    mu = mu_rwkv
    v0 = v_lora = None
    if vres is not None:
        w_vres, mu_vres, v0, v_lora = vres
        w_comb = jnp.concatenate([w_comb, w_vres], axis=1)
        mu = jnp.concatenate([mu_rwkv, mu_vres], axis=0)
    proj = xn @ w_comb

    c_b, c_c, c_x = jnp.split(proj[..., :OFF_SB], 3, axis=-1)
    y_conv = c_b * causal_dwconv(c_c * c_x, conv_w)

    q, k, v = jnp.split(proj[..., OFF_SB:OFF_GATE], 3, axis=-1)

    def to_heads(t):
        return t.reshape(b, s, SB_HEADS, SB_HEAD_DIM).transpose(0, 2, 1, 3)

    y_sb = stick_breaking_attention(to_heads(q), to_heads(k), to_heads(v))
    y_sb = y_sb.transpose(0, 2, 1, 3).reshape(b, s, MIX_W)

    y_rwkv, v_first = rwkv7_time_mix(proj[..., OFF_RWKV:], mu, w0, w_lora, a0, a_lora, g_lora,
                                     k_k, k_a, r_k, lnx_w, lnx_b, v_first, v0, v_lora)

    gates = jax.nn.sigmoid(
        proj[..., OFF_GATE:OFF_RWKV].reshape(b, s, N_BRANCH, D_MODEL).astype(jnp.float32)
        + gate_b).astype(xn.dtype)
    ys = jnp.stack([y_conv.astype(xn.dtype), y_sb.astype(xn.dtype), y_rwkv.astype(xn.dtype)],
                   axis=2)
    branches = jnp.einsum("bsnc,ncd->bsnd", ys, branch_proj)
    merged = jnp.einsum("bsnd,bsnd->bsd", gates, branches)
    return merged @ w_mix_out, v_first

def memory_cross_attention(hn, mem_n, wq, wkv, wo):
    b, s, _ = hn.shape
    m = mem_n.shape[1]
    q = (hn @ wq).reshape(b, s, CA_HEADS, CA_HEAD_DIM)
    k, v = jnp.split(mem_n @ wkv, 2, axis=-1)
    k = k.reshape(b, m, CA_HEADS, CA_HEAD_DIM)
    v = v.reshape(b, m, CA_HEADS, CA_HEAD_DIM)
    scores = jnp.einsum("bshd,bmhd->bhsm", q, k).astype(jnp.float32) * (CA_HEAD_DIM ** -0.5)
    probs = jax.nn.softmax(scores, axis=-1).astype(v.dtype)
    out = jnp.einsum("bhsm,bmhd->bshd", probs, v).reshape(b, s, D_MODEL)
    return out @ wo

def conv_ffn(hn, w_up, conv_w, conv_b, w_down):
    u = causal_dwconv(hn @ w_up, conv_w) + conv_b
    gate, val = jnp.split(u, 2, axis=-1)
    return (jax.nn.silu(gate) * val) @ w_down

def first_inputs(seed: int = 0) -> dict:
    key = jax.random.key(seed)
    ks = iter(jax.random.split(key, 48))

    def nrm(shape, scale):
        return jax.random.normal(next(ks), shape, jnp.float32) * scale

    def gain(shape):
        return 1.0 + nrm(shape, 0.02)

    L, Lv, D, W, F = DEPTH, DEPTH - 1, D_MODEL, MIX_W, FFN_DIM
    return {
        "x": nrm((BATCH, SEQ, D), 1.0),
        "mem": nrm((BATCH, MEM_LEN, D), 1.0),
        "norm_mix": gain((L, D)),
        "w_comb": nrm((L, D, COMB_COLS), D ** -0.5),
        "conv_w": nrm((L, CONV_K, W), 0.5),
        "mu_rwkv": jax.random.uniform(next(ks), (L, RWKV_COLS), jnp.float32),
        "w0": 0.5 + nrm((L, W), 0.5),
        "w_lora": nrm((L, DECAY_LORA, W), 0.1),
        "a0": nrm((L, W), 0.3),
        "a_lora": nrm((L, ICLR_LORA, W), 0.1),
        "g_lora": nrm((L, GATE_LORA, W), GATE_LORA ** -0.5),
        "k_k": 1.0 + nrm((L, W), 0.1),
        "k_a": 1.0 + nrm((L, W), 0.1),
        "r_k": nrm((L, RWKV_HEADS, RWKV_HEAD), 0.1),
        "lnx_w": gain((L, W)),
        "lnx_b": nrm((L, W), 0.02),
        "w_vres": nrm((Lv, D, VRES_LORA), D ** -0.5),
        "mu_vres": jax.random.uniform(next(ks), (Lv, VRES_LORA), jnp.float32),
        "v0": nrm((Lv, W), 0.3),
        "v_lora": nrm((Lv, VRES_LORA, W), 0.1),
        "branch_proj": nrm((L, N_BRANCH, W, D), W ** -0.5),
        "gate_b": nrm((L, N_BRANCH, D), 0.01),
        "w_mix_out": nrm((L, D, D), D ** -0.5),
        "norm_ca": gain((L, D)),
        "norm_mem": gain((L, D)),
        "ca_wq": nrm((L, D, D), D ** -0.5),
        "ca_wkv": nrm((L, D, 2 * D), D ** -0.5),
        "ca_wo": nrm((L, D, D), D ** -0.5),
        "norm_ffn": gain((L, D)),
        "ffn_up": nrm((L, D, 2 * F), D ** -0.5),
        "ffn_conv_w": nrm((L, FFN_CONV_K, 2 * F), 0.5),
        "ffn_conv_b": nrm((L, 2 * F), 0.02),
        "ffn_down": nrm((L, F, D), F ** -0.5),
        "norm_final": gain((D,)),
    }

def first_block(x, mem, norm_mix, w_comb, conv_w, mu_rwkv, w0, w_lora, a0, a_lora, g_lora, k_k,
              k_a, r_k, lnx_w, lnx_b, w_vres, mu_vres, v0, v_lora, branch_proj, gate_b,
              w_mix_out, norm_ca, norm_mem, ca_wq, ca_wkv, ca_wo, norm_ffn, ffn_up, ffn_conv_w,
              ffn_conv_b, ffn_down, norm_final):
    h = x
    v_first = None
    for l in range(DEPTH):
        vres = None if l == 0 else (w_vres[l - 1], mu_vres[l - 1], v0[l - 1], v_lora[l - 1])
        mix, v_first = hybrid_token_mixer(
            rms_norm(h, norm_mix[l]), w_comb[l], conv_w[l], mu_rwkv[l], w0[l], w_lora[l], a0[l],
            a_lora[l], g_lora[l], k_k[l], k_a[l], r_k[l], lnx_w[l], lnx_b[l], branch_proj[l],
            gate_b[l], w_mix_out[l], v_first, vres)
        h = h + mix
        h = h + memory_cross_attention(rms_norm(h, norm_ca[l]), rms_norm(mem, norm_mem[l]),
                                       ca_wq[l], ca_wkv[l], ca_wo[l])
        h = h + conv_ffn(rms_norm(h, norm_ffn[l]), ffn_up[l], ffn_conv_w[l], ffn_conv_b[l],
                         ffn_down[l])
    return rms_norm(h, norm_final)


DEPTH_2 = 2

N_EVEN = (DEPTH_2 + 1) // 2
N_ODD = DEPTH_2 // 2
D_PLE = 256
D_FF = 2816
EPS = 1e-6
N_NORMS = 5
NEG_BIG = -1e30
F_MIN = 1e-6
LB_MAX = 0.999

A_HEADS = 8
A_HEAD_DIM = 64
A_WIDTH = A_HEADS * A_HEAD_DIM
A_CHUNK = 128
B_HEADS = 4
B_KEY_DIM = 128
B_VAL_DIM = 128
B_KW = B_HEADS * B_KEY_DIM
B_VW = B_HEADS * B_VAL_DIM
B_CHUNK = 64
EVEN_IN = 2 * A_WIDTH + 2 * B_KW + 2 * B_VW
EVEN_OUT = A_WIDTH + B_VW
C_HEADS = 8
C_NOPE = 128
C_ROPE = 64
C_V = 128
C_QK = C_NOPE + C_ROPE
Q_LORA = 384
KV_LORA = 256
ODD_IN = Q_LORA + KV_LORA + C_ROPE
ATTN_BLOCK = 128
ROPE_THETA = 10000.0
ATTN_SCALE = C_QK ** -0.5


def rms_norm_2(x, g):
    x32 = x.astype(jnp.float32)
    y = x32 * lax.rsqrt(jnp.mean(x32 * x32, axis=-1, keepdims=True) + EPS)
    return (y * g.astype(jnp.float32)).astype(x.dtype)

def swiglu(h, w_gate, w_up, w_down):
    return (jax.nn.silu(h @ w_gate) * (h @ w_up)) @ w_down

def gmlp_spatial(u, v, v_norm, w_s, b_s):
    bsz, seq = u.shape[:2]
    n_chunks = seq // A_CHUNK
    v = rms_norm_2(v, v_norm)
    vc = v.reshape(bsz, n_chunks, A_CHUNK, A_HEADS, A_HEAD_DIM)
    causal = jnp.tril(jnp.ones((A_CHUNK, A_CHUNK), dtype=bool))
    w = jnp.where(causal[None], w_s, 0.0).astype(vc.dtype)
    mixed = jnp.einsum('hts,bcshd->bcthd', w, vc) + b_s.T[None, None, :, :, None].astype(vc.dtype)
    return u * mixed.reshape(bsz, seq, A_HEADS, A_HEAD_DIM)

def hgrn2_chunkwise(q, log_f, k, v):
    bsz, seq = q.shape[:2]
    n = seq // B_CHUNK

    def to_chunks(t):
        t = t.astype(jnp.float32).reshape(bsz, n, B_CHUNK, B_HEADS, t.shape[-1])
        return jnp.transpose(t, (1, 0, 3, 2, 4))

    qc, kc, vc = to_chunks(q), to_chunks(k), to_chunks(v)
    bc = jnp.cumsum(to_chunks(log_f), axis=3)
    causal = jnp.tril(jnp.ones((B_CHUNK, B_CHUNK), dtype=bool))[:, :, None]

    def step(state, xs):
        q_, k_, v_, b_ = xs
        diff = b_[:, :, :, None, :] - b_[:, :, None, :, :]
        decay = jnp.exp(jnp.where(causal, diff, NEG_BIG))
        scores = jnp.einsum('bhtd,bhtsd->bhts', q_, decay * k_[:, :, None, :, :])
        o = jnp.einsum('bhts,bhse->bhte', scores, v_)
        o = o + jnp.einsum('bhtd,bhde->bhte', q_ * jnp.exp(b_), state)
        b_last = b_[:, :, -1:, :]
        state = jnp.exp(b_last)[:, :, 0, :, None] * state + jnp.einsum(
            'bhsd,bhse->bhde', k_ * jnp.exp(b_last - b_), v_)
        return state, o

    state0 = jnp.zeros((bsz, B_HEADS, B_KEY_DIM, B_VAL_DIM), jnp.float32)
    _, oc = lax.scan(step, state0, (qc, kc, vc, bc))
    return jnp.transpose(oc, (1, 0, 3, 2, 4)).reshape(bsz, seq, B_HEADS, B_VAL_DIM)

def even_mixer(h, w_in, v_norm, w_s, b_s, lb, out_norm, w_out):
    bsz, seq, _ = h.shape
    z = h @ w_in
    a_u, a_v, b_q, b_f, b_i, b_g = jnp.split(
        z, [A_WIDTH, 2 * A_WIDTH, 2 * A_WIDTH + B_KW, 2 * A_WIDTH + 2 * B_KW,
            2 * A_WIDTH + 2 * B_KW + B_VW], axis=-1)
    a_u = jax.nn.gelu(a_u).reshape(bsz, seq, A_HEADS, A_HEAD_DIM)
    a_v = jax.nn.gelu(a_v).reshape(bsz, seq, A_HEADS, A_HEAD_DIM)
    a_out = gmlp_spatial(a_u, a_v, v_norm, w_s, b_s).reshape(bsz, seq, A_WIDTH)
    zf = b_f.astype(jnp.float32)
    f = lb + (1.0 - lb) * jax.nn.sigmoid(zf)
    log_f = jnp.log(jnp.maximum(f, F_MIN))
    k = 1.0 - f
    o = hgrn2_chunkwise(b_q.reshape(bsz, seq, B_HEADS, B_KEY_DIM),
                        log_f.reshape(bsz, seq, B_HEADS, B_KEY_DIM),
                        k.reshape(bsz, seq, B_HEADS, B_KEY_DIM),
                        b_i.reshape(bsz, seq, B_HEADS, B_VAL_DIM))
    o = rms_norm_2(o, out_norm).astype(h.dtype) * jax.nn.silu(b_g.reshape(bsz, seq, B_HEADS, B_VAL_DIM))
    mixed = jnp.concatenate([a_out, o.reshape(bsz, seq, B_VW)], axis=-1)
    return mixed @ w_out

def rotate_half(x, cos, sin):
    x1, x2 = jnp.split(x, 2, axis=-1)
    return jnp.concatenate([x1 * cos - x2 * sin, x2 * cos + x1 * sin], axis=-1).astype(x.dtype)

def mla_mixer(h, positions, w_in, q_a_norm, kv_a_norm, w_q_b, w_kv_b, q_norm, k_norm, w_out):
    bsz, seq, _ = h.shape
    z = h @ w_in
    c_q, c_kv, k_rope = jnp.split(z, [Q_LORA, Q_LORA + KV_LORA], axis=-1)
    q = (rms_norm_2(c_q, q_a_norm) @ w_q_b).reshape(bsz, seq, C_HEADS, C_QK)
    kv = (rms_norm_2(c_kv, kv_a_norm) @ w_kv_b).reshape(bsz, seq, C_HEADS, C_NOPE + C_V)
    k_nope, v = jnp.split(kv, [C_NOPE], axis=-1)
    k_rope = jnp.broadcast_to(k_rope[:, :, None, :], (bsz, seq, C_HEADS, C_ROPE))
    k = jnp.concatenate([k_nope, k_rope], axis=-1)
    q = rms_norm_2(q, q_norm)
    k = rms_norm_2(k, k_norm)
    inv_freq = ROPE_THETA ** (-jnp.arange(0, C_ROPE, 2, dtype=jnp.float32) / C_ROPE)
    ang = positions.astype(jnp.float32)[..., None] * inv_freq
    cos = jnp.cos(ang)[:, :, None, :]
    sin = jnp.sin(ang)[:, :, None, :]
    q = jnp.concatenate([q[..., :C_NOPE], rotate_half(q[..., C_NOPE:], cos, sin)], axis=-1)
    k = jnp.concatenate([k[..., :C_NOPE], rotate_half(k[..., C_NOPE:], cos, sin)], axis=-1)
    q = jnp.transpose(q, (0, 2, 1, 3))
    k = jnp.transpose(k, (0, 2, 1, 3))
    v = jnp.transpose(v, (0, 2, 1, 3))
    n_blocks = seq // ATTN_BLOCK
    q_blocks = jnp.transpose(q.reshape(bsz, C_HEADS, n_blocks, ATTN_BLOCK, C_QK), (2, 0, 1, 3, 4))
    key_pos = jnp.arange(seq)

    def attend(args):
        qb, start = args
        s = jnp.einsum('bhqd,bhkd->bhqk', qb, k).astype(jnp.float32) * ATTN_SCALE
        q_pos = start + jnp.arange(ATTN_BLOCK)
        s = jnp.where(key_pos[None, :] <= q_pos[:, None], s, NEG_BIG)
        pr = jax.nn.softmax(s, axis=-1).astype(v.dtype)
        return jnp.einsum('bhqk,bhkd->bhqd', pr, v)

    out = lax.map(attend, (q_blocks, jnp.arange(n_blocks) * ATTN_BLOCK))
    out = jnp.transpose(out, (1, 0, 3, 2, 4)).reshape(bsz, seq, C_HEADS * C_V)
    return out @ w_out

def per_layer_embedding(h, p_i, w_gate, w_proj, post_norm):
    return rms_norm_2(jax.nn.sigmoid(h @ w_gate) * (p_i @ w_proj), post_norm)

def second_inputs(seed: int = 0) -> dict:
    key = jax.random.key(seed)
    ks = jax.random.split(key, 32)
    f32 = jnp.float32

    def nrm(k, shape, fan_in):
        return jax.random.normal(k, shape, f32) * (fan_in ** -0.5)

    def gain(k, shape):
        return 1.0 + 0.02 * jax.random.normal(k, shape, f32)

    x = jax.random.normal(ks[0], (BATCH, SEQ, D_MODEL), f32)
    p = jax.random.normal(ks[1], (DEPTH_2, BATCH, SEQ, D_PLE), f32)
    offset = jax.random.randint(ks[2], (BATCH, 1), 0, 1024, dtype=jnp.int32)
    positions = offset + jnp.arange(SEQ, dtype=jnp.int32)[None, :]
    return {
        'x': x,
        'p': p,
        'positions': positions,
        'norm_gains': gain(ks[3], (DEPTH_2, N_NORMS, D_MODEL)),
        'ffn_w_gate': nrm(ks[4], (DEPTH_2, 2, D_MODEL, D_FF), D_MODEL),
        'ffn_w_up': nrm(ks[5], (DEPTH_2, 2, D_MODEL, D_FF), D_MODEL),
        'ffn_w_down': nrm(ks[6], (DEPTH_2, 2, D_FF, D_MODEL), D_FF),
        'ple_w_gate': nrm(ks[7], (DEPTH_2, D_MODEL, D_MODEL), D_MODEL),
        'ple_w_proj': nrm(ks[8], (DEPTH_2, D_PLE, D_MODEL), D_PLE),
        'even_w_in': nrm(ks[9], (N_EVEN, D_MODEL, EVEN_IN), D_MODEL),
        'gmlp_v_norm': gain(ks[10], (N_EVEN, A_HEADS, A_HEAD_DIM)),
        'gmlp_w_s': nrm(ks[11], (N_EVEN, A_HEADS, A_CHUNK, A_CHUNK), A_CHUNK),
        'gmlp_b_s': 1.0 + 0.01 * jax.random.normal(ks[12], (N_EVEN, A_HEADS, A_CHUNK), f32),
        'hgrn_lb_raw': 0.5 * jax.random.normal(ks[13], (N_EVEN, B_KW), f32),
        'hgrn_out_norm': gain(ks[14], (N_EVEN, B_VAL_DIM)),
        'even_w_out': nrm(ks[15], (N_EVEN, EVEN_OUT, D_MODEL), EVEN_OUT),
        'mla_w_in': nrm(ks[16], (N_ODD, D_MODEL, ODD_IN), D_MODEL),
        'mla_q_a_norm': gain(ks[17], (N_ODD, Q_LORA)),
        'mla_kv_a_norm': gain(ks[18], (N_ODD, KV_LORA)),
        'mla_w_q_b': nrm(ks[19], (N_ODD, Q_LORA, C_HEADS * C_QK), Q_LORA),
        'mla_w_kv_b': nrm(ks[20], (N_ODD, KV_LORA, C_HEADS * (C_NOPE + C_V)), KV_LORA),
        'mla_q_norm': gain(ks[21], (N_ODD, C_QK)),
        'mla_k_norm': gain(ks[22], (N_ODD, C_QK)),
        'mla_w_out': nrm(ks[23], (N_ODD, C_HEADS * C_V, D_MODEL), C_HEADS * C_V),
    }

def second_block(x, p, positions, norm_gains, ffn_w_gate, ffn_w_up, ffn_w_down,
              ple_w_gate, ple_w_proj, even_w_in, gmlp_v_norm, gmlp_w_s, gmlp_b_s,
              hgrn_lb_raw, hgrn_out_norm, even_w_out, mla_w_in, mla_q_a_norm,
              mla_kv_a_norm, mla_w_q_b, mla_w_kv_b, mla_q_norm, mla_k_norm, mla_w_out):
    lb_sm = jax.nn.softmax(hgrn_lb_raw.astype(jnp.float32), axis=0)
    lower_bounds = jnp.clip(jnp.cumsum(lb_sm, axis=0) - lb_sm[0], 0.0, LB_MAX)
    for i in range(DEPTH_2):
        g = norm_gains[i]
        x = x + 0.5 * swiglu(rms_norm_2(x, g[0]), ffn_w_gate[i, 0], ffn_w_up[i, 0], ffn_w_down[i, 0])
        h = rms_norm_2(x, g[1])
        j = i // 2
        if i % 2 == 0:
            m = even_mixer(h, even_w_in[j], gmlp_v_norm[j], gmlp_w_s[j], gmlp_b_s[j],
                           lower_bounds[j], hgrn_out_norm[j], even_w_out[j])
        else:
            m = mla_mixer(h, positions, mla_w_in[j], mla_q_a_norm[j], mla_kv_a_norm[j],
                          mla_w_q_b[j], mla_w_kv_b[j], mla_q_norm[j], mla_k_norm[j], mla_w_out[j])
        x = x + m
        x = x + 0.5 * swiglu(rms_norm_2(x, g[2]), ffn_w_gate[i, 1], ffn_w_up[i, 1], ffn_w_down[i, 1])
        x = x + per_layer_embedding(rms_norm_2(x, g[3]), p[i], ple_w_gate[i], ple_w_proj[i], g[4])
    return x


def setup_inputs(seed=0):
    out = dict(first_inputs(seed))
    for name, value in second_inputs(seed + 1).items():
        if name != "x":
            out[name + "_2"] = value
    return out


def reference(
    x, mem, norm_mix, w_comb, conv_w, mu_rwkv, w0, w_lora, a0, a_lora, g_lora, k_k, k_a, r_k,
    lnx_w, lnx_b, w_vres, mu_vres, v0, v_lora, branch_proj, gate_b, w_mix_out, norm_ca,
    norm_mem, ca_wq, ca_wkv, ca_wo, norm_ffn, ffn_up, ffn_conv_w, ffn_conv_b, ffn_down,
    norm_final, p_2, positions_2, norm_gains_2, ffn_w_gate_2, ffn_w_up_2, ffn_w_down_2,
    ple_w_gate_2, ple_w_proj_2, even_w_in_2, gmlp_v_norm_2, gmlp_w_s_2, gmlp_b_s_2,
    hgrn_lb_raw_2, hgrn_out_norm_2, even_w_out_2, mla_w_in_2, mla_q_a_norm_2, mla_kv_a_norm_2,
    mla_w_q_b_2, mla_w_kv_b_2, mla_q_norm_2, mla_k_norm_2, mla_w_out_2,
):
    x = first_block(
        x, mem, norm_mix, w_comb, conv_w, mu_rwkv, w0, w_lora, a0, a_lora, g_lora, k_k, k_a,
        r_k, lnx_w, lnx_b, w_vres, mu_vres, v0, v_lora, branch_proj, gate_b, w_mix_out, norm_ca,
        norm_mem, ca_wq, ca_wkv, ca_wo, norm_ffn, ffn_up, ffn_conv_w, ffn_conv_b, ffn_down,
        norm_final,
    )
    return second_block(
        x, p_2, positions_2, norm_gains_2, ffn_w_gate_2, ffn_w_up_2, ffn_w_down_2, ple_w_gate_2,
        ple_w_proj_2, even_w_in_2, gmlp_v_norm_2, gmlp_w_s_2, gmlp_b_s_2, hgrn_lb_raw_2,
        hgrn_out_norm_2, even_w_out_2, mla_w_in_2, mla_q_a_norm_2, mla_kv_a_norm_2, mla_w_q_b_2,
        mla_w_kv_b_2, mla_q_norm_2, mla_k_norm_2, mla_w_out_2,
    )


_drawn_inputs = setup_inputs


def setup_inputs(seed=0):
    import zlib

    import numpy as np

    out = dict(_drawn_inputs(seed))
    spreads = {}
    factors = {'norm_mix': 2.784,
     'k_k': 8.0,
     'lnx_w': 8.0,
     'lnx_b': 8.0,
     'gate_b': 8.0,
     'norm_ca': 8.0,
     'norm_mem': 8.0,
     'norm_ffn': 5.45,
     'ffn_conv_b': 4.936,
     'norm_final': 2.819,
     'gmlp_v_norm_2': 8.0,
     'gmlp_b_s_2': 8.0,
     'hgrn_out_norm_2': 8.0,
     'mla_q_a_norm_2': 8.0,
     'mla_kv_a_norm_2': 8.0,
     'mla_q_norm_2': 8.0,
     'mla_k_norm_2': 8.0}
    for name, (base, spread) in spreads.items():
        noise = np.random.default_rng([zlib.crc32(name.encode()), seed]).standard_normal(out[name].shape)
        drawn = base * np.exp(spread * noise) if base else spread * noise
        out[name] = jnp.asarray(drawn.astype(out[name].dtype))
    for name, factor in factors.items():
        out[name] = (out[name] * factor).astype(out[name].dtype)
    return out
```

```python
from contextlib import ExitStack

import numpy as np
import concourse.bass as bass
from concourse import mybir

F32 = mybir.dt.float32
F32R = mybir.dt.float32r
I32 = mybir.dt.int32
ALU = mybir.AluOpType
ACT = mybir.ActivationFunctionType
AX = mybir.AxisListType

P = 128
T = 256
D = 1024
KT = D // P
W = 512
WT = W // P
HEADS = 8
HD = 64
F = 2816
FP = F // (2 * P)
SLAB = 16 * P
CH = 64
EPS = 1e-6
GN_EPS = 64e-5
DECAY_SCALE = float(np.exp(-0.5))
ROPE_THETA = 10000.0
NEG_BIG = -1e30

STREAM = [
    ("conv", 6), ("sb_qk", 4), ("sb_v", 2), ("rwkv", 7), ("gates", 12), ("branch", 6), ("mix_out", 4),
    ("ca_k", 4), ("ca_v", 4), ("ca_q", 4), ("ca_o", 4), ("ffn_c", 33),
    ("ffn_0", 33), ("even_in", 8), ("even_v", 4), ("even_out", 4), ("ffn_1", 33), ("ple_0", 5),
    ("ffn_2", 33), ("mla_in", 3), ("mla_q", 3), ("mla_kv", 2), ("mla_out", 4), ("ffn_3", 33), ("ple_1", 5),
]
START = {}
N_SLABS = 0
for _name, _n in STREAM:
    START[_name] = N_SLABS
    N_SLABS += _n

COLUMNS = [
    ("norm_mix", 8), ("conv_w", 12), ("mu", 14), ("w0", 4), ("a0", 4), ("k_k", 4), ("k_a", 4), ("r_k", 4),
    ("lnx_w", 4), ("lnx_b", 4), ("gate_b", 24), ("norm_ca", 8), ("norm_mem", 8), ("norm_ffn", 8),
    ("ffn_conv_w", 132), ("ffn_conv_b", 44), ("norm_final", 8), ("norm_gains", 80), ("hgrn_lb", 4),
    ("hgrn_out_norm", 1), ("q_a_norm", 3), ("kv_a_norm", 2), ("q_nope", 1), ("q_rope", 1), ("k_nope", 1),
    ("k_rope", 1), ("inv_freq", 1),
]
COL = {}
N_COLS = 0
for _name, _n in COLUMNS:
    COL[_name] = N_COLS
    N_COLS += _n

LEVELS = [1, 2, 4, 8, 16, 32, 64]
TABLES = ["identity", "ones", "head_ones", "before", "before_chunk", "upto_chunk", "upto", "past", "future_penalty",
          "after", "first_half", "second_half", "swap"] + \
    [f"level{b}" for b in LEVELS]


def constant_tables():
    s, t = np.meshgrid(np.arange(P), np.arange(P), indexing="ij")
    tab = {
        "identity": s == t,
        "ones": np.ones((P, P)),
        "head_ones": s // HD == t // HD,
        "before": s < t,
        "before_chunk": (s < t) & (s // CH == t // CH),
        "upto_chunk": (s <= t) & (s // CH == t // CH),
        "upto": s <= t,
        "past": s >= t,
        "future_penalty": np.where(s >= t, 0.0, NEG_BIG),
        "first_half": s < HD,
        "second_half": s >= HD,
        "after": s > t,
    }
    half = HD // 2
    swap = np.zeros((P, P))
    for base in (0, HD):
        for j in range(half):
            swap[base + half + j, base + j] = -1.0
            swap[base + j, base + half + j] = 1.0
    tab["swap"] = swap
    for b in LEVELS:
        tab[f"level{b}"] = (s // (2 * b) == t // (2 * b)) & (s % (2 * b) < b) & (t % (2 * b) >= b)
    return np.ascontiguousarray(np.stack([tab[n].astype(np.float32) for n in TABLES], axis=1))


def program(nc, ins, out_t):
    ctx = ExitStack()
    with ctx:
        def sb(name, shape, dt=F32):
            return ctx.enter_context(nc.sbuf_tensor(name, shape, dt))

        sems = {}

        def sem(name):
            if name not in sems:
                sems[name] = ctx.enter_context(nc.semaphore(name))
            return sems[name]

        ring_raw = sb("ring_raw", [P, 3, SLAB])
        ring_hi = sb("ring_hi", [P, 3, SLAB], F32R)
        ring_lo = sb("ring_lo", [P, 3, SLAB], F32R)
        XH = sb("operand_hi", [P, 20, T], F32R)
        XL = sb("operand_lo", [P, 20, T], F32R)
        HH = sb("hidden_hi", [P, 2, T], F32R)
        HL = sb("hidden_lo", [P, 2, T], F32R)
        zeros = sb("zeros", [P, 512], F32R)
        H = sb("residual", [P, KT, T])
        prm = sb("params", [P, N_COLS])
        tab = sb("tables", [P, len(TABLES), P])
        root = sb("root", [P, T])
        inv = sb("inv", [P, T])
        one_minus_mu = sb("one_minus_mu", [P, 14])
        small = sb("small", [P, 64])
        U = 1024
        arena = sb("arena", [P, 16 * U])
        PS = ctx.enter_context(nc.psum_tensor("PS", [P, 8, 512], F32))

        def area(start, tiles, width=T):
            a = int(start * U)
            return arena[:, a:a + tiles * width].rearrange("p (n t) -> p n t", t=width)

        def col(name, i=0, n=1):
            return prm[:, COL[name] + i:COL[name] + i + n]

        def table(name):
            return tab[:, TABLES.index(name), :]

        def per_head(name, n=4):
            return table(name).unsqueeze(1).to_broadcast([P, n, P])

        def bank(b, n=1):
            return PS[:, b:b + n, :].rearrange("p b c -> p (b c)")

        def tiles_of(b, n):
            return bank(b, (n + 1) // 2).rearrange("p (n t) -> p n t", t=T)[:, 0:n, :]

        def flat(ap):
            return ap.rearrange("p n t -> p (n t)")

        squares = area(12, 8)
        silu_out, hidden = flat(area(14, 2)), flat(area(14.5, 2))
        conv_acc = area(15, 2)
        conv_acc2 = area(15.5, 2)
        conv_in = area(0, 12)
        conv_u, conv_y = area(3, 4), area(4, 4)
        sbq = area(5, 8)
        sbv = area(7, 2, W)
        sb_z = [flat(area(8 + 1.5 * q, 6)) for q in range(2)]
        sb_w = [flat(area(11 + 1.5 * q, 6)) for q in range(2)]
        rp = area(0, 14)
        R_, K_, V_, LORA = rp[:, 0:4], rp[:, 4:8], rp[:, 8:12], rp[:, 12:14]
        A_, G_, KK, BN = (area(3.5 + i, 4) for i in range(4))
        LW, LC, EP, TM = (area(7.5 + i, 4) for i in range(4))
        lora_w = area(11.5, 2, W)
        Vt, Kt, Bt = area(7.5, 1, W), area(8, 1, W), area(8.5, 1, W)
        ZP = area(9, 8, P)
        Xm, Ym, Yt, Fm, Xb = (area(10 + i, 8, P) for i in range(5))
        MT = area(15, 4, HD)
        state = area(15.25, 4, HD)
        chunk_decay = small[:, 0:16].rearrange("p (f c) -> p f c", c=4)
        gates = area(0, 24)
        merged, gated = area(6, 8), area(8, 4)
        mem = area(0, 8)
        ca_k, ca_v, ca_q = area(2, 8), area(4, 2, D), area(6, 8)
        probs, probs_t = area(8, 8), area(10, 8)
        ev = area(0, 16)
        AU, BQ, BF, BG = ev[:, 0:4], ev[:, 4:8], ev[:, 8:12], ev[:, 12:16]
        AV, BI = area(4, 2, W), area(5, 2, W)
        spatial_b = arena[0:1, 6 * U:7 * U]
        KB, BC = area(6, 4), area(7, 4)
        DIF = [area(8, 4), area(9, 4)]
        XM = [area(10, 4), area(11, 4)]
        AT = area(12, 8, P)
        AC, AM = area(13, 4, P), area(13.5, 4, P)
        spatial_w = area(14, 8, P)
        v_gain = area(15, 1, W)
        ple_in = area(14, 2)
        ple_p, ple_g = area(0, 8), area(2, 8)
        MI, MQ, MK, MV = area(0, 6), area(1.5, 12), area(4.5, 8), area(6.5, 2, D)
        RQ, RK, KRP = area(8.5, 8), area(10.5, 8), area(12.5, 8)
        msq = area(12.5, 12)
        cosines, sines = area(15.5, 1), area(15.75, 1)
        ang, turns = area(8.5, 1), area(8.75, 1)
        S0, S1 = area(8.5, 8, P), area(9.5, 8)
        PT0, PT1 = area(11.5, 8), area(13.5, 8, P)

        landed = [sem(f"landed{s}") for s in range(3)]
        hi_split, lo_split = sem("hi_split"), sem("lo_split")
        multiplied = sem("multiplied")

        def place(g0, i=0):
            return g0 % 3, i + g0 // 3, i * 3 + g0

        block = ctx.enter_context(nc.Block())

        @block.sync
        def _(sp):
            stream = ins["w_stream"]
            for g in range(3):
                sp.dma_start(ring_raw[:, g, :], stream[g]).then_inc(landed[g], 16)
            turns_ = (N_SLABS - 3) // 3
            with sp.Fori(0, turns_) as i:
                for j in range(3):
                    sp.wait_ge(lo_split, i * 3 + (j + 1))
                    sp.dma_start(ring_raw[:, j, :], stream[bass.ds(i * 3 + (j + 3), 1)].squeeze(0))\
                        .then_inc(landed[j], 16)
            for g in range(3 + 3 * turns_, N_SLABS):
                sp.wait_ge(lo_split, g - 2)
                sp.dma_start(ring_raw[:, g % 3, :], stream[g]).then_inc(landed[g % 3], 16)
            sp.wait_ge(sem("residual_ready"), 12)
            sp.dma_start(out_t.rearrange("(k p) t -> p k t", p=P), H[:]).then_inc(sem("stored"), 16)
            sp.wait_ge(sem("stored"), 16)

        @block.gpsimd
        def _(pool):
            nc.gpsimd.memset(zeros[:].bitcast(F32), 0.0).then_inc(sem("zeros_ready"), 1)
            pool.dma_start(tab[:], ins["tables"]).then_inc(sem("tables_landed"), 16)
            pool.wait_ge(sem("operand_lo"), KT + 2)
            pool.dma_start(lora_w[:, 0, :], ins["wa_lora"]).then_inc(sem("lora_landed"), 16)
            pool.dma_start(lora_w[:, 1, :], ins["g_lora"]).then_inc(sem("lora_landed"), 16)
            pool.wait_ge(sem("residual_ready"), 1)
            pool.dma_start(mem, ins["mem_t"].rearrange("(k p) t -> p k t", p=P)).then_inc(sem("mem_landed"), 16)
            pool.wait_ge(sem("residual_ready"), 5)
            pool.dma_start(spatial_w, ins["spatial_t"]).then_inc(sem("spatial_landed"), 16)
            pool.dma_start(spatial_b, ins["spatial_b"]).then_inc(sem("spatial_landed"), 16)
            pool.dma_start(v_gain[:, 0, :], ins["v_gain"].to_broadcast([P, W])).then_inc(sem("spatial_landed"), 16)
            for n, after in enumerate((7, 11)):
                pool.wait_ge(sem("residual_ready"), after)
                pool.dma_start(ple_in, ins["ple_t"][n].rearrange("(k p) t -> p k t", p=P))\
                    .then_inc(sem("ple_landed"), 16)
                if n == 0:
                    pool.wait_ge(sem("residual_ready"), 9)
                    pool.dma_start(cosines.bitcast(I32)[:, 0, :], ins["positions"].to_broadcast([P, T]))\
                        .then_inc(sem("positions_landed"), 16)

        @block.tensor
        def _(pe):
            taken = [0]
            split_tiles = [0]

            def mm(out, lhs, rhs, start=True, stop=True):
                return nc.tensor.matmul(out, lhs, rhs, start=start, stop=stop, skip_group_check=True)

            def block_product(out, slot, b, xh, xl, start, stop):
                w = slice(b * P, (b + 1) * P)
                mm(out, ring_hi[:, slot, w], xh, start, False)
                mm(out, ring_hi[:, slot, w], xl, False, False)
                return mm(out, ring_lo[:, slot, w], xh, False, stop)

            def output_slab(g0, x0, out, i=0):
                slot, _, g = place(g0, i)
                pe.wait_ge(lo_split, g + 1)
                for m in range(2):
                    for k in range(KT):
                        last = block_product(out[:, m * T:(m + 1) * T], slot, m * KT + k,
                                             XH[:, x0 + k, :], XL[:, x0 + k, :], k == 0, k == KT - 1)
                last.then_inc(multiplied, 1)

            def operands(n):
                split_tiles[0] += n
                pe.wait_ge(sem("operand_lo"), split_tiles[0])

            def free_bank(i=0):
                if taken[0] >= 3:
                    pe.wait_ge(sem("output_taken"), taken[0] - 2)
                b = taken[0] % 3
                taken[0] += 1
                return b

            def project(name, x0, n):
                for j in range(n):
                    output_slab(START[name] + j, x0, bank(free_bank()))

            def project_by_token(name, x0, n):
                for j in range(n):
                    out = bank(free_bank())
                    slot, _, g = place(START[name] + j)
                    pe.wait_ge(lo_split, g + 1)
                    for tt in range(2):
                        tok = slice(tt * P, (tt + 1) * P)
                        for k in range(KT):
                            w = slice(k * T, (k + 1) * T)
                            o = out[:, tt * T:(tt + 1) * T]
                            mm(o, XH[:, x0 + k, tok], ring_hi[:, slot, w], k == 0, False)
                            mm(o, XL[:, x0 + k, tok], ring_hi[:, slot, w], False, False)
                            last = mm(o, XH[:, x0 + k, tok], ring_lo[:, slot, w], False, k == KT - 1)
                    last.then_inc(multiplied, 1)

            norms = [0]

            def norm_sum(n):
                norms[0] += 1
                pe.wait_ge(sem("norm_squared"), norms[0])
                for k in range(n):
                    last = mm(bank(7)[:, 0:T], table("ones"), squares[:, k, :], k == 0, k == n - 1)
                last.then_inc(sem("norm_summed"), 1)

            ffns = [0]

            def feed_forward(name):
                g0, n = START[name], ffns[0]
                for b in range(3, 7):
                    mm(bank(b), zeros[:, 0:P], zeros[:], True, False)
                split = sem("hidden_lo")
                gate_taken, up_taken = sem("gate_taken"), sem("up_taken")
                if n:
                    pe.wait_ge(gate_taken, n * FP)
                    pe.wait_ge(up_taken, n * FP)
                operands(KT)
                output_slab(g0, 0, bank(0))
                output_slab(g0 + 1, 0, bank(1))

                def down(at, i=0):
                    slot, _, g = place(at, i)
                    pe.wait_ge(lo_split, g + 1)
                    pe.wait_ge(split, i + (n * FP + (FP if at == g0 + 32 else 1)))
                    for k in range(2):
                        for m in range(KT):
                            last = block_product(bank(3 + m // 2)[:, m % 2 * T:(m % 2 + 1) * T], slot, k * KT + m,
                                                 HH[:, k, :], HL[:, k, :], False, False)
                    last.then_inc(multiplied, 1)

                with pe.Fori(0, FP - 1) as i:
                    pe.wait_ge(gate_taken, i + (n * FP + 1))
                    output_slab(g0 + 2, 0, bank(0), i)
                    pe.wait_ge(up_taken, i + (n * FP + 1))
                    output_slab(g0 + 3, 0, bank(1), i)
                    down(g0 + 4, i)
                down(g0 + 32)
                ffns[0] += 1

            def residual_bank(name):
                project(name, 0, 4)

            pe.wait_ge(sem("zeros_ready"), 1)
            pe.wait_ge(sem("tables_landed"), 16)
            norm_sum(KT)
            operands(KT)
            project("conv", 0, 6)
            project("sb_qk", 0, 4)
            project_by_token("sb_v", 0, 2)

            pe.wait_ge(sem("output_taken"), taken[0])
            for q in range(2):
                rows = slice(HD * q, HD * (q + 1))
                if q:
                    pe.wait_ge(sem("sb_z_taken"), q)
                for f in range(4):
                    qt, kt = sbq[rows, f, :], sbq[rows, 4 + f, :]
                    o = slice(f * P, (f + 1) * P)
                    mm(bank(0)[:, o], kt[:, 0:P], qt[:, 0:P])
                    mm(bank(1)[:, o], kt[:, 0:P], qt[:, P:T])
                    last = mm(bank(2)[:, o], kt[:, P:T], qt[:, P:T])
                last.then_inc(sem("sb_z"), 1)
            for q in range(2):
                pe.wait_ge(sem("sb_log"), q + 1)
                if q:
                    pe.wait_ge(sem("sb_logw"), q)
                z = sb_z[q]
                mm(bank(3), table("after"), z[:, 0:512])
                mm(bank(4), table("after"), z[:, 512:1024], True, False)
                mm(bank(4), table("ones"), z[:, 1024:1536], False, True)
                mm(bank(5), table("after"), z[:, 1024:1536]).then_inc(sem("sb_suffix"), 1)
            for q in range(2):
                pe.wait_ge(sem("sb_att"), q + 1)
                w = sb_w[q].rearrange("p (b f t) -> p b f t", b=3, f=4)
                for f in range(4):
                    o = bank(6 + f // 2)[HD * q:HD * (q + 1), f % 2 * T:(f % 2 + 1) * T]
                    h = slice((2 * f + q) * HD, (2 * f + q + 1) * HD)
                    mm(o[:, 0:P], sbv[:, 0, h], w[:, 0, f, :])
                    mm(o[:, P:T], sbv[:, 0, h], w[:, 1, f, :], True, False)
                    last = mm(o[:, P:T], sbv[:, 1, h], w[:, 2, f, :], False, True)
            last.then_inc(sem("sb_y"), 1)

            for j in range(7):
                output_slab(START["rwkv"] + j, 0, bank(free_bank()))
            pe.wait_ge(sem("lora_landed"), 32)
            pe.wait_ge(sem("rk_lora_in"), 1)
            pe.wait_ge(sem("output_taken"), taken[0])
            pe.wait_ge(sem("operand_lo"), KT + 2)
            for f in range(4):
                c = slice(f * P, (f + 1) * P)
                o = slice(f % 2 * T, (f % 2 + 1) * T)
                mm(bank(0 + f // 2)[:, o], lora_w[0:HD, 0, c], LORA[0:HD, 0, :])
                mm(bank(2 + f // 2)[:, o], lora_w[HD:P, 0, c], LORA[HD:P, 0, :])
                last = mm(bank(4 + f // 2)[:, o], lora_w[:, 1, c], LORA[:, 1, :])
            last.then_inc(sem("rk_lora_out"), 1)
            pe.wait_ge(sem("rk_squares"), 1)
            for h in range(2):
                last = mm(bank(6 + h), table("head_ones"), flat(TM)[:, 512 * h:512 * (h + 1)])
            last.then_inc(sem("rk_norms"), 1)
            pe.wait_ge(sem("rk_bonus_in"), 1)
            for h in range(2):
                last = mm(bank(6 + h), table("head_ones"), flat(BN)[:, 512 * h:512 * (h + 1)])
            last.then_inc(sem("rk_bonus_sums"), 1)
            pe.wait_ge(sem("rk_prep"), 1)

            def heads(q):
                return [(f, 2 * f + q) for f in range(4)]

            for tt in range(2):
                tok = slice(tt * P, (tt + 1) * P)
                if tt:
                    pe.wait_ge(sem("rk_tile_done"), 1)
                for f in range(4):
                    c = slice(f * P, (f + 1) * P)
                    nc.tensor.transpose(bank(0)[:, c], V_[:, f, tok], table("identity"))
                    nc.tensor.transpose(bank(1)[:, c], KK[:, f, tok], table("identity"))
                    nc.tensor.transpose(bank(2)[:, c], K_[:, f, tok], table("identity"))
                    last = nc.tensor.transpose(bank(3)[:, c], A_[:, f, tok], table("identity"))
                last.then_inc(sem("rk_turned"), 1)
                for q in range(2):
                    rows = slice(HD * q, HD * (q + 1))
                    for f in range(4):
                        c = slice(f * P, (f + 1) * P)
                        mm(bank(4 + q)[:, c], K_[rows, f, tok], KK[rows, f, tok])
                        last = mm(bank(6 + q)[:, c], A_[rows, f, tok], KK[rows, f, tok])
                last.then_inc(sem("rk_pairs"), 1)
                pe.wait_ge(sem("rk_masked"), tt + 1)
                pe.wait_ge(sem("rk_turned_act"), tt + 1)
                for q in range(2):
                    for f, h in heads(q):
                        last = mm(bank(0)[:, h * HD:(h + 1) * HD], Fm[:, 4 * q + f, :], Vt[:, 0, h * HD:(h + 1) * HD])
                last.then_inc(sem("rk_p"), 1)
                pe.wait_ge(sem("rk_p_taken"), tt + 1)
                for li in range(6):
                    for q in range(2):
                        n = (tt * 6 + li) * 2 + q
                        pe.wait_ge(sem("rk_x"), n + 1)
                        if li:
                            pe.wait_ge(sem("rk_y"), n - 1)
                        for f in range(4):
                            rhs = Yt[:, 4 * q + f, :] if li else table("identity")
                            last = mm(bank(1 + q)[:, f * P:(f + 1) * P], Xb[:, 4 * q + f, :], rhs)
                        last.then_inc(sem("rk_f"), 1)
                    for q in range(2):
                        n = (tt * 6 + li) * 2 + q
                        pe.wait_ge(sem("rk_f_taken"), n + 1)
                        for f in range(4):
                            c, e = slice(f * P, (f + 1) * P), 4 * q + f
                            last = mm(bank(3 + q)[:, c], Fm[:, e, :], Ym[:, e, :] if li else table("identity"))
                            if li < 5:
                                last = mm(bank(5 + q)[:, c], Ym[:, e, :] if li else table("identity"), Fm[:, e, :])
                        last.then_inc(sem("rk_dy"), 1)
                pe.wait_ge(sem("rk_y"), (tt + 1) * 12)
                for q in range(2):
                    for f, h in heads(q):
                        last = mm(bank(3 + q)[:, f * P:(f + 1) * P], Ym[:, 4 * q + f, :], ZP[:, h, :])
                last.then_inc(sem("rk_wu"), 1)
                for q in range(2):
                    rows = slice(HD * q, HD * (q + 1))
                    for f in range(4):
                        c = slice(f * P, (f + 1) * P)
                        mm(bank(5 + q)[:, c], K_[rows, f, tok], R_[rows, f, tok])
                        last = mm(bank(1 + q)[:, c], A_[rows, f, tok], R_[rows, f, tok])
                last.then_inc(sem("rk_out_pairs"), 1)
                pe.wait_ge(sem("rk_wu_taken"), tt + 1)
                pe.wait_ge(sem("rk_out_masked"), tt + 1)
                for q in range(2):
                    for f, h in heads(q):
                        e = 4 * q + f
                        mm(bank(7)[HD * q:HD * (q + 1), f * P:(f + 1) * P], Xb[:, e, 0:HD], Fm[:, e, :])
                        o = bank(3)[HD * q:HD * (q + 1), f * P:(f + 1) * P]
                        mm(o, Vt[:, 0, h * HD:(h + 1) * HD], Yt[:, e, :], True, False)
                        last = mm(o, Xb[:, e, HD:P], Fm[:, e, :], False, True)
                last.then_inc(sem("rk_inner"), 1)
                cm = slice(HD, P) if tt == 0 else slice(0, HD)
                for q in range(2):
                    for f, h in heads(q):
                        last = mm(bank(0)[HD * q:HD * (q + 1), f * HD:(f + 1) * HD], Xb[cm, 4 * q + f, 0:HD],
                                  Bt[cm, 0, h * HD:(h + 1) * HD])
                last.then_inc(sem("rk_transition"), 1)
                pe.wait_ge(sem("rk_transition_taken"), tt + 1)
                pe.wait_ge(sem("rk_inner_taken"), tt + 1)
                for c in range(2):
                    gc = 2 * tt + c
                    rows_c = slice(c * CH, (c + 1) * CH)
                    if gc:
                        pe.wait_ge(sem("rk_state"), gc)
                        for q in range(2):
                            rows = slice(HD * q, HD * (q + 1))
                            for f in range(4):
                                last = mm(bank(6 + q)[rows, f * P + c * CH:f * P + (c + 1) * CH], state[rows, f, :],
                                          R_[rows, f, gc * CH:(gc + 1) * CH])
                        if gc != 2:
                            last.then_inc(sem("rk_carried"), 1)
                    if gc == 3:
                        continue
                    for q in range(2):
                        rows = slice(HD * q, HD * (q + 1))
                        for f, h in heads(q):
                            hc = slice(h * HD, (h + 1) * HD)
                            o = bank(5)[rows, f * HD:(f + 1) * HD]
                            mm(o, Kt[rows_c, 0, hc], Vt[rows_c, 0, hc], True, False)
                            last = mm(o, Bt[rows_c, 0, hc], Xb[rows_c, 4 * q + f, HD:P], False, True)
                            if gc:
                                last = mm(bank(1 + q)[rows, f * HD:(f + 1) * HD], MT[rows, f, :], state[rows, f, :])
                    last.then_inc(sem("rk_update"), 1)
            pe.wait_ge(sem("rk_out"), 1)
            for h in range(2):
                last = mm(bank(h), table("head_ones"), flat(KK)[:, 512 * h:512 * (h + 1)])
            last.then_inc(sem("rk_mean"), 1)
            pe.wait_ge(sem("rk_centred"), 1)
            for h in range(2):
                last = mm(bank(2 + h), table("head_ones"), flat(TM)[:, 512 * h:512 * (h + 1)])
            last.then_inc(sem("rk_var"), 1)

            pe.wait_ge(sem("rk_root"), 1)
            with pe.Fori(0, 4) as i:
                for j in range(3):
                    b = (taken[0] + j) % 3
                    pe.wait_ge(sem("output_taken"), i * 3 + (taken[0] + j - 2))
                    output_slab(START["gates"] + j, 0, bank(b), i)
            taken[0] += 12
            operands(3)
            pe.wait_ge(sem("output_taken"), taken[0])
            for j in range(6):
                if j >= 3:
                    pe.wait_ge(sem("branch_taken"), j - 2)
                slot, _, g = place(START["branch"] + j)
                pe.wait_ge(lo_split, g + 1)
                out = bank(2 * (j % 3), 2)
                for m in range(4):
                    for k in range(4):
                        x = 8 + 4 * (j // 2) + k
                        last = block_product(out[:, m * T:(m + 1) * T], slot, 4 * m + k, XH[:, x, :], XL[:, x, :],
                                             k == 0, k == 3)
                last.then_inc(multiplied, 1)
            operands(1)
            residual_bank("mix_out")

            norm_sum(KT)
            norm_sum(KT)
            operands(2 * KT)
            project("ca_k", 8, 4)
            project_by_token("ca_v", 8, 4)
            project("ca_q", 0, 4)
            pe.wait_ge(sem("output_taken"), taken[0])
            for tt in range(2):
                for h in range(4):
                    i = 4 * tt + h
                    for d in range(2):
                        last = mm(bank(i // 2)[:, i % 2 * T:(i % 2 + 1) * T], ca_q[:, 2 * h + d, tt * P:(tt + 1) * P],
                                  ca_k[:, 2 * h + d, :], d == 0, d == 1)
            last.then_inc(sem("ca_scores"), 1)
            pe.wait_ge(sem("ca_probs"), 1)
            for i in range(8):
                tt, h = divmod(i, 4)
                for mt in range(2):
                    last = nc.tensor.transpose(bank(4 + h)[:, mt * T + tt * P:mt * T + (tt + 1) * P],
                                               probs[:, i, mt * P:(mt + 1) * P], table("identity"))
            last.then_inc(sem("ca_turned"), 1)
            pe.wait_ge(sem("ca_turned_taken"), 1)
            for h in range(4):
                for d in range(2):
                    for mt in range(2):
                        last = mm(bank(h)[:, d * T:(d + 1) * T], ca_v[:, mt, (2 * h + d) * P:(2 * h + d + 1) * P],
                                  probs_t[:, 2 * h + mt, :], mt == 0, mt == 1)
            last.then_inc(sem("ca_out"), 1)
            operands(1)
            residual_bank("ca_o")

            norm_sum(KT)
            feed_forward("ffn_c")
            norm_sum(KT)

            norm_sum(KT)
            feed_forward("ffn_0")

            norm_sum(KT)
            operands(KT)
            pe.wait_ge(sem("gate_taken"), ffns[0] * FP)
            project("even_in", 0, 8)
            project_by_token("even_v", 0, 4)
            pe.wait_ge(sem("output_taken"), taken[0])
            pe.wait_ge(sem("spatial_ready"), 1)
            pe.wait_ge(sem("spatial_landed"), 48)
            for f in range(4):
                for q in range(2):
                    h = 2 * f + q
                    for tt in range(2):
                        o = bank(f // 2)[HD * q:HD * (q + 1), f % 2 * T + tt * P:f % 2 * T + (tt + 1) * P]
                        mm(o, AV[:, tt, h * HD:(h + 1) * HD], spatial_w[:, h, :], True, False)
                        last = mm(o, table("ones")[0:1, 0:HD], spatial_b[:, h * P:(h + 1) * P], False, True)
            last.then_inc(sem("spatial_mixed"), 1)
            for li in range(9):
                pe.wait_ge(sem("gl_factors"), li + 1)
                if li >= 2:
                    pe.wait_ge(sem("gl_added"), li - 1)
                if li < 8:
                    for tt in range(2):
                        tok = slice(tt * P, (tt + 1) * P)
                        for h in range(4):
                            k = KB[:, h, tok] if li == 0 else XM[li % 2][:, h, tok]
                            q = BQ[:, h, tok] if li == 0 else XM[li % 2][:, h, tok]
                            last = mm(bank(2 + 2 * (li % 2) + tt)[:, h * P:(h + 1) * P], k, q)
                else:
                    for h in range(4):
                        last = mm(bank(2)[:, h * P:(h + 1) * P], XM[0][:, h, 0:P], XM[0][:, h, P:T])
                last.then_inc(sem("gl_pairs"), 1)
            pe.wait_ge(sem("gl_added"), 9)
            for h in range(4):
                o, c = bank(6 + h // 2)[:, h % 2 * T:(h % 2 + 1) * T], slice(h * P, (h + 1) * P)
                mm(o[:, 0:P], BI[:, 0, c], AT[:, h, :])
                mm(o[:, P:T], BI[:, 1, c], AT[:, 4 + h, :], True, False)
                last = mm(o[:, P:T], BI[:, 0, c], AC[:, h, :], False, True)
            last.then_inc(sem("gl_out"), 1)
            pe.wait_ge(sem("gl_squares"), 1)
            for h in range(2):
                last = mm(bank(2 + h), table("ones"), flat(KB)[:, 512 * h:512 * (h + 1)])
            last.then_inc(sem("gl_norms"), 1)
            operands(2)
            project("even_out", 8, 4)

            def per_layer(name, n):
                g0 = START[name]
                norm_sum(KT)
                operands(1)
                pe.wait_ge(sem("up_taken"), ffns[0] * FP)
                slot, _, g = place(g0)
                pe.wait_ge(lo_split, g + 1)
                for m in range(KT):
                    for k in range(2):
                        last = block_product(bank(3 + m // 2)[:, m % 2 * T:(m % 2 + 1) * T], slot, k * KT + m,
                                             XH[:, 8 + k, :], XL[:, 8 + k, :], k == 0, k == 1)
                last.then_inc(multiplied, 1)
                operands(KT)
                for j in range(4):
                    output_slab(g0 + 1 + j, 0, bank(free_bank()))
                norm_sum(KT)

            norm_sum(KT)
            feed_forward("ffn_1")
            per_layer("ple_0", 0)
            norm_sum(KT)
            feed_forward("ffn_2")

            norm_sum(KT)
            operands(KT)
            pe.wait_ge(sem("gate_taken"), ffns[0] * FP)
            project("mla_in", 0, 3)
            norm_sum(3)
            norm_sum(2)
            operands(5)
            pe.wait_ge(sem("output_taken"), taken[0])
            for j in range(3):
                slot, _, g = place(START["mla_q"] + j)
                pe.wait_ge(lo_split, g + 1)
                out = bank(2 * j, 2)
                for m in range(4):
                    for k in range(3):
                        last = block_product(out[:, m * T:(m + 1) * T], slot, 3 * m + k, XH[:, 8 + k, :],
                                             XL[:, 8 + k, :], k == 0, k == 2)
                last.then_inc(multiplied, 1)
            slot, _, g = place(START["mla_kv"])
            pe.wait_ge(lo_split, g + 1)
            pe.wait_ge(sem("mla_taken"), 2)
            for m in range(8):
                for k in range(2):
                    last = block_product(bank(m // 2)[:, m % 2 * T:(m % 2 + 1) * T], slot, 2 * m + k,
                                         XH[:, 11 + k, :], XL[:, 11 + k, :], k == 0, k == 1)
            last.then_inc(multiplied, 1)
            slot, _, g = place(START["mla_kv"] + 1)
            pe.wait_ge(lo_split, g + 1)
            pe.wait_ge(sem("mla_taken"), 3)
            for tt in range(2):
                tok = slice(tt * P, (tt + 1) * P)
                for n in range(2):
                    o = bank(4 + 2 * tt + n)
                    for k in range(2):
                        w = slice(k * D + n * 512, k * D + (n + 1) * 512)
                        mm(o, XH[:, 11 + k, tok], ring_hi[:, slot, w], k == 0, False)
                        mm(o, XL[:, 11 + k, tok], ring_hi[:, slot, w], False, False)
                        last = mm(o, XH[:, 11 + k, tok], ring_lo[:, slot, w], False, k == 1)
            last.then_inc(multiplied, 1)
            pe.wait_ge(sem("mla_taken"), 5)
            for side in range(2):
                pe.wait_ge(sem("mla_squares"), side + 1)
                if side:
                    pe.wait_ge(sem("mla_roots"), 1)
                for h in range(8):
                    o = bank(h // 2)[:, h % 2 * T:(h % 2 + 1) * T]
                    mm(o, table("ones"), msq[:, h, :], True, False)
                    rope = msq[:, 8 + h // 2, :] if side == 0 else msq[:, 8, :]
                    half = ["first_half", "second_half"][h % 2] if side == 0 else "first_half"
                    last = mm(o, table(half), rope, False, True)
                last.then_inc(sem("mla_sums"), 1)
            pe.wait_ge(sem("mla_rope_in"), 1)
            for n in range(2):
                mm(bank(4 + n), table("swap"), flat(MQ[:, 8:12])[:, 512 * n:512 * (n + 1)])
            mm(bank(6)[:, 0:T], table("swap"), MI[:, 5, :]).then_inc(sem("mla_swapped"), 1)
            pe.wait_ge(sem("mla_qk"), 1)
            for h in range(8):
                o = bank(h // 4)[:, h % 4 * P:(h % 4 + 1) * P]
                mm(o, MQ[:, h, 0:P], MK[:, h, 0:P], True, False)
                mm(o, MQ[:, 8 + h // 2, 0:P], KRP[:, h, 0:P], False, True)
                o = bank(2 + h // 2)[:, h % 2 * T:(h % 2 + 1) * T]
                mm(o, MQ[:, h, P:T], MK[:, h, :], True, False)
                last = mm(o, MQ[:, 8 + h // 2, P:T], KRP[:, h, :], False, True)
            last.then_inc(sem("mla_scores"), 1)
            pe.wait_ge(sem("mla_probs"), 1)
            for h in range(8):
                o = bank(h // 2)[:, h % 2 * T:(h % 2 + 1) * T]
                nc.tensor.transpose(o[:, 0:P], S0[:, h, :], table("identity"))
                nc.tensor.transpose(o[:, P:T], S1[:, h, 0:P], table("identity"))
                last = nc.tensor.transpose(bank(4 + h // 4)[:, h % 4 * P:(h % 4 + 1) * P], S1[:, h, P:T],
                                           table("identity"))
            last.then_inc(sem("mla_turned"), 1)
            pe.wait_ge(sem("mla_turned_taken"), 1)
            for h in range(8):
                o, c = bank(h // 2)[:, h % 2 * T:(h % 2 + 1) * T], slice(h * P, (h + 1) * P)
                mm(o, MV[:, 0, c], PT0[:, h, :], True, False)
                last = mm(o[:, P:T], MV[:, 1, c], PT1[:, h, :], False, True)
            last.then_inc(sem("mla_out"), 1)
            operands(1)
            residual_bank("mla_out")

            norm_sum(KT)
            feed_forward("ffn_3")
            per_layer("ple_1", 1)

        @block.scalar
        def _(act):
            taken = [0]
            splits = [0]
            steps = [0]

            def run(out, in_, func=ACT.Copy, **kw):
                return nc.scalar.activation(out, in_, func, **kw)

            def step(ins_):
                steps[0] += 1
                ins_.then_inc(sem("act_step"), 1)
                act.wait_ge(sem("act_step"), steps[0])

            def split_slab(g0, i=0):
                if g0 >= N_SLABS:
                    return
                slot, use, g = place(g0, i)
                act.wait_ge(landed[slot], (use + 1) * 16)
                if g0 >= 3:
                    act.wait_ge(multiplied, g - 2)
                run(ring_hi[:, slot, :], ring_raw[:, slot, :]).then_inc(hi_split, 1)

            def output(g0, i=0):
                split_slab(g0 + 2, i)
                act.wait_ge(multiplied, place(g0, i)[2] + 1)
                b = taken[0] % 3
                taken[0] += 1
                return b

            def output_elsewhere(name, n):
                for j in range(n):
                    split_slab(START[name] + j + 2)
                taken[0] += n

            def operand(out, in_, **kw):
                splits[0] += 1
                return run(out, in_, **kw).then_inc(sem("operand_hi"), 1)

            norms = [0]
            scaled = [0]

            def norm(src, n, ready, gain=None, x0=0, width=None):
                act.wait_ge(sem(ready[0]), ready[1])
                norms[0] += 1
                if splits[0]:
                    act.wait_ge(sem("operand_lo"), splits[0])
                run(flat(squares[:, 0:n]), flat(src), ACT.Square).then_inc(sem("norm_squared"), 1)
                act.wait_ge(sem("norm_summed"), norms[0])
                run(root[:], bank(7)[:, 0:T], ACT.Sqrt, bias=eps_col(EPS), scale=1.0 / (n * P))\
                    .then_inc(sem("norm_root"), 1)
                if gain is not None:
                    scaled[0] += 1
                    act.wait_ge(sem("norm_scaled"), scaled[0])
                    for k in range(n):
                        operand(XH[:, x0 + k, :], squares[:, k, :], scale=col(gain[0], gain[1] + k))

            def eps_col(value):
                return small[:, {EPS: 32, GN_EPS: 33, 1.0: 34, 0.0: 35}[value]:][:, 0:1]

            ffns = [0]

            def feed_forward(name, conv=False):
                g0, n = START[name], ffns[0]
                up_taken, gate_taken, conv_done = sem("up_taken"), sem("gate_taken"), sem("conv_done")

                def gate(at, i=0, t=0):
                    pair = i + t
                    act.wait_ge(multiplied, place(at, i)[2] + 1)
                    if conv:
                        if t:
                            act.wait_ge(up_taken, i + t)
                        conv_start(conv_acc, 0, pair, i)
                        act.wait_ge(conv_done, i + (t + 1))
                        run(silu_out, flat(conv_acc), ACT.Silu).then_inc(gate_taken, 1)
                    else:
                        if n or t:
                            act.wait_ge(up_taken, i + (n * FP + t))
                        run(silu_out, bank(0), ACT.Silu).then_inc(gate_taken, 1)

                def conv_start(acc, second, pair, i):
                    for m in range(2):
                        tile_ = pair * 2 + (m + 2 * FP * second)
                        w2 = prm[:, bass.ds(tile_ + (COL["ffn_conv_w"] + 2 * 4 * FP), 1)]
                        b = prm[:, bass.ds(tile_ + COL["ffn_conv_b"], 1)]
                        last = run(acc[:, m, :], bank(second)[:, m * T:(m + 1) * T], ACT.Identity, scale=w2, bias=b)
                    last.then_inc(sem("conv_started"), 1)

                def hidden_hi(i=0, t=0, at=None):
                    act.wait_ge(up_taken, i + (n * FP + t + 1))
                    if t or at is not None:
                        act.wait_ge(multiplied, place(at, i)[2])
                    run(flat(HH[:]), hidden).then_inc(sem("hidden_hi"), 1)

                def up(at, i=0, t=0):
                    if conv:
                        act.wait_ge(multiplied, place(at, i)[2] + 1)
                        conv_start(conv_acc2, 1, i + t, i)

                split_slab(g0 + 2)
                gate(g0)
                split_slab(g0 + 3)
                up(g0 + 1)
                with act.Fori(0, FP - 1) as i:
                    split_slab(g0 + 4, i)
                    hidden_hi(i, 0, g0 + 2)
                    gate(g0 + 2, i, 1)
                    split_slab(g0 + 5, i)
                    up(g0 + 3, i, 1)
                    split_slab(g0 + 6, i)
                split_slab(g0 + 34)
                hidden_hi(0, FP - 1, g0 + 32)
                ffns[0] += 1

            act.dma_start(H[:], ins["x_t"].rearrange("(k p) t -> p k t", p=P)).then_inc(sem("x_landed"), 16)
            act.dma_start(prm[:], ins["params"]).then_inc(sem("params_landed"), 16)
            act.wait_ge(sem("small_ready"), 1)
            act.wait_ge(sem("params_landed"), 16)
            split_slab(0)
            norm(H[:], KT, ("x_landed", 16), ("norm_mix", 0))
            split_slab(1)

            for j in range(6):
                b = output(START["conv"] + j)
                run(flat(conv_in[:, 2 * j:2 * j + 2]), bank(b)).then_inc(sem("output_taken"), 1)
            for j in range(4):
                b = output(START["sb_qk"] + j)
                run(flat(sbq[:, 2 * j:2 * j + 2]), bank(b)).then_inc(sem("output_taken"), 1)
            for j in range(2):
                b = output(START["sb_v"] + j)
                run(sbv[:, :, j * T:(j + 1) * T], tiles_of(b, 2)).then_inc(sem("output_taken"), 1)
            act.wait_ge(sem("conv_y"), 1)
            operand(flat(XH[:, 8:12]), flat(conv_y))
            for q in range(2):
                act.wait_ge(sem("sb_z"), q + 1)
                z, w = sb_z[q], sb_w[q]
                run(z, bank(0, 3), scale=HD ** -0.5).then_inc(sem("sb_z_taken"), 1)
                act.wait_ge(sem("sb_z_taken"), q + 1)
                step(run(w, z, ACT.Abs))
                step(run(w, w, ACT.Exp, scale=-1.0))
                run(w, w, ACT.Ln, bias=eps_col(1.0)).then_inc(sem("sb_softplus"), 1)
            for q in range(2):
                act.wait_ge(sem("sb_logw"), q + 1)
                run(sb_w[q], sb_w[q], ACT.Exp).then_inc(sem("sb_exp"), 1)
            act.wait_ge(sem("sb_y"), 1)
            operand(flat(XH[:, 12:16]), bank(6, 2))

            for j in range(7):
                b = output(START["rwkv"] + j)
                if j == 0:
                    act.wait_ge(sem("operand_lo"), KT + 2)
                for m in range(2):
                    t = 2 * j + m
                    last = run(rp[:, t, :], bank(b)[:, m * T:(m + 1) * T], scale=one_minus_mu[:, t:t + 1])
                last.then_inc(sem("rk_scaled"), 1)
            act.wait_ge(sem("output_taken"), taken[0])
            run(LORA[0:HD, 0, :], LORA[0:HD, 0, :], ACT.Tanh)
            run(LORA[:, 1, :], LORA[:, 1, :], ACT.Sigmoid).then_inc(sem("rk_lora_in"), 1)
            act.wait_ge(sem("rk_lora_out"), 1)
            for f in range(4):
                run(LW[:, f, :], tiles_of(0, 4)[:, f, :], ACT.Sigmoid, bias=col("w0", f))
                run(A_[:, f, :], tiles_of(2, 4)[:, f, :], ACT.Sigmoid, bias=col("a0", f))
            run(flat(G_), bank(4, 2)).then_inc(sem("rk_gates"), 1)
            act.wait_ge(sem("rk_norms"), 1)
            run(flat(TM), bank(6, 2), ACT.Sqrt, bias=eps_col(0.0)).then_inc(sem("rk_kk_root"), 1)
            act.wait_ge(sem("rk_decays"), 1)
            run(flat(EP), flat(LC), ACT.Exp)
            run(flat(LW), flat(LW), ACT.Exp)
            step(run(flat(LC), flat(LC), ACT.Exp, scale=-1.0))
            run(chunk_decay, EP[:, :, CH - 1:T:CH]).then_inc(sem("rk_exps"), 1)
            for tt in range(2):
                act.wait_ge(sem("rk_turned"), tt + 1)
                if tt == 0:
                    act.wait_ge(sem("rk_prep"), 1)
                run(Vt[:, 0, :], bank(0))
                run(ZP[:, :, 0:HD], bank(1).rearrange("p (h k) -> p h k", k=HD)).then_inc(sem("rk_turned_act"), 1)
                act.wait_ge(sem("rk_p"), tt + 1)
                run(ZP[:, :, HD:P], bank(0).rearrange("p (h k) -> p h k", k=HD)).then_inc(sem("rk_p_taken"), 1)
                for n in range(12 * tt, 12 * (tt + 1)):
                    act.wait_ge(sem("rk_f"), n + 1)
                    q = n % 2
                    run(flat(Fm[:, 4 * q:4 * q + 4]), bank(1 + q)).then_inc(sem("rk_f_taken"), 1)
                act.wait_ge(sem("rk_wu"), tt + 1)
                for q in range(2):
                    last = run(flat(Xb[:, 4 * q:4 * q + 4]), bank(3 + q))
                last.then_inc(sem("rk_wu_taken"), 1)
                act.wait_ge(sem("rk_inner"), tt + 1)
                run(KK[:, :, tt * P:(tt + 1) * P], bank(3).rearrange("p (f t) -> p f t", f=4))\
                    .then_inc(sem("rk_inner_copied"), 1)
                act.wait_ge(sem("rk_transition"), tt + 1)
                run(flat(MT), bank(0)[:, 0:4 * HD]).then_inc(sem("rk_transition_taken"), 1)
            act.wait_ge(sem("rk_var"), 1)
            run(flat(TM), bank(2, 2), ACT.Sqrt, bias=eps_col(GN_EPS), scale=1.0 / HD).then_inc(sem("rk_root"), 1)
            act.wait_ge(sem("rk_y_out"), 1)
            operand(flat(XH[:, 16:20]), flat(KK))

            act.wait_ge(sem("operand_lo"), KT + 3)
            with act.Fori(0, 4) as i:
                for j in range(3):
                    split_slab(START["gates"] + j + 2, i)
                    act.wait_ge(multiplied, place(START["gates"] + j, i)[2] + 1)
                    b = (taken[0] + j) % 3
                    for m in range(2):
                        t = i * 6 + (2 * j + m)
                        last = run(gates[:, bass.ds(t, 1), :].squeeze(1), bank(b)[:, m * T:(m + 1) * T], ACT.Sigmoid,
                                   bias=prm[:, bass.ds(t + COL["gate_b"], 1)])
                    last.then_inc(sem("output_taken"), 1)
            taken[0] += 12
            for j in range(6):
                split_slab(START["branch"] + j + 2)
            act.wait_ge(sem("branch_taken"), 6)
            operand(flat(XH[:, 0:8]), flat(merged))
            output_elsewhere("mix_out", 4)

            norm(H[:], KT, ("residual_ready", 1), ("norm_ca", 0))
            norm(mem, KT, ("mem_landed", 16), ("norm_mem", 0), 8)
            for j in range(4):
                b = output(START["ca_k"] + j)
                run(flat(ca_k[:, 2 * j:2 * j + 2]), bank(b)).then_inc(sem("output_taken"), 1)
            for j in range(4):
                b = output(START["ca_v"] + j)
                run(ca_v[:, :, j * T:(j + 1) * T], tiles_of(b, 2)).then_inc(sem("output_taken"), 1)
            for j in range(4):
                b = output(START["ca_q"] + j)
                run(flat(ca_q[:, 2 * j:2 * j + 2]), bank(b)).then_inc(sem("output_taken"), 1)
            act.wait_ge(sem("ca_max"), 1)
            for i in range(8):
                last = run(probs[:, i, :], tiles_of(0, 8)[:, i, :], ACT.Exp, scale=1.0 / 16, bias=small[:, 8 + i:9 + i],
                           accum_out=small[:, 16 + i:17 + i])
            last.then_inc(sem("ca_exp"), 1)
            act.wait_ge(sem("ca_turned"), 1)
            run(flat(probs_t), bank(4, 4)).then_inc(sem("ca_turned_taken"), 1)
            act.wait_ge(sem("ca_out"), 1)
            operand(flat(XH[:, 0:8]), bank(0, 4))
            output_elsewhere("ca_o", 4)

            norm(H[:], KT, ("residual_ready", 2), ("norm_ffn", 0))
            feed_forward("ffn_c", conv=True)
            norm(H[:], KT, ("residual_ready", 3))
            norm(H[:], KT, ("residual_ready", 4), ("norm_gains", 0))
            feed_forward("ffn_0")

            norm(H[:], KT, ("residual_ready", 5), ("norm_gains", 8))
            funcs = [ACT.Gelu_apprx_tanh, ACT.Copy, ACT.Sigmoid, ACT.Silu]
            for j in range(8):
                b = output(START["even_in"] + j)
                run(flat(ev[:, 2 * j:2 * j + 2]), bank(b), funcs[j // 2]).then_inc(sem("output_taken"), 1)
            for j in range(4):
                b = output(START["even_v"] + j)
                dst = [AV, BI][j // 2]
                run(dst[:, :, j % 2 * T:(j % 2 + 1) * T], tiles_of(b, 2), funcs[j // 2]).then_inc(sem("output_taken"), 1)
            act.wait_ge(sem("av_sums"), 1)
            run(small[:, 16:32], small[:, 0:16], ACT.Sqrt, bias=eps_col(EPS), scale=1.0 / HD).then_inc(sem("av_root"), 1)
            act.wait_ge(sem("gl_lb"), 1)
            run(small[:, 44:48], small[:, 40:44], ACT.Exp).then_inc(sem("gl_lb_exp"), 1)
            act.wait_ge(sem("gl_forget"), 1)
            run(flat(BF), flat(BF), ACT.Ln, bias=eps_col(0.0)).then_inc(sem("gl_log"), 1)
            act.wait_ge(sem("mixed_gated"), 1)
            operand(flat(XH[:, 8:12]), flat(AU))
            for li in range(1, 9):
                act.wait_ge(sem("gl_diff"), li)
                d = flat(DIF[li % 2])
                step(run(d, d, ACT.Abs))
                run(d, d, ACT.Exp, scale=-1.0).then_inc(sem("gl_exp"), 1)
            act.wait_ge(sem("gl_out"), 1)
            run(flat(BC), bank(6, 2)).then_inc(sem("gl_copied"), 1)
            act.wait_ge(sem("gl_copied"), 1)
            run(flat(KB), flat(BC), ACT.Square).then_inc(sem("gl_squares"), 1)
            act.wait_ge(sem("gl_norms"), 1)
            run(flat(DIF[0]), bank(2, 2), ACT.Sqrt, bias=eps_col(EPS), scale=1.0 / P).then_inc(sem("gl_root"), 1)
            act.wait_ge(sem("gl_y"), 1)
            operand(flat(XH[:, 12:16]), flat(BC))
            output_elsewhere("even_out", 4)

            def per_layer(name, n, ready):
                g0 = START[name]
                act.wait_ge(sem("ple_landed"), 16 * (n + 1))
                operand(flat(XH[:, 8:10]), flat(ple_in))
                norm(H[:], KT, ("residual_ready", ready), ("norm_gains", (5 * n + 3) * 8))
                split_slab(g0 + 2)
                act.wait_ge(multiplied, g0 + 1)
                run(flat(ple_p), bank(3, 4)).then_inc(sem("ple_copied"), 1)
                for j in range(4):
                    b = output(g0 + 1 + j)
                    run(flat(ple_g[:, 2 * j:2 * j + 2]), bank(b), ACT.Sigmoid).then_inc(sem("output_taken"), 1)
                norm(ple_p, KT, ("ple_product", n + 1))

            norm(H[:], KT, ("residual_ready", 6), ("norm_gains", 16))
            feed_forward("ffn_1")
            per_layer("ple_0", 0, 7)
            norm(H[:], KT, ("residual_ready", 8), ("norm_gains", 40))
            feed_forward("ffn_2")

            norm(H[:], KT, ("residual_ready", 9), ("norm_gains", 48))
            for j in range(3):
                b = output(START["mla_in"] + j)
                run(flat(MI[:, 2 * j:2 * j + 2]), bank(b)).then_inc(sem("output_taken"), 1)
            norm(MI[:, 0:3], 3, ("output_taken", taken[0]), ("q_a_norm", 0), 8)
            norm(MI[:, 3:5], 2, ("output_taken", taken[0]), ("kv_a_norm", 0), 11)
            act.wait_ge(sem("angles"), 1)
            run(flat(sines), flat(sines), ACT.Sin, bias=eps_col(0.0))
            run(flat(cosines), flat(cosines), ACT.Sin, bias=eps_col(0.0)).then_inc(sem("angles_done"), 1)
            for j in range(3):
                split_slab(START["mla_q"] + j + 2)
                act.wait_ge(multiplied, START["mla_q"] + j + 1)
                run(flat(MQ[:, 4 * j:4 * j + 4]), bank(2 * j, 2)).then_inc(sem("mla_taken"), 1)
            split_slab(START["mla_kv"] + 2)
            act.wait_ge(multiplied, START["mla_kv"] + 1)
            run(flat(MK), bank(0, 4)).then_inc(sem("mla_taken"), 1)
            split_slab(START["mla_kv"] + 3)
            act.wait_ge(multiplied, START["mla_kv"] + 2)
            run(flat(MV), bank(4, 4)).then_inc(sem("mla_taken"), 1)
            act.wait_ge(sem("mla_taken"), 5)
            act.wait_ge(sem("operand_lo"), splits[0])
            run(flat(msq), flat(MQ), ACT.Square).then_inc(sem("mla_squares"), 1)
            act.wait_ge(sem("mla_sums"), 1)
            run(flat(RQ), bank(0, 4), ACT.Sqrt, bias=eps_col(EPS), scale=1.0 / 192).then_inc(sem("mla_roots"), 1)
            run(flat(msq[:, 0:8]), flat(MK), ACT.Square)
            run(msq[:, 8, :], MI[:, 5, :], ACT.Square).then_inc(sem("mla_squares"), 1)
            act.wait_ge(sem("mla_sums"), 2)
            run(flat(RK), bank(0, 4), ACT.Sqrt, bias=eps_col(EPS), scale=1.0 / 192).then_inc(sem("mla_roots"), 1)
            act.wait_ge(sem("mla_max"), 1)
            for h in range(8):
                run(S0[:, h, :], S0[:, h, :], ACT.Exp, scale=192 ** -0.5, bias=small[:, h:h + 1],
                    accum_out=small[:, 16 + h:17 + h])
                last = run(S1[:, h, :], S1[:, h, :], ACT.Exp, scale=192 ** -0.5, bias=small[:, 8 + h:9 + h],
                           accum_out=small[:, 24 + h:25 + h])
            last.then_inc(sem("mla_exp"), 1)
            act.wait_ge(sem("mla_turned"), 1)
            run(flat(PT0), bank(0, 4))
            run(flat(PT1), bank(4, 2)).then_inc(sem("mla_turned_taken"), 1)
            act.wait_ge(sem("mla_out"), 1)
            operand(flat(XH[:, 0:8]), bank(0, 4))
            output_elsewhere("mla_out", 4)

            norm(H[:], KT, ("residual_ready", 10), ("norm_gains", 56))
            feed_forward("ffn_3")
            per_layer("ple_1", 1, 11)

        @block.vector
        def _(dve):
            v = nc.vector
            taken = [0]
            splits = [0]
            steps = [0]

            def step(ins_):
                steps[0] += 1
                ins_.then_inc(sem("dve_step"), 1)
                dve.wait_ge(sem("dve_step"), steps[0])

            def tt_(out, a, b, op):
                return v.tensor_tensor(out, a, b, op)

            def mul(out, a, b):
                return v.tensor_tensor(out, a, b, ALU.mult)

            def over(ap, n):
                return ap.unsqueeze(1).to_broadcast([P, n, ap.shape[-1]])

            def split_slab(g0, i=0):
                if g0 >= N_SLABS:
                    return
                slot, _, g = place(g0, i)
                dve.wait_ge(hi_split, g + 1)
                tt_(ring_lo[:, slot, :], ring_raw[:, slot, :], ring_hi[:, slot, :].bitcast(F32), ALU.subtract)\
                    .then_inc(lo_split, 1)

            def pass_slabs(name, n, ahead=2, banks=True):
                for j in range(n):
                    split_slab(START[name] + j + ahead)
                if banks:
                    taken[0] += n

            def operand(out, in_, hi):
                splits[0] += 1
                dve.wait_ge(sem("operand_hi"), splits[0])
                return tt_(out, in_, hi.bitcast(F32), ALU.subtract).then_inc(sem("operand_lo"), 1)

            norms = [0]

            def norm_scale(src, n, last_in=None):
                norms[0] += 1
                dve.wait_ge(sem("norm_root"), norms[0])
                step(v.reciprocal(inv[:], root[:]))
                return mul(squares[:, 0:n], src, over(inv[:], n))

            def norm(src, n, gain, x0=0):
                norm_scale(src, n).then_inc(sem("norm_scaled"), 1)
                scaled[0] += 1
                dve.wait_ge(sem("norm_scaled"), scaled[0])
                for k in range(n):
                    splits[0] += 1
                    dve.wait_ge(sem("operand_hi"), splits[0])
                    v.scalar_tensor_tensor(out=XL[:, x0 + k, :], in0=squares[:, k, :], scalar=col(gain[0], gain[1] + k),
                                           in1=XH[:, x0 + k, :].bitcast(F32), op0=ALU.mult, op1=ALU.subtract)\
                     .then_inc(sem("operand_lo"), 1)

            scaled = [0]

            def residual(name):
                for j in range(4):
                    split_slab(START[name] + j + 2)
                    dve.wait_ge(multiplied, START[name] + j + 1)
                    b = taken[0] % 3
                    taken[0] += 1
                    h = flat(H[:, 2 * j:2 * j + 2])
                    tt_(h, h, bank(b), ALU.add).then_inc(sem("output_taken"), 1)
                dve.wait_ge(sem("output_taken"), taken[0])
                v.memset(small[:, 63:64], 0.0).then_inc(sem("residual_ready"), 1)

            ffns = [0]

            def feed_forward(name, conv=False):
                g0, n = START[name], ffns[0]
                gate_taken, up_taken = sem("gate_taken"), sem("up_taken")

                def gate(at, i=0, t=0):
                    if conv:
                        dve.wait_ge(sem("conv_started"), i * 2 + (2 * t + 1))
                        taps(conv_acc, 0, i + t, i * 7 + 7 * t, sem("conv_done"))

                def taps(acc, second, pair, before, done):
                    for m in range(2):
                        w1 = prm[:, bass.ds(pair * 2 + (m + 2 * FP * second + COL["ffn_conv_w"] + 4 * FP), 1)]
                        v.scalar_tensor_tensor(out=acc[:, m, 1:T], in0=bank(second)[:, m * T:(m + 1) * T - 1],
                                               scalar=w1, in1=acc[:, m, 1:T], op0=ALU.mult, op1=ALU.add)\
                         .then_inc(sem("conv_tap"), 1)
                    dve.wait_ge(sem("conv_tap"), before + 2)
                    for m in range(2):
                        w0 = prm[:, bass.ds(pair * 2 + (m + 2 * FP * second + COL["ffn_conv_w"]), 1)]
                        v.scalar_tensor_tensor(out=acc[:, m, 2:T], in0=bank(second)[:, m * T:(m + 1) * T - 2],
                                               scalar=w0, in1=acc[:, m, 2:T], op0=ALU.mult, op1=ALU.add)\
                         .then_inc(done if m == 1 else sem("conv_tap"), 1)

                def up(at, i=0, t=0):
                    dve.wait_ge(gate_taken, i + (n * FP + t + 1))
                    dve.wait_ge(multiplied, place(at, i)[2] + 1)
                    if n or t:
                        dve.wait_ge(sem("hidden_lo"), i + (n * FP + t))
                    if conv:
                        dve.wait_ge(sem("conv_started"), i * 2 + (2 * t + 2))
                        taps(conv_acc2, 1, i + t, i * 7 + (7 * t + 3), sem("conv_tap"))
                        dve.wait_ge(sem("conv_tap"), i * 7 + (7 * t + 7))
                        mul(hidden, silu_out, flat(conv_acc2)).then_inc(up_taken, 1)
                    else:
                        mul(hidden, silu_out, bank(1)).then_inc(up_taken, 1)

                def hidden_lo(i=0, t=0):
                    dve.wait_ge(sem("hidden_hi"), i + (n * FP + t + 1))
                    tt_(flat(HL[:]), hidden, flat(HH[:]).bitcast(F32), ALU.subtract).then_inc(sem("hidden_lo"), 1)

                split_slab(g0 + 2)
                gate(g0)
                split_slab(g0 + 3)
                up(g0 + 1)
                with dve.Fori(0, FP - 1) as i:
                    split_slab(g0 + 4, i)
                    hidden_lo(i)
                    gate(g0 + 2, i, 1)
                    split_slab(g0 + 5, i)
                    up(g0 + 3, i, 1)
                    split_slab(g0 + 6, i)
                split_slab(g0 + 34)
                hidden_lo(0, FP - 1)
                dve.wait_ge(multiplied, g0 + 33)
                v.scalar_tensor_tensor(out=flat(H[:]), in0=bank(3, 4), scalar=1.0 if conv else 0.5, in1=flat(H[:]),
                                       op0=ALU.mult, op1=ALU.add).then_inc(sem("residual_ready"), 1)
                ffns[0] += 1

            for value, c in ((EPS, 32), (GN_EPS, 33), (1.0, 34), (0.0, 35)):
                last = v.memset(small[:, c:c + 1], value)
            last.then_inc(sem("small_ready"), 1)
            dve.wait_ge(sem("params_landed"), 16)
            step(v.tensor_scalar(one_minus_mu[:], col("mu", 0, 14), -1.0, 1.0, ALU.mult, ALU.add))
            split_slab(0)
            norm(H[:], KT, ("norm_mix", 0))
            split_slab(1)

            pass_slabs("conv", 6)
            pass_slabs("sb_qk", 4)
            pass_slabs("sb_v", 2)
            dve.wait_ge(sem("output_taken"), 6)
            step(mul(conv_u, conv_in[:, 4:8], conv_in[:, 8:12]))
            for f in range(4):
                last = v.tensor_scalar(conv_y[:, f, :], conv_u[:, f, :], col("conv_w", 8 + f), None, ALU.mult)
            step(last)
            for back in (1, 2):
                for f in range(4):
                    last = v.scalar_tensor_tensor(out=conv_y[:, f, back:T], in0=conv_u[:, f, 0:T - back],
                                                  scalar=col("conv_w", 4 * (2 - back) + f), in1=conv_y[:, f, back:T],
                                                  op0=ALU.mult, op1=ALU.add)
                step(last)
            mul(conv_y, conv_y, conv_in[:, 0:4]).then_inc(sem("conv_y"), 1)
            dve.wait_ge(sem("conv_y"), 1)
            operand(flat(XL[:, 8:12]), flat(conv_y), flat(XH[:, 8:12]))

            def masked(q, buf):
                for b in (0, 2):
                    blk = buf[:, b * 512:(b + 1) * 512].rearrange("p (f t) -> p f t", f=4)
                    last_ = mul(blk, blk, per_head("before"))
                return last_

            for q in range(2):
                dve.wait_ge(sem("sb_softplus"), q + 1)
                z, w = sb_z[q], sb_w[q]
                step(v.scalar_tensor_tensor(out=w, in0=z, scalar=0.0, in1=w, op0=ALU.min, op1=ALU.subtract))
                step(tt_(z, w, z, ALU.subtract))
                masked(q, z).then_inc(sem("sb_log"), 1)
            for q in range(2):
                dve.wait_ge(sem("sb_suffix"), q + 1)
                tt_(sb_w[q], sb_w[q], bank(3, 3), ALU.add).then_inc(sem("sb_logw"), 1)
                dve.wait_ge(sem("sb_exp"), q + 1)
                masked(q, sb_w[q]).then_inc(sem("sb_att"), 1)
            dve.wait_ge(sem("sb_y"), 1)
            operand(flat(XL[:, 12:16]), bank(6, 2), flat(XH[:, 12:16]))

            for j in range(7):
                split_slab(START["rwkv"] + j + 2)
                b = taken[0] % 3
                taken[0] += 1
                dve.wait_ge(sem("rk_scaled"), j + 1)
                for m in range(2):
                    t = 2 * j + m
                    last = v.scalar_tensor_tensor(out=rp[:, t, 1:T], in0=bank(b)[:, m * T:(m + 1) * T - 1],
                                                  scalar=col("mu", t), in1=rp[:, t, 1:T], op0=ALU.mult, op1=ALU.add)
                last.then_inc(sem("output_taken"), 1)
            dve.wait_ge(sem("output_taken"), taken[0])
            for f in range(4):
                last = v.tensor_scalar(KK[:, f, :], K_[:, f, :], col("k_k", f), None, ALU.mult)
            step(last)
            mul(TM, KK, KK).then_inc(sem("rk_squares"), 1)
            dve.wait_ge(sem("rk_gates"), 1)
            step(v.tensor_scalar(flat(LW), flat(LW), -DECAY_SCALE, None, ALU.mult))
            for f in range(4):
                for c in range(4):
                    t = slice(c * CH, (c + 1) * CH)
                    last = v.tensor_tensor_scan(LC[:, f, t], table("ones")[:, 0:CH], LW[:, f, t], 0.0, ALU.mult, ALU.add)
            step(last)
            tt_(flat(LW), flat(LC), flat(LW), ALU.subtract).then_inc(sem("rk_decays"), 1)
            dve.wait_ge(sem("rk_kk_root"), 1)
            step(v.tensor_scalar(flat(TM), flat(TM), 1e-12, None, ALU.max))
            step(v.reciprocal(flat(TM), flat(TM)))
            step(mul(KK, KK, TM))
            for f in range(4):
                last = v.tensor_scalar(TM[:, f, :], A_[:, f, :], -1.0, col("k_a", f), ALU.add, ALU.mult)
            step(last)
            step(v.scalar_tensor_tensor(out=flat(K_), in0=flat(TM), scalar=1.0, in1=flat(K_), op0=ALU.add, op1=ALU.mult))
            step(v.scalar_tensor_tensor(out=flat(A_), in0=flat(KK), scalar=-1.0, in1=flat(A_), op0=ALU.mult,
                                        op1=ALU.mult))
            for f in range(4):
                last = v.scalar_tensor_tensor(out=BN[:, f, :], in0=R_[:, f, :], scalar=col("r_k", f), in1=K_[:, f, :],
                                              op0=ALU.mult, op1=ALU.mult)
            last.then_inc(sem("rk_bonus_in"), 1)
            dve.wait_ge(sem("rk_exps"), 1)
            dve.wait_ge(sem("rk_bonus_in"), 1)
            mul(R_, R_, EP)
            mul(KK, KK, LW)
            mul(K_, K_, LC)
            step(mul(A_, A_, LC))
            dve.wait_ge(sem("rk_bonus_sums"), 1)
            mul(flat(BN), flat(V_), bank(6, 2)).then_inc(sem("rk_prep"), 1)
            for tt in range(2):
                tok = slice(tt * P, (tt + 1) * P)
                dve.wait_ge(sem("rk_turned"), tt + 1)
                v.tensor_copy(Kt[:, 0, :], bank(2))
                v.tensor_copy(Bt[:, 0, :], bank(3))
                dve.wait_ge(sem("rk_pairs"), tt + 1)
                for q in range(2):
                    e = slice(4 * q, 4 * q + 4)
                    mul(Fm[:, e, :], bank(4 + q).rearrange("p (f t) -> p f t", f=4), per_head("before_chunk"))
                    last = mul(Xm[:, e, :], bank(6 + q).rearrange("p (f t) -> p f t", f=4), per_head("before_chunk"))
                last.then_inc(sem("rk_masked"), 1)
                dve.wait_ge(sem("rk_masked"), tt + 1)
                for li in range(6):
                    for q in range(2):
                        n = (tt * 6 + li) * 2 + q
                        e = slice(4 * q, 4 * q + 4)
                        if li:
                            dve.wait_ge(sem("rk_f"), n - 1)
                        mul(Xb[:, e, :], Xm[:, e, :], per_head(f"level{LEVELS[li]}")).then_inc(sem("rk_x"), 1)
                    for q in range(2):
                        n = (tt * 6 + li) * 2 + q
                        e = slice(4 * q, 4 * q + 4)
                        dve.wait_ge(sem("rk_dy"), n + 1)
                        if li:
                            dve.wait_ge(sem("rk_y"), n - 1)
                        if li < 5:
                            y = Yt[:, e, :] if li else per_head("identity")
                            tt_(Yt[:, e, :], y, bank(5 + q).rearrange("p (f t) -> p f t", f=4), ALU.add)
                        y = Ym[:, e, :] if li else per_head("identity")
                        tt_(Ym[:, e, :], y, bank(3 + q).rearrange("p (f t) -> p f t", f=4), ALU.add)\
                            .then_inc(sem("rk_y"), 1)
                dve.wait_ge(sem("rk_out_pairs"), tt + 1)
                for q in range(2):
                    e = slice(4 * q, 4 * q + 4)
                    mul(Yt[:, e, :], bank(5 + q).rearrange("p (f t) -> p f t", f=4), per_head("upto_chunk"))
                    last = mul(Fm[:, e, :], bank(1 + q).rearrange("p (f t) -> p f t", f=4), per_head("upto_chunk"))
                last.then_inc(sem("rk_out_masked"), 1)
                dve.wait_ge(sem("rk_inner"), tt + 1)
                tt_(R_[:, :, tok], R_[:, :, tok], bank(7).rearrange("p (f t) -> p f t", f=4), ALU.add)\
                    .then_inc(sem("rk_inner_taken"), 1)
                dve.wait_ge(sem("rk_inner_copied"), tt + 1)
                for c in range(2):
                    gc = 2 * tt + c
                    if gc in (1, 3):
                        dve.wait_ge(sem("rk_carried"), 1 + tt)
                        t = slice(gc * CH, (gc + 1) * CH) if gc == 1 else tok
                        o = slice(CH, P) if gc == 1 else slice(0, P)
                        for q in range(2):
                            rows = slice(HD * q, HD * (q + 1))
                            part = bank(6 + q)[rows, :].rearrange("p (f t) -> p f t", f=4)[:, :, o]
                            last = tt_(KK[rows, :, t], KK[rows, :, t], part, ALU.add)
                        if gc == 3:
                            last.then_inc(sem("rk_out"), 1)
                            continue
                    dve.wait_ge(sem("rk_update"), gc + 1)
                    g_ = chunk_decay[:, :, gc:gc + 1].to_broadcast([P, 4, HD])
                    new = bank(5)[:, 0:4 * HD].rearrange("p (f v) -> p f v", f=4)
                    if gc:
                        step(tt_(state, state, new, ALU.add))
                        for q in range(2):
                            rows = slice(HD * q, HD * (q + 1))
                            old = bank(1 + q)[rows, 0:4 * HD].rearrange("p (f v) -> p f v", f=4)
                            last = tt_(state[rows], state[rows], old, ALU.add)
                        step(last)
                        if gc == 1:
                            step(mul(state, state, g_))
                            v.memset(small[:, 62:63], 0.0).then_inc(sem("rk_state"), 1)
                        else:
                            mul(state, state, g_).then_inc(sem("rk_state"), 1)
                    else:
                        mul(state, new, g_).then_inc(sem("rk_state"), 1)
                        dve.wait_ge(sem("rk_state"), 1)
                    if gc == 1:
                        v.memset(small[:, 61:62], 0.0).then_inc(sem("rk_tile_done"), 1)
            dve.wait_ge(sem("rk_mean"), 1)
            step(v.scalar_tensor_tensor(out=flat(KK), in0=bank(0, 2), scalar=-1.0 / HD, in1=flat(KK), op0=ALU.mult,
                                        op1=ALU.add))
            mul(TM, KK, KK).then_inc(sem("rk_centred"), 1)
            dve.wait_ge(sem("rk_root"), 1)
            step(v.reciprocal(flat(TM), flat(TM)))
            step(mul(KK, KK, TM))
            for f in range(4):
                last = v.tensor_scalar(KK[:, f, :], KK[:, f, :], col("lnx_w", f), col("lnx_b", f), ALU.mult, ALU.add)
            step(last)
            step(tt_(KK, KK, BN, ALU.add))
            mul(KK, KK, G_).then_inc(sem("rk_y_out"), 1)
            dve.wait_ge(sem("rk_y_out"), 1)
            operand(flat(XL[:, 16:20]), flat(KK), flat(XH[:, 16:20]))

            with dve.Fori(0, 4) as i:
                for j in range(3):
                    split_slab(START["gates"] + j + 2, i)
            taken[0] += 12
            dve.wait_ge(sem("output_taken"), taken[0])
            for j in range(6):
                split_slab(START["branch"] + j + 2)
                dve.wait_ge(multiplied, START["branch"] + j + 1)
                n, half = divmod(j, 2)
                out = merged[:, 4 * half:4 * half + 4]
                g_ = gates[:, 8 * n + 4 * half:8 * n + 4 * half + 4]
                src = bank(2 * (j % 3), 2).rearrange("p (m t) -> p m t", t=T)
                if n == 0:
                    step(mul(out, src, g_))
                else:
                    step(mul(gated, src, g_))
                    step(tt_(out, out, gated, ALU.add))
                v.memset(small[:, 60:61], 0.0).then_inc(sem("branch_taken"), 1)
            operand(flat(XL[:, 0:8]), flat(merged), flat(XH[:, 0:8]))
            residual("mix_out")

            norm(H[:], KT, ("norm_ca", 0))
            norm(mem, KT, ("norm_mem", 0), 8)
            for name in ("ca_k", "ca_v", "ca_q"):
                pass_slabs(name, 4)
            dve.wait_ge(sem("ca_scores"), 1)
            step(v.tensor_reduce(small[:, 0:8], tiles_of(0, 8), AX.X, ALU.max))
            v.tensor_scalar(small[:, 8:16], small[:, 0:8], -1.0 / 16, None, ALU.mult).then_inc(sem("ca_max"), 1)
            dve.wait_ge(sem("ca_exp"), 1)
            step(v.reciprocal(small[:, 24:32], small[:, 16:24]))
            mul(probs, probs, small[:, 24:32].unsqueeze(2).to_broadcast([P, 8, T])).then_inc(sem("ca_probs"), 1)
            dve.wait_ge(sem("ca_out"), 1)
            operand(flat(XL[:, 0:8]), bank(0, 4), flat(XH[:, 0:8]))
            residual("ca_o")

            norm(H[:], KT, ("norm_ffn", 0))
            feed_forward("ffn_c", conv=True)
            step(norm_scale(H[:], KT))
            for k in range(KT):
                last = v.tensor_scalar(H[:, k, :], squares[:, k, :], col("norm_final", k), None, ALU.mult)
            last.then_inc(sem("residual_ready"), 1)
            dve.wait_ge(sem("residual_ready"), 4)

            norm(H[:], KT, ("norm_gains", 0))
            feed_forward("ffn_0")

            norm(H[:], KT, ("norm_gains", 8))
            pass_slabs("even_in", 8)
            pass_slabs("even_v", 4)
            dve.wait_ge(sem("output_taken"), taken[0])
            avf = AV.rearrange("p a b -> p (a b)")
            sqv = flat(BC)
            step(mul(sqv, avf, avf))
            v.tensor_reduce(small[:, 0:16], sqv.rearrange("p (n d) -> p n d", d=HD), AX.X, ALU.add)\
             .then_inc(sem("av_sums"), 1)
            dve.wait_ge(sem("av_sums"), 1)
            tt_(small[:, 40:44], col("hgrn_lb", 0, 4), col("hgrn_lb", 0, 4), ALU.subtract).then_inc(sem("gl_lb"), 1)
            dve.wait_ge(sem("spatial_landed"), 48)
            mul(spatial_w, spatial_w, per_head("upto", 8))
            dve.wait_ge(sem("av_root"), 1)
            step(v.reciprocal(small[:, 0:16], small[:, 16:32]))
            avh = avf.rearrange("p (n d) -> p n d", d=HD)
            step(mul(avh, avh, small[:, 0:16].unsqueeze(2).to_broadcast([P, 16, HD])))
            mul(AV, AV, v_gain[:, 0, :].unsqueeze(1).to_broadcast([P, 2, W])).then_inc(sem("spatial_ready"), 1)
            dve.wait_ge(sem("gl_lb_exp"), 1)
            step(v.reciprocal(small[:, 48:52], small[:, 44:48]))
            step(mul(small[:, 52:56], small[:, 44:48], small[:, 48:52]))
            step(tt_(small[:, 40:44], small[:, 52:56], small[:, 52:56], ALU.subtract))
            step(v.tensor_scalar(small[:, 40:44], small[:, 40:44], 0.0, 0.999, ALU.max, ALU.min))
            step(v.tensor_scalar(small[:, 44:48], small[:, 40:44], -1.0, 1.0, ALU.mult, ALU.add))
            for h in range(4):
                last = v.tensor_scalar(BF[:, h, :], BF[:, h, :], small[:, 44 + h:45 + h], small[:, 40 + h:41 + h],
                                       ALU.mult, ALU.add)
            step(last)
            dve.wait_ge(sem("spatial_mixed"), 1)
            mul(flat(AU), flat(AU), bank(0, 2)).then_inc(sem("mixed_gated"), 1)
            step(v.tensor_scalar(flat(KB), flat(BF), -1.0, 1.0, ALU.mult, ALU.add))
            v.tensor_scalar(flat(BF), flat(BF), 1e-6, None, ALU.max).then_inc(sem("gl_forget"), 1)
            dve.wait_ge(sem("mixed_gated"), 1)
            operand(flat(XL[:, 8:12]), flat(AU), flat(XH[:, 8:12]))
            dve.wait_ge(sem("gl_log"), 1)
            for h in range(4):
                for tt in range(2):
                    t = slice(tt * P, (tt + 1) * P)
                    last = v.tensor_tensor_scan(BC[:, h, t], table("ones"), BF[:, h, t], 0.0, ALU.mult, ALU.add)
            last.then_inc(sem("gl_factors"), 1)
            dve.wait_ge(sem("gl_factors"), 1)

            def gl_mask(li):
                dve.wait_ge(sem("gl_pairs"), li + 1)
                if li == 8:
                    v.tensor_copy(AC, bank(2).rearrange("p (h t) -> p h t", h=4)).then_inc(sem("gl_added"), 1)
                    return
                name = f"level{LEVELS[li - 1]}" if li else "identity"
                for tt in range(2):
                    src = bank(2 + 2 * (li % 2) + tt).rearrange("p (h t) -> p h t", h=4)
                    a = AT[:, 4 * tt:4 * tt + 4, :]
                    if li == 0:
                        last_ = mul(a, src, per_head(name))
                    else:
                        step(mul(AM, src, per_head(name)))
                        last_ = tt_(a, a, AM, ALU.add)
                        if tt == 0:
                            step(last_)
                last_.then_inc(sem("gl_added"), 1)
                dve.wait_ge(sem("gl_added"), li + 1)

            def gl_diff(li):
                d = DIF[li % 2]
                if li < 8:
                    b = LEVELS[li - 1]
                    bc = flat(BC).rearrange("p (n c) -> p n c", c=2 * b)
                    ref = bc[:, :, b - 1:b].to_broadcast([P, 4 * T // (2 * b), 2 * b])
                    tt_(flat(d).rearrange("p (n c) -> p n c", c=2 * b), bc, ref, ALU.subtract)\
                        .then_inc(sem("gl_diff"), 1)
                else:
                    v.tensor_copy(d[:, :, P:T], BC[:, :, P:T])
                    tt_(d[:, :, 0:P], BC[:, :, 0:P], BC[:, :, P - 1:P].to_broadcast([P, 4, P]), ALU.subtract)\
                        .then_inc(sem("gl_diff"), 1)

            def gl_factor(li):
                b = LEVELS[li - 1] if li < 8 else P
                dve.wait_ge(sem("gl_exp"), li)
                if li >= 2:
                    dve.wait_ge(sem("gl_pairs"), li - 1)
                blocks = [flat(a).rearrange("p (n c) -> p n c", c=2 * b) for a in (XM[li % 2], DIF[li % 2], KB, BQ)]
                x, e, k, q = blocks
                mul(x[:, :, 0:b], e[:, :, 0:b], k[:, :, 0:b])
                mul(x[:, :, b:2 * b], e[:, :, b:2 * b], q[:, :, b:2 * b]).then_inc(sem("gl_factors"), 1)

            gl_diff(1)
            for li in range(1, 9):
                if li < 8:
                    if li > 1:
                        dve.wait_ge(sem("gl_factors"), li)
                    gl_diff(li + 1)
                gl_factor(li)
                gl_mask(li - 1)
            gl_mask(8)
            dve.wait_ge(sem("gl_root"), 1)
            step(v.reciprocal(flat(DIF[0]), flat(DIF[0])))
            step(v.scalar_tensor_tensor(out=flat(BC), in0=flat(BC), scalar=col("hgrn_out_norm"), in1=flat(DIF[0]),
                                        op0=ALU.mult, op1=ALU.mult))
            mul(BC, BC, BG).then_inc(sem("gl_y"), 1)
            dve.wait_ge(sem("gl_y"), 1)
            operand(flat(XL[:, 12:16]), flat(BC), flat(XH[:, 12:16]))
            residual("even_out")

            def per_layer(name, n):
                g0 = START[name]
                dve.wait_ge(sem("ple_landed"), 16 * (n + 1))
                operand(flat(XL[:, 8:10]), flat(ple_in), flat(XH[:, 8:10]))
                norm(H[:], KT, ("norm_gains", (5 * n + 3) * 8))
                for j in range(5):
                    split_slab(g0 + j + 2)
                taken[0] += 4
                dve.wait_ge(sem("output_taken"), taken[0])
                mul(ple_p, ple_p, ple_g).then_inc(sem("ple_product"), 1)
                dve.wait_ge(sem("ple_product"), n + 1)
                step(norm_scale(ple_p, KT))
                for k in range(KT):
                    last_ = v.scalar_tensor_tensor(out=H[:, k, :], in0=squares[:, k, :],
                                                   scalar=col("norm_gains", (5 * n + 4) * 8 + k), in1=H[:, k, :],
                                                   op0=ALU.mult, op1=ALU.add)
                last_.then_inc(sem("residual_ready"), 1)

            norm(H[:], KT, ("norm_gains", 16))
            feed_forward("ffn_1")
            per_layer("ple_0", 0)
            dve.wait_ge(sem("residual_ready"), 8)
            norm(H[:], KT, ("norm_gains", 40))
            feed_forward("ffn_2")

            norm(H[:], KT, ("norm_gains", 48))
            pass_slabs("mla_in", 3)
            norm(MI[:, 0:3], 3, ("q_a_norm", 0), 8)
            norm(MI[:, 3:5], 2, ("kv_a_norm", 0), 11)
            dve.wait_ge(sem("positions_landed"), 16)
            two_pi = 2 * np.pi
            magic = 1.5 * 2.0 ** 23
            c1 = 6.28125
            c2 = float(np.float32(two_pi - c1))
            c2 = float(np.round(c2 * 2 ** 20) / 2 ** 20)
            c3 = float(two_pi - c1 - c2)
            a_, n_ = flat(ang), flat(turns)
            step(v.tensor_copy(a_, cosines.bitcast(I32)[:, 0, :]))
            step(v.tensor_scalar(a_, a_, col("inv_freq"), None, ALU.mult))
            step(v.tensor_scalar(n_, a_, 1 / two_pi, None, ALU.mult))
            step(v.tensor_scalar(n_, n_, magic, None, ALU.add))
            step(v.tensor_scalar(n_, n_, -magic, None, ALU.add))
            for c in (c1, c2, c3):
                step(v.scalar_tensor_tensor(out=a_, in0=n_, scalar=-c, in1=a_, op0=ALU.mult, op1=ALU.add))
            limit = 3.1415925
            v.tensor_scalar(flat(sines), a_, limit, -limit, ALU.min, ALU.max)
            step(v.tensor_scalar(a_, a_, np.pi / 2, None, ALU.add))
            step(v.tensor_scalar(n_, a_, np.pi, -two_pi, ALU.is_gt, ALU.mult))
            step(tt_(a_, a_, n_, ALU.add))
            v.tensor_scalar(flat(cosines), a_, limit, -limit, ALU.min, ALU.max).then_inc(sem("angles"), 1)
            pass_slabs("mla_q", 3, banks=False)
            pass_slabs("mla_kv", 2, banks=False)
            dve.wait_ge(sem("mla_taken"), 5)
            dve.wait_ge(sem("mla_squares"), 2)
            qr, kr = MQ[:, 8:12], MI[:, 5:6]
            v.tensor_scalar(flat(qr), flat(qr), col("q_rope"), None, ALU.mult)
            v.tensor_scalar(flat(kr), flat(kr), col("k_rope"), None, ALU.mult).then_inc(sem("mla_rope_in"), 1)
            dve.wait_ge(sem("mla_roots"), 2)
            step(v.reciprocal(flat(RQ), flat(RQ)))
            step(v.reciprocal(flat(RK), flat(RK)))
            v.scalar_tensor_tensor(out=flat(MQ[:, 0:8]), in0=flat(MQ[:, 0:8]), scalar=col("q_nope"), in1=flat(RQ),
                                   op0=ALU.mult, op1=ALU.mult)
            v.scalar_tensor_tensor(out=flat(MK), in0=flat(MK), scalar=col("k_nope"), in1=flat(RK),
                                   op0=ALU.mult, op1=ALU.mult)
            dve.wait_ge(sem("angles_done"), 1)
            dve.wait_ge(sem("mla_swapped"), 1)
            rot = KRP[:, 0:5]
            mul(rot[:, 0:4], tiles_of(4, 4), over(sines[:, 0, :], 4))
            mul(rot[:, 4:5], tiles_of(6, 1), sines)
            mul(qr, qr, over(cosines[:, 0, :], 4))
            step(mul(kr, kr, cosines))
            tt_(qr, qr, rot[:, 0:4], ALU.add)
            step(tt_(kr, kr, rot[:, 4:5], ALU.add))
            step(v.memset(flat(KRP), 0.0))
            for q in range(2):
                rows = slice(HD * q, HD * (q + 1))
                mul(qr[rows], qr[rows], RQ[rows, q:8:2, :])
                last = mul(KRP[rows, q:8:2, :], RK[rows, q:8:2, :], kr[rows, 0, :].unsqueeze(1).to_broadcast([HD, 4, T]))
            last.then_inc(sem("mla_qk"), 1)
            dve.wait_ge(sem("mla_scores"), 1)
            diag = S1[:, :, P:T]
            v.tensor_copy(S1[:, :, 0:P], tiles_of(2, 8)[:, :, 0:P])
            mul(diag, tiles_of(2, 8)[:, :, P:T], per_head("past", 8))
            step(mul(S0, bank(0, 2).rearrange("p (h s) -> p h s", s=P), per_head("past", 8)))
            tt_(diag, diag, per_head("future_penalty", 8), ALU.add)
            step(tt_(S0, S0, per_head("future_penalty", 8), ALU.add))
            v.tensor_reduce(small[:, 0:8], S0, AX.X, ALU.max)
            step(v.tensor_reduce(small[:, 8:16], S1, AX.X, ALU.max))
            v.tensor_scalar(small[:, 0:16], small[:, 0:16], -(192 ** -0.5), None, ALU.mult).then_inc(sem("mla_max"), 1)
            dve.wait_ge(sem("mla_exp"), 1)
            step(v.reciprocal(small[:, 16:32], small[:, 16:32]))
            mul(S0, S0, small[:, 16:24].unsqueeze(2).to_broadcast([P, 8, P]))
            mul(S1, S1, small[:, 24:32].unsqueeze(2).to_broadcast([P, 8, T])).then_inc(sem("mla_probs"), 1)
            dve.wait_ge(sem("mla_out"), 1)
            operand(flat(XL[:, 0:8]), bank(0, 4), flat(XH[:, 0:8]))
            residual("mla_out")

            norm(H[:], KT, ("norm_gains", 56))
            feed_forward("ffn_3")
            per_layer("ple_1", 1)


def by_output(w):
    n = w.shape[1] // (2 * P)
    return w.reshape(KT, P, n, 2, P).transpose(2, 1, 3, 0, 4).reshape(n, P, SLAB)


def by_token(w):
    n = w.shape[1] // (2 * P)
    return w.reshape(KT, P, n, 2 * P).transpose(2, 1, 0, 3).reshape(n, P, SLAB)


def by_input(w):
    n = w.shape[0] // (2 * P)
    return w.reshape(n, 2, P, D).transpose(0, 2, 1, 3).reshape(n, P, SLAB)


def feed_forward(first, second, down):
    a, b, c = by_output(first), by_output(second), by_input(down)
    out = [a[0], b[0]]
    for i in range(1, FP):
        out += [a[i], b[i], c[i - 1]]
    return np.stack(out + [c[FP - 1]])


def kernel(**inputs):
    import concourse.bacc as _bacc
    from concourse.bass_utils import run_bass_kernel_spmd as _run

    a = {n: np.asarray(v) for n, v in inputs.items()}
    wc = a["w_comb"][0]
    conv_end, sb_end, gate_end = 3 * W, 6 * W, 6 * W + 3 * D
    ew = a["even_w_in_2"][0]
    mi = a["mla_w_in_2"][0]
    qb = a["mla_w_q_b_2"][0].reshape(3, P, HEADS, 192)
    kvb = a["mla_w_kv_b_2"][0].reshape(2, P, HEADS, 256)
    q_tiles = np.concatenate([
        qb[:, :, :, :P].transpose(0, 1, 2, 3),
        qb[:, :, :, P:].reshape(3, P, 4, P)], axis=2)
    q_slabs = q_tiles.reshape(3, P, 3, 4, P).transpose(2, 1, 3, 0, 4).reshape(3, P, 12 * P)
    q_slabs = np.concatenate([q_slabs, q_slabs[:, :, :4 * P]], axis=2)
    k_slab = kvb[:, :, :, :P].transpose(1, 2, 0, 3).reshape(1, P, SLAB)
    v_slab = kvb[:, :, :, P:].reshape(2, P, 1024).transpose(1, 0, 2).reshape(1, P, SLAB)
    ffw = [feed_forward(a["ffn_w_gate_2"][i, j], a["ffn_w_up_2"][i, j], a["ffn_w_down_2"][i, j])
           for i in range(2) for j in range(2)]
    parts = {
        "conv": by_output(wc[:, :conv_end]),
        "sb_qk": by_output(wc[:, conv_end:conv_end + 2 * W]),
        "sb_v": by_token(wc[:, conv_end + 2 * W:sb_end]),
        "gates": by_output(wc[:, sb_end:gate_end]),
        "rwkv": by_output(wc[:, gate_end:]),
        "branch": a["branch_proj"][0].reshape(3, 4, P, 2, 4, P).transpose(0, 3, 2, 4, 1, 5).reshape(6, P, SLAB),
        "mix_out": by_output(a["w_mix_out"][0]),
        "ca_k": by_output(a["ca_wkv"][0][:, :D]),
        "ca_v": by_token(a["ca_wkv"][0][:, D:]),
        "ca_q": by_output(a["ca_wq"][0]),
        "ca_o": by_output(a["ca_wo"][0]),
        "ffn_c": feed_forward(a["ffn_up"][0][:, :F], a["ffn_up"][0][:, F:], a["ffn_down"][0]),
        "ffn_0": ffw[0], "ffn_1": ffw[1], "ffn_2": ffw[2], "ffn_3": ffw[3],
        "even_in": by_output(np.concatenate([ew[:, :W], ew[:, 2 * W:4 * W], ew[:, 5 * W:]], axis=1)),
        "even_v": by_token(np.concatenate([ew[:, W:2 * W], ew[:, 4 * W:5 * W]], axis=1)),
        "even_out": by_output(a["even_w_out_2"][0]),
        "ple_0": np.concatenate([by_input(a["ple_w_proj_2"][0]), by_output(a["ple_w_gate_2"][0])]),
        "ple_1": np.concatenate([by_input(a["ple_w_proj_2"][1]), by_output(a["ple_w_gate_2"][1])]),
        "mla_in": by_output(np.concatenate([mi, mi[:, -HD:]], axis=1)),
        "mla_q": q_slabs,
        "mla_kv": np.concatenate([k_slab, v_slab]),
        "mla_out": by_output(a["mla_w_out_2"][0]),
    }
    for name, n in STREAM:
        assert parts[name].shape == (n, P, SLAB), name

    def cols(v):
        return np.ascontiguousarray(v).reshape(-1, P).T

    inv_freq = ROPE_THETA ** (-np.arange(0, HD, 2, dtype=np.float32) / np.float32(HD))
    qn, kn = a["mla_q_norm_2"][0], a["mla_k_norm_2"][0]
    tables = {
        "norm_mix": a["norm_mix"], "conv_w": a["conv_w"], "mu": a["mu_rwkv"], "w0": a["w0"], "a0": a["a0"],
        "k_k": a["k_k"], "k_a": a["k_a"], "r_k": a["r_k"], "lnx_w": a["lnx_w"], "lnx_b": a["lnx_b"],
        "gate_b": a["gate_b"], "norm_ca": a["norm_ca"], "norm_mem": a["norm_mem"], "norm_ffn": a["norm_ffn"],
        "ffn_conv_w": a["ffn_conv_w"], "ffn_conv_b": a["ffn_conv_b"], "norm_final": a["norm_final"],
        "norm_gains": a["norm_gains_2"], "hgrn_lb": a["hgrn_lb_raw_2"], "hgrn_out_norm": a["hgrn_out_norm_2"],
        "q_a_norm": a["mla_q_a_norm_2"], "kv_a_norm": a["mla_kv_a_norm_2"],
        "q_nope": qn[:P], "q_rope": np.concatenate([qn[P:], qn[P:]]),
        "k_nope": kn[:P], "k_rope": np.concatenate([kn[P:], kn[P:]]),
        "inv_freq": np.tile(inv_freq.astype(np.float32), 4),
    }
    arrays = {
        "w_stream": np.concatenate([parts[n] for n, _ in STREAM]),
        "x_t": a["x"][0].T,
        "mem_t": a["mem"][0].T,
        "ple_t": a["p_2"][:, 0].transpose(0, 2, 1),
        "params": np.concatenate([cols(tables[n]) for n, _ in COLUMNS], axis=1),
        "tables": constant_tables(),
        "wa_lora": np.concatenate([a["w_lora"][0], a["a_lora"][0]]),
        "g_lora": a["g_lora"][0],
        "spatial_t": a["gmlp_w_s_2"][0].transpose(2, 0, 1),
        "spatial_b": a["gmlp_b_s_2"].reshape(1, HEADS * P),
        "v_gain": a["gmlp_v_norm_2"].reshape(1, W),
        "positions": a["positions_2"].reshape(1, T),
    }
    nc = _bacc.Bacc("TRN2", target_bir_lowering=False, num_devices=1)
    ins, given = {}, {}
    for name, v in arrays.items():
        v = np.ascontiguousarray(v)
        given[f"in_{name}"] = v
        ins[name] = nc.dram_tensor(f"in_{name}", v.shape, mybir.dt.from_np(v.dtype), kind="ExternalInput").ap()
    out = nc.dram_tensor("out_t", (D, T), F32, kind="ExternalOutput").ap()
    program(nc, ins, out)
    r = _run(nc, [given], core_ids=[0])
    return np.ascontiguousarray(r.results[0]["out_t"].T)[None]
```

```python
from contextlib import ExitStack

import numpy as np
import concourse.bass as bass
from concourse import mybir

F32 = mybir.dt.float32
F32R = mybir.dt.float32r
I32 = mybir.dt.int32
ALU = mybir.AluOpType
ACT = mybir.ActivationFunctionType
AX = mybir.AxisListType

P = 128
T = 256
D = 1024
KT = D // P
W = 512
WT = W // P
HEADS = 8
HD = 64
F = 2816
FP = F // (2 * P)
SLAB = 16 * P
CH = 64
EPS = 1e-6
GN_EPS = 64e-5
DECAY_SCALE = float(np.exp(-0.5))
ROPE_THETA = 10000.0
NEG_BIG = -1e30

STREAM = [
    ("conv", 6), ("sb_qk", 4), ("sb_v", 2), ("rwkv", 7), ("gates", 12), ("branch", 6), ("mix_out", 4),
    ("ca_k", 4), ("ca_v", 4), ("ca_q", 4), ("ca_o", 4), ("ffn_c", 33),
    ("ffn_0", 33), ("even_in", 8), ("even_v", 4), ("even_out", 4), ("ffn_1", 33), ("ple_0", 5),
    ("ffn_2", 33), ("mla_in", 3), ("mla_q", 3), ("mla_kv", 2), ("mla_out", 4), ("ffn_3", 33), ("ple_1", 5),
]
START = {}
N_SLABS = 0
for _name, _n in STREAM:
    START[_name] = N_SLABS
    N_SLABS += _n

STAGES = ["mix_out", "ca_o", "ffn_c", "final", "ffn_0", "even_out", "ffn_1", "ple_0", "ffn_2", "mla_out", "ffn_3",
          "ple_1"]

COLUMNS = [
    ("norm_mix", 8), ("conv_w", 12), ("mu", 14), ("w0", 4), ("a0", 4), ("k_k", 4), ("k_a", 4), ("r_k", 4),
    ("lnx_w", 4), ("lnx_b", 4), ("gate_b", 24), ("norm_ca", 8), ("norm_mem", 8), ("norm_ffn", 8),
    ("ffn_conv_w", 132), ("ffn_conv_b", 44), ("norm_final", 8), ("norm_gains", 80), ("hgrn_lb", 4),
    ("hgrn_out_norm", 1), ("q_a_norm", 3), ("kv_a_norm", 2), ("q_nope", 1), ("q_rope", 1), ("k_nope", 1),
    ("k_rope", 1), ("inv_freq", 1),
]
COL = {}
N_COLS = 0
for _name, _n in COLUMNS:
    COL[_name] = N_COLS
    N_COLS += _n

LEVELS = [1, 2, 4, 8, 16, 32, 64]
TABLES = ["identity", "ones", "head_ones", "before", "before_chunk", "upto_chunk", "upto", "past", "future_penalty",
          "after", "first_half", "middle", "pair_middle", "swap"] + \
    [f"level{b}" for b in LEVELS]


def constant_tables():
    s, t = np.meshgrid(np.arange(P), np.arange(P), indexing="ij")
    tab = {
        "identity": s == t,
        "ones": np.ones((P, P)),
        "head_ones": s // HD == t // HD,
        "before": s < t,
        "before_chunk": (s < t) & (s // CH == t // CH),
        "upto_chunk": (s <= t) & (s // CH == t // CH),
        "upto": s <= t,
        "past": s >= t,
        "future_penalty": np.where(s >= t, 0.0, NEG_BIG),
        "first_half": s < HD,
        "middle": t == HD,
        "pair_middle": t == HD + s // HD,
        "after": s > t,
    }
    half = HD // 2
    swap = np.zeros((P, P))
    for base in (0, HD):
        for j in range(half):
            swap[base + half + j, base + j] = -1.0
            swap[base + j, base + half + j] = 1.0
    tab["swap"] = swap
    for b in LEVELS:
        tab[f"level{b}"] = (s // (2 * b) == t // (2 * b)) & (s % (2 * b) < b) & (t % (2 * b) >= b)
    return np.ascontiguousarray(np.stack([tab[n].astype(np.float32) for n in TABLES], axis=1))


def program(nc, ins, out_t):
    ctx = ExitStack()
    with ctx:
        def sb(name, shape, dt=F32):
            return ctx.enter_context(nc.sbuf_tensor(name, shape, dt))

        sems = {}

        def sem(name):
            if name not in sems:
                sems[name] = ctx.enter_context(nc.semaphore(name))
            return sems[name]

        ring_raw = sb("ring_raw", [P, 3, SLAB])
        ring_hi = sb("ring_hi", [P, 3, SLAB], F32R)
        ring_lo = sb("ring_lo", [P, 3, SLAB], F32R)
        XH = sb("operand_hi", [P, 20, T], F32R)
        XL = sb("operand_lo", [P, 20, T], F32R)
        HH = sb("hidden_hi", [P, 2, 2, T], F32R)
        HL = sb("hidden_lo", [P, 2, 2, T], F32R)
        zeros = sb("zeros", [P, T], F32R)
        H = sb("residual", [P, KT, T])
        prm = sb("params", [P, N_COLS])
        tab = sb("tables", [P, len(TABLES), P])
        root = sb("root", [P, T + 2])
        inv = sb("inv", [P, T + 2])
        one_minus_mu = sb("one_minus_mu", [P, 14])
        small = sb("small", [P, 64])
        U = 1024
        arena = sb("arena", [P, 16 * U])
        PS = ctx.enter_context(nc.psum_tensor("PS", [P, 8, 512], F32))

        def area(start, tiles, width=T):
            a = int(start * U)
            return arena[:, a:a + tiles * width].rearrange("p (n t) -> p n t", t=width)

        def col(name, i=0, n=1):
            return prm[:, COL[name] + i:COL[name] + i + n]

        def table(name):
            return tab[:, TABLES.index(name), :]

        def per_head(name, n=4):
            return table(name).unsqueeze(1).to_broadcast([P, n, P])

        def bank(b, n=1):
            return PS[:, b:b + n, :].rearrange("p b c -> p (b c)")

        def tiles_of(b, n):
            return bank(b, (n + 1) // 2).rearrange("p (n t) -> p n t", t=T)[:, 0:n, :]

        def flat(ap):
            return ap.rearrange("p n t -> p (n t)")

        squares = area(12, 8)
        silu_out, hidden = flat(area(14, 2)), flat(area(14.5, 2))
        conv_x = [area(0, 2), area(0.5, 2)]
        conv_acc = area(15, 2)
        conv_acc2 = area(15.5, 2)
        conv_in = area(0, 12)
        conv_u, conv_y = area(3, 4), area(4, 4)
        sbq = area(5, 8)
        sbv = area(7, 2, W)
        sb_z = [flat(area(8 + 1.5 * q, 6)) for q in range(2)]
        sb_w = [flat(area(11 + 1.5 * q, 6)) for q in range(2)]
        rp = area(0, 14)
        shift_in = [area(14, 2), area(14.5, 2)]
        R_, K_, V_, LORA = rp[:, 0:4], rp[:, 4:8], rp[:, 8:12], rp[:, 12:14]
        A_, G_, KK, BN = (area(3.5 + i, 4) for i in range(4))
        LW, LC, EP, TM = (area(7.5 + i, 4) for i in range(4))
        lora_w = area(11.5, 2, W)
        Vt, Kt, Bt = area(7.5, 1, W), area(8, 1, W), area(8.5, 1, W)
        ZP = area(9, 8, P)
        Xm, Ym, Yt, Fm, Xb = (area(10 + i, 8, P) for i in range(5))
        MT = area(15, 4, HD)
        state = area(15.25, 4, HD)
        chunk_decay = small[:, 0:16].rearrange("p (f c) -> p f c", c=4)
        gates = area(0, 24)
        merged, gated = area(6, 8), area(8, 4)
        mem = area(10, 8)
        ca_k, ca_v, ca_q = area(2, 8), area(4, 2, D), area(6, 8)
        probs, probs_t = area(8, 8), area(10, 8)
        ev = area(0, 16)
        AU, BQ, BF, BG = ev[:, 0:4], ev[:, 4:8], ev[:, 8:12], ev[:, 12:16]
        AV, BI = area(4, 2, W), area(5, 2, W)
        spatial_b = arena[0:1, 6 * U:7 * U]
        KB, BC = area(6, 4), area(7, 4)
        DIF = [area(8, 4), area(9, 4)]
        XM = [area(10, 4), area(11, 4)]
        AT = area(12, 8, P)
        AC, AM = area(13, 4, P), area(13.5, 4, P)
        spatial_w = area(14, 8, P)
        v_gain = area(15, 1, W)
        ple_in = area(4, 2)
        ple_p, ple_g, ple_add = area(0, 8), area(2, 8), area(6, 8)
        MI, MQ, MK, MV = area(0, 6), area(1.5, 12), area(4.5, 8), area(6.5, 2, D)
        KRP = area(12.5, 8)
        msq = area(9.5, 12)
        cosines, sines = area(15.5, 1), area(15.75, 1)
        ang, turns = area(9, 1), area(9.25, 1)
        latent_rs = area(14, 2)
        head_rs = arena[0:8, int(9 * U):int(9.5 * U)]
        pick_head = arena[0:8, int(14.5 * U):int(15.5 * U)].rearrange("p (h c) -> p h c", c=P)
        pick_pair = arena[0:8, int(8.5 * U):int(9 * U)].rearrange("p (h c) -> p h c", c=P)
        S0, S1 = area(8.5, 8, P), area(9.5, 8)
        PT0, PT1 = area(11.5, 8), area(13.5, 8, P)

        landed = [sem(f"landed{s}") for s in range(3)]
        hi_split, lo_split = sem("hi_split"), sem("lo_split")
        multiplied = sem("multiplied")

        def chunks_until(stage, chunks=4):
            return 4 * STAGES.index(stage) + chunks

        def place(g0, i=0, by=3):
            return g0 % 3, i * (by // 3) + g0 // 3, i * by + g0

        block = ctx.enter_context(nc.Block())

        @block.sync
        def _(sp):
            stream = ins["w_stream"]
            for g in range(3):
                sp.dma_start(ring_raw[:, g, :], stream[g]).then_inc(landed[g], 16)
            turns_ = (N_SLABS - 3) // 3
            with sp.Fori(0, turns_) as i:
                for j in range(3):
                    sp.wait_ge(lo_split, i * 3 + (j + 1))
                    sp.dma_start(ring_raw[:, j, :], stream[bass.ds(i * 3 + (j + 3), 1)].squeeze(0))\
                        .then_inc(landed[j], 16)
            for g in range(3 + 3 * turns_, N_SLABS):
                sp.wait_ge(lo_split, g - 2)
                sp.dma_start(ring_raw[:, g % 3, :], stream[g]).then_inc(landed[g % 3], 16)
            sp.wait_ge(sem("residual_ready"), chunks_until("ple_1"))
            sp.dma_start(out_t.rearrange("(k p) t -> p k t", p=P), H[:]).then_inc(sem("stored"), 16)
            sp.wait_ge(sem("stored"), 16)

        @block.gpsimd
        def _(pool):
            adds = [0]

            def add(out, a, b):
                return nc.gpsimd.tensor_tensor(out, a, b, ALU.add)

            def step(ins_):
                adds[0] += 1
                ins_.then_inc(sem("pool_step"), 1)
                pool.wait_ge(sem("pool_step"), adds[0])

            norms = [0]

            def norm_fold():
                norms[0] += 1
                pool.wait_ge(sem("norm_squared"), norms[0])
                step(add(squares[:, 0:4], squares[:, 0:4], squares[:, 4:8]))
                step(add(squares[:, 0:2], squares[:, 0:2], squares[:, 2:4]))
                add(squares[:, 0], squares[:, 0], squares[:, 1]).then_inc(sem("norm_folded"), 1)

            folds = [0]

            def ple_fold(n):
                pool.wait_ge(sem("ple_squared"), 4 * n + 3)
                step(add(squares[:, 0:2], squares[:, 0:2], squares[:, 2:4]))
                add(squares[:, 0:2], squares[:, 0:2], squares[:, 4:6]).then_inc(sem("ple_folded"), 1)

            nc.gpsimd.memset(zeros[:].bitcast(F32), 0.0)
            for c in range(4):
                pool.wait_ge(sem(f"x_landed{c}"), 16)
            pool.dma_start(tab[:], ins["tables"]).then_inc(sem("tables_landed"), 16)
            norm_fold()
            pool.wait_ge(sem("operand_lo"), KT + 2)
            pool.dma_start(lora_w[:, 0, :], ins["wa_lora"]).then_inc(sem("lora_landed"), 16)
            pool.dma_start(lora_w[:, 1, :], ins["g_lora"]).then_inc(sem("lora_landed"), 16)
            pool.wait_ge(sem("operand_lo"), KT + 3)
            pool.dma_start(mem, ins["mem_t"].rearrange("(k p) t -> p k t", p=P)).then_inc(sem("mem_landed"), 16)
            for _ in range(5):
                norm_fold()
            pool.wait_ge(sem("residual_ready"), chunks_until("ffn_0"))
            pool.dma_start(spatial_w, ins["spatial_t"]).then_inc(sem("spatial_landed"), 16)
            pool.dma_start(spatial_b, ins["spatial_b"]).then_inc(sem("spatial_landed"), 16)
            pool.dma_start(v_gain[:, 0, :], ins["v_gain"].to_broadcast([P, W])).then_inc(sem("spatial_landed"), 16)
            norm_fold()
            for n, (before, folds_) in enumerate((("even_out", 2), ("mla_out", 2))):
                pool.wait_ge(sem("residual_ready"), chunks_until(before))
                if n == 0:
                    pool.dma_start(cosines.bitcast(I32)[:, 0, :], ins["positions"].to_broadcast([P, T]))\
                        .then_inc(sem("positions_landed"), 16)
                pool.dma_start(ple_in, ins["ple_t"][n].rearrange("(k p) t -> p k t", p=P))\
                    .then_inc(sem("ple_landed"), 16)
                for _ in range(folds_):
                    norm_fold()
                ple_fold(n)
                if n == 0:
                    norm_fold()
                    norm_fold()

        @block.tensor
        def _(pe):
            taken = [0]
            split_tiles = [0]

            def mm(out, lhs, rhs, start=True, stop=True):
                return nc.tensor.matmul(out, lhs, rhs, start=start, stop=stop, skip_group_check=True)

            def block_product(out, slot, b, xh, xl, start, stop):
                w = slice(b * P, (b + 1) * P)
                mm(out, ring_hi[:, slot, w], xh, start, False)
                mm(out, ring_hi[:, slot, w], xl, False, False)
                return mm(out, ring_lo[:, slot, w], xh, False, stop)

            def output_slab(g0, x0, out, i=0, by=3, fresh=()):
                slot, _, g = place(g0, i, by)
                pe.wait_ge(lo_split, g + 1)
                for m in range(2):
                    for k in range(KT):
                        if m == 0 and k in fresh:
                            operands(1)
                        last = block_product(out[:, m * T:(m + 1) * T], slot, m * KT + k,
                                             XH[:, x0 + k, :], XL[:, x0 + k, :], k == 0, k == KT - 1)
                last.then_inc(multiplied, 1)

            def operands(n):
                split_tiles[0] += n
                pe.wait_ge(sem("operand_lo"), split_tiles[0])

            def free_bank(i=0):
                if taken[0] >= 3:
                    pe.wait_ge(sem("output_taken"), taken[0] - 2)
                b = taken[0] % 3
                taken[0] += 1
                return b

            def project(name, x0, n, fresh=(), norm=False, by_token=False):
                for j in range(n):
                    output_slab(START[name] + j, x0, bank(free_bank()), fresh=fresh if j == 0 else ())
                    if norm and j == min(1, n - 1):
                        norm_sum(by_token)

            def project_by_token(name, x0, n):
                for j in range(n):
                    out = bank(free_bank())
                    slot, _, g = place(START[name] + j)
                    pe.wait_ge(lo_split, g + 1)
                    for tt in range(2):
                        tok = slice(tt * P, (tt + 1) * P)
                        for k in range(KT):
                            w = slice(k * T, (k + 1) * T)
                            o = out[:, tt * T:(tt + 1) * T]
                            mm(o, XH[:, x0 + k, tok], ring_hi[:, slot, w], k == 0, False)
                            mm(o, XL[:, x0 + k, tok], ring_hi[:, slot, w], False, False)
                            last = mm(o, XH[:, x0 + k, tok], ring_lo[:, slot, w], False, k == KT - 1)
                    last.then_inc(multiplied, 1)

            norms = [0]

            def norm_sum(by_token=False, b=7):
                norms[0] += 1
                pe.wait_ge(sem("norm_folded"), norms[0])
                last = mm(bank(b)[:, 0:T], table("ones"), squares[:, 0, :])
                if by_token:
                    for tt in range(2):
                        last = mm(bank(b)[:, T + tt:T + tt + 1], squares[:, 0, tt * P:(tt + 1) * P],
                                  table("ones")[:, 0:1])
                last.then_inc(sem("norm_summed"), 1)

            ffns = [0]
            EVERY = tuple(range(KT))

            def feed_forward(name):
                g0, n = START[name], ffns[0]
                split, gate_scaled, up_taken = sem("hidden_lo"), sem("gate_scaled"), sem("up_taken")

                def down(at, odd, i, pairs):
                    slot, _, g = place(at, i, 6)
                    pe.wait_ge(lo_split, g + 1)
                    pe.wait_ge(split, pairs)
                    for k in range(2):
                        for m in range(KT):
                            last = block_product(bank(3 + m // 2)[:, m % 2 * T:(m % 2 + 1) * T], slot, k * KT + m,
                                                 HH[:, odd, k, :], HL[:, odd, k, :], False, False)
                    last.then_inc(multiplied, 1)

                output_slab(g0, 0, bank(0), fresh=EVERY)
                output_slab(g0 + 1, 0, bank(1))
                for b in range(3, 7):
                    for m in range(2):
                        mm(bank(b)[:, m * T:(m + 1) * T], zeros[:, 0:P], zeros[:], True, False)
                norm_sum()
                with pe.Fori(0, FP // 2) as i:
                    pe.wait_ge(gate_scaled, i * 2 + (n * FP + 1))
                    output_slab(g0 + 2, 0, bank(2), i, 6)
                    pe.wait_ge(sem("norm_root"), norms[0])
                    pe.wait_ge(up_taken, i * 2 + (n * FP + 1))
                    output_slab(g0 + 3, 0, bank(7), i, 6)
                    down(g0 + 4, 0, i, i * 2 + (n * FP + 1))
                    pe.wait_ge(gate_scaled, i * 2 + (n * FP + 2))
                    output_slab(g0 + 5, 0, bank(0), i, 6)
                    pe.wait_ge(up_taken, i * 2 + (n * FP + 2))
                    output_slab(g0 + 6, 0, bank(1), i, 6)
                    down(g0 + 7, 1, i, i * 2 + (n * FP + 2))
                slot, _, g = place(g0 + 32)
                pe.wait_ge(lo_split, g + 1)
                pe.wait_ge(split, (n + 1) * FP)
                for m in range(KT):
                    for k in range(2):
                        last = block_product(bank(3 + m // 2)[:, m % 2 * T:(m % 2 + 1) * T], slot, k * KT + m,
                                             HH[:, 0, k, :], HL[:, 0, k, :], False, k == 1)
                    if m % 2 and m < KT - 1:
                        last.then_inc(sem("down_bank"), 1)
                last.then_inc(multiplied, 1)
                ffns[0] += 1

            def residual_project(name, x0, fresh):
                for j in range(4):
                    output_slab(START[name] + j, x0, bank((6, 7, 4, 5)[j]), fresh=fresh if j == 0 else ())

            for j in range(6):
                output_slab(START["conv"] + j, 0, bank(free_bank()), fresh=EVERY if j == 0 else ())
                if j == 1:
                    pe.wait_ge(sem("tables_landed"), 16)
                    norm_sum(True)
            project("sb_qk", 0, 4)
            project_by_token("sb_v", 0, 2)

            pe.wait_ge(sem("output_taken"), taken[0])
            for q in range(2):
                rows = slice(HD * q, HD * (q + 1))
                if q:
                    pe.wait_ge(sem("sb_z_taken"), q)
                for f in range(4):
                    qt, kt = sbq[rows, f, :], sbq[rows, 4 + f, :]
                    o = slice(f * P, (f + 1) * P)
                    mm(bank(0)[:, o], kt[:, 0:P], qt[:, 0:P])
                    mm(bank(1)[:, o], kt[:, 0:P], qt[:, P:T])
                    last = mm(bank(2)[:, o], kt[:, P:T], qt[:, P:T])
                last.then_inc(sem("sb_z"), 1)
            for q in range(2):
                pe.wait_ge(sem("sb_log"), q + 1)
                if q:
                    pe.wait_ge(sem("sb_logw"), q)
                z = sb_z[q]
                mm(bank(3), table("after"), z[:, 0:512])
                mm(bank(4), table("after"), z[:, 512:1024], True, False)
                mm(bank(4), table("ones"), z[:, 1024:1536], False, True)
                mm(bank(5), table("after"), z[:, 1024:1536]).then_inc(sem("sb_suffix"), 1)
            for q in range(2):
                pe.wait_ge(sem("sb_att"), q + 1)
                w = sb_w[q].rearrange("p (b f t) -> p b f t", b=3, f=4)
                for f in range(4):
                    o = bank(6 + f // 2)[HD * q:HD * (q + 1), f % 2 * T:(f % 2 + 1) * T]
                    h = slice((2 * f + q) * HD, (2 * f + q + 1) * HD)
                    mm(o[:, 0:P], sbv[:, 0, h], w[:, 0, f, :])
                    mm(o[:, P:T], sbv[:, 0, h], w[:, 1, f, :], True, False)
                    last = mm(o[:, P:T], sbv[:, 1, h], w[:, 2, f, :], False, True)
            last.then_inc(sem("sb_y"), 1)

            for j in range(7):
                output_slab(START["rwkv"] + j, 0, bank(free_bank()))
            pe.wait_ge(sem("lora_landed"), 32)
            pe.wait_ge(sem("rk_lora_in"), 1)
            pe.wait_ge(sem("output_taken"), taken[0])
            pe.wait_ge(sem("operand_lo"), KT + 2)
            for f in range(4):
                c = slice(f * P, (f + 1) * P)
                o = slice(f % 2 * T, (f % 2 + 1) * T)
                mm(bank(0 + f // 2)[:, o], lora_w[0:HD, 0, c], LORA[0:HD, 0, :])
                mm(bank(2 + f // 2)[:, o], lora_w[HD:P, 0, c], LORA[HD:P, 0, :])
                last = mm(bank(4 + f // 2)[:, o], lora_w[:, 1, c], LORA[:, 1, :])
            last.then_inc(sem("rk_lora_out"), 1)
            pe.wait_ge(sem("rk_squares"), 1)
            for h in range(2):
                last = mm(bank(6 + h), table("head_ones"), flat(TM)[:, 512 * h:512 * (h + 1)])
            last.then_inc(sem("rk_norms"), 1)
            pe.wait_ge(sem("rk_bonus_in"), 1)
            for h in range(2):
                last = mm(bank(6 + h), table("head_ones"), flat(BN)[:, 512 * h:512 * (h + 1)])
            last.then_inc(sem("rk_bonus_sums"), 1)
            pe.wait_ge(sem("rk_prep"), 1)

            def heads(q):
                return [(f, 2 * f + q) for f in range(4)]

            for tt in range(2):
                tok = slice(tt * P, (tt + 1) * P)
                if tt:
                    pe.wait_ge(sem("rk_tile_done"), 1)
                for f in range(4):
                    c = slice(f * P, (f + 1) * P)
                    nc.tensor.transpose(bank(0)[:, c], V_[:, f, tok], table("identity"))
                    nc.tensor.transpose(bank(1)[:, c], KK[:, f, tok], table("identity"))
                    nc.tensor.transpose(bank(2)[:, c], K_[:, f, tok], table("identity"))
                    last = nc.tensor.transpose(bank(3)[:, c], A_[:, f, tok], table("identity"))
                last.then_inc(sem("rk_turned"), 1)
                for q in range(2):
                    rows = slice(HD * q, HD * (q + 1))
                    for f in range(4):
                        c = slice(f * P, (f + 1) * P)
                        mm(bank(4 + q)[:, c], K_[rows, f, tok], KK[rows, f, tok])
                        last = mm(bank(6 + q)[:, c], A_[rows, f, tok], KK[rows, f, tok])
                last.then_inc(sem("rk_pairs"), 1)
                pe.wait_ge(sem("rk_masked"), tt + 1)
                pe.wait_ge(sem("rk_turned_act"), tt + 1)
                for q in range(2):
                    for f, h in heads(q):
                        last = mm(bank(0)[:, h * HD:(h + 1) * HD], Fm[:, 4 * q + f, :], Vt[:, 0, h * HD:(h + 1) * HD])
                last.then_inc(sem("rk_p"), 1)
                pe.wait_ge(sem("rk_p_taken"), tt + 1)
                for li in range(6):
                    for q in range(2):
                        n = (tt * 6 + li) * 2 + q
                        pe.wait_ge(sem("rk_x"), n + 1)
                        if li:
                            pe.wait_ge(sem("rk_y"), n - 1)
                        for f in range(4):
                            rhs = Yt[:, 4 * q + f, :] if li else table("identity")
                            last = mm(bank(1 + q)[:, f * P:(f + 1) * P], Xb[:, 4 * q + f, :], rhs)
                        last.then_inc(sem("rk_f"), 1)
                    for q in range(2):
                        n = (tt * 6 + li) * 2 + q
                        pe.wait_ge(sem("rk_f_taken"), n + 1)
                        for f in range(4):
                            c, e = slice(f * P, (f + 1) * P), 4 * q + f
                            last = mm(bank(3 + q)[:, c], Fm[:, e, :], Ym[:, e, :] if li else table("identity"))
                            if li < 5:
                                last = mm(bank(5 + q)[:, c], Ym[:, e, :] if li else table("identity"), Fm[:, e, :])
                        last.then_inc(sem("rk_dy"), 1)
                pe.wait_ge(sem("rk_y"), (tt + 1) * 12)
                for q in range(2):
                    for f, h in heads(q):
                        last = mm(bank(3 + q)[:, f * P:(f + 1) * P], Ym[:, 4 * q + f, :], ZP[:, h, :])
                last.then_inc(sem("rk_wu"), 1)
                for q in range(2):
                    rows = slice(HD * q, HD * (q + 1))
                    for f in range(4):
                        c = slice(f * P, (f + 1) * P)
                        mm(bank(5 + q)[:, c], K_[rows, f, tok], R_[rows, f, tok])
                        last = mm(bank(1 + q)[:, c], A_[rows, f, tok], R_[rows, f, tok])
                last.then_inc(sem("rk_out_pairs"), 1)
                pe.wait_ge(sem("rk_wu_taken"), tt + 1)
                pe.wait_ge(sem("rk_out_masked"), tt + 1)
                for q in range(2):
                    for f, h in heads(q):
                        e = 4 * q + f
                        mm(bank(7)[HD * q:HD * (q + 1), f * P:(f + 1) * P], Xb[:, e, 0:HD], Fm[:, e, :])
                        o = bank(3)[HD * q:HD * (q + 1), f * P:(f + 1) * P]
                        mm(o, Vt[:, 0, h * HD:(h + 1) * HD], Yt[:, e, :], True, False)
                        last = mm(o, Xb[:, e, HD:P], Fm[:, e, :], False, True)
                last.then_inc(sem("rk_inner"), 1)
                cm = slice(HD, P) if tt == 0 else slice(0, HD)
                for q in range(2):
                    for f, h in heads(q):
                        last = mm(bank(0)[HD * q:HD * (q + 1), f * HD:(f + 1) * HD], Xb[cm, 4 * q + f, 0:HD],
                                  Bt[cm, 0, h * HD:(h + 1) * HD])
                last.then_inc(sem("rk_transition"), 1)
                pe.wait_ge(sem("rk_transition_taken"), tt + 1)
                pe.wait_ge(sem("rk_inner_taken"), tt + 1)
                for c in range(2):
                    gc = 2 * tt + c
                    rows_c = slice(c * CH, (c + 1) * CH)
                    if gc:
                        pe.wait_ge(sem("rk_state"), gc)
                        for q in range(2):
                            rows = slice(HD * q, HD * (q + 1))
                            for f in range(4):
                                last = mm(bank(6 + q)[rows, f * P + c * CH:f * P + (c + 1) * CH], state[rows, f, :],
                                          R_[rows, f, gc * CH:(gc + 1) * CH])
                        if gc != 2:
                            last.then_inc(sem("rk_carried"), 1)
                    if gc == 3:
                        continue
                    for q in range(2):
                        rows = slice(HD * q, HD * (q + 1))
                        for f, h in heads(q):
                            hc = slice(h * HD, (h + 1) * HD)
                            o = bank(5)[rows, f * HD:(f + 1) * HD]
                            mm(o, Kt[rows_c, 0, hc], Vt[rows_c, 0, hc], True, False)
                            last = mm(o, Bt[rows_c, 0, hc], Xb[rows_c, 4 * q + f, HD:P], False, True)
                            if gc:
                                last = mm(bank(1 + q)[rows, f * HD:(f + 1) * HD], MT[rows, f, :], state[rows, f, :])
                    last.then_inc(sem("rk_update"), 1)
            pe.wait_ge(sem("rk_out"), 1)
            for h in range(2):
                last = mm(bank(h), table("head_ones"), flat(KK)[:, 512 * h:512 * (h + 1)])
            last.then_inc(sem("rk_mean"), 1)
            pe.wait_ge(sem("rk_centred"), 1)
            for h in range(2):
                last = mm(bank(2 + h), table("head_ones"), flat(TM)[:, 512 * h:512 * (h + 1)])
            last.then_inc(sem("rk_var"), 1)

            pe.wait_ge(sem("rk_root"), 1)
            with pe.Fori(0, 4) as i:
                for j in range(3):
                    b = (taken[0] + j) % 3
                    pe.wait_ge(sem("output_taken"), i * 3 + (taken[0] + j - 2))
                    output_slab(START["gates"] + j, 0, bank(b), i)
            taken[0] += 12
            operands(3)
            pe.wait_ge(sem("output_taken"), taken[0])
            for j in range(6):
                if j >= 3:
                    pe.wait_ge(sem("branch_taken"), j - 2)
                slot, _, g = place(START["branch"] + j)
                pe.wait_ge(lo_split, g + 1)
                out = bank(2 * (j % 3), 2)
                for m in range(4):
                    for k in range(4):
                        x = 8 + 4 * (j // 2) + k
                        last = block_product(out[:, m * T:(m + 1) * T], slot, 4 * m + k, XH[:, x, :], XL[:, x, :],
                                             k == 0, k == 3)
                last.then_inc(multiplied, 1)
                if j == 2:
                    norm_sum()
            pe.wait_ge(sem("norm_root"), norms[0])
            residual_project("mix_out", 0, (0, 4))

            pe.wait_ge(sem("output_taken"), taken[0])
            pe.wait_ge(sem("branch_taken"), 6)
            operands(KT)
            project("ca_k", 8, 4)
            project_by_token("ca_v", 8, 4)
            norm_sum()
            project("ca_q", 0, 4, fresh=EVERY)
            pe.wait_ge(sem("output_taken"), taken[0])
            for tt in range(2):
                for h in range(4):
                    i = 4 * tt + h
                    for d in range(2):
                        last = mm(bank(i // 2)[:, i % 2 * T:(i % 2 + 1) * T], ca_q[:, 2 * h + d, tt * P:(tt + 1) * P],
                                  ca_k[:, 2 * h + d, :], d == 0, d == 1)
                last.then_inc(sem("ca_scores"), 1)
            for i in range(8):
                tt, h = divmod(i, 4)
                pe.wait_ge(sem("ca_probs"), tt + 1)
                for mt in range(2):
                    last = nc.tensor.transpose(bank(4 + h)[:, mt * T + tt * P:mt * T + (tt + 1) * P],
                                               probs[:, i, mt * P:(mt + 1) * P], table("identity"))
            last.then_inc(sem("ca_turned"), 1)
            pe.wait_ge(sem("ca_turned_taken"), 1)
            for h in range(4):
                for d in range(2):
                    for mt in range(2):
                        last = mm(bank(h)[:, d * T:(d + 1) * T], ca_v[:, mt, (2 * h + d) * P:(2 * h + d + 1) * P],
                                  probs_t[:, 2 * h + mt, :], mt == 0, mt == 1)
                last.then_inc(sem("ca_out"), 1)
            residual_project("ca_o", 8, (0, 2, 4, 6))

            feed_forward("ffn_c")
            norm_sum()

            feed_forward("ffn_0")

            project("even_in", 0, 8, fresh=EVERY, norm=True, by_token=True)
            project_by_token("even_v", 0, 4)
            pe.wait_ge(sem("output_taken"), taken[0])
            pe.wait_ge(sem("spatial_ready"), 1)
            pe.wait_ge(sem("spatial_landed"), 48)
            for f in range(4):
                for q in range(2):
                    h = 2 * f + q
                    for tt in range(2):
                        o = bank(f // 2)[HD * q:HD * (q + 1), f % 2 * T + tt * P:f % 2 * T + (tt + 1) * P]
                        mm(o, AV[:, tt, h * HD:(h + 1) * HD], spatial_w[:, h, :], True, False)
                        last = mm(o, table("ones")[0:1, 0:HD], spatial_b[:, h * P:(h + 1) * P], False, True)
            last.then_inc(sem("spatial_mixed"), 1)
            for li in range(9):
                pe.wait_ge(sem("gl_factors"), li + 1)
                if li >= 2:
                    pe.wait_ge(sem("gl_added"), li - 1)
                if li < 8:
                    for tt in range(2):
                        tok = slice(tt * P, (tt + 1) * P)
                        for h in range(4):
                            k = KB[:, h, tok] if li == 0 else XM[li % 2][:, h, tok]
                            q = BQ[:, h, tok] if li == 0 else XM[li % 2][:, h, tok]
                            last = mm(bank(2 + 2 * (li % 2) + tt)[:, h * P:(h + 1) * P], k, q)
                else:
                    for h in range(4):
                        last = mm(bank(2)[:, h * P:(h + 1) * P], XM[0][:, h, 0:P], XM[0][:, h, P:T])
                last.then_inc(sem("gl_pairs"), 1)
            pe.wait_ge(sem("gl_added"), 9)
            for h in range(4):
                o, c = bank(6 + h // 2)[:, h % 2 * T:(h % 2 + 1) * T], slice(h * P, (h + 1) * P)
                mm(o[:, 0:P], BI[:, 0, c], AT[:, h, :])
                mm(o[:, P:T], BI[:, 1, c], AT[:, 4 + h, :], True, False)
                last = mm(o[:, P:T], BI[:, 0, c], AC[:, h, :], False, True)
            last.then_inc(sem("gl_out"), 1)
            pe.wait_ge(sem("gl_squares"), 1)
            for h in range(2):
                last = mm(bank(2 + h), table("ones"), flat(KB)[:, 512 * h:512 * (h + 1)])
            last.then_inc(sem("gl_norms"), 1)
            operands(2)
            residual_project("even_out", 8, ())

            def per_layer(name, n):
                g0 = START[name]
                operands(1)
                slot, _, g = place(g0)
                pe.wait_ge(lo_split, g + 1)
                for m in range(KT):
                    for k in range(2):
                        last = block_product(bank((0, 1, 2, 7)[m // 2])[:, m % 2 * T:(m % 2 + 1) * T], slot,
                                             k * KT + m, XH[:, 8 + k, :], XL[:, 8 + k, :], k == 0, k == 1)
                last.then_inc(multiplied, 1)
                for j in range(4):
                    output_slab(g0 + 1 + j, 0, bank(3 + j), fresh=EVERY if j == 0 else ())
                    if j == 1:
                        pe.wait_ge(sem("ple_copied"), n + 1)
                        norm_sum()
                pe.wait_ge(sem("ple_folded"), n + 1)
                pe.wait_ge(sem("ple_squared"), 4 * (n + 1))
                for i, k in enumerate((0, 1, 6, 7)):
                    last = mm(bank(0)[:, 0:T], table("ones"), squares[:, k, :], i == 0, i == 3)
                last.then_inc(sem("ple_summed"), 1)

            feed_forward("ffn_1")
            per_layer("ple_0", 0)
            feed_forward("ffn_2")

            project("mla_in", 0, 3, fresh=EVERY, norm=True)
            pe.wait_ge(sem("output_taken"), taken[0])
            for j in range(3):
                slot, _, g = place(START["mla_q"] + j)
                pe.wait_ge(lo_split, g + 1)
                out = bank(2 * j, 2)
                for m in range(4):
                    for k in range(3):
                        if j == 0 and m == 0:
                            operands(1)
                        last = block_product(out[:, m * T:(m + 1) * T], slot, 3 * m + k, XH[:, 8 + k, :],
                                             XL[:, 8 + k, :], k == 0, k == 2)
                last.then_inc(multiplied, 1)
                if j == 0:
                    pe.wait_ge(sem("latent_squared"), 1)
                    for k in range(5):
                        side = k // 3
                        mm(bank(7)[:, side * T:(side + 1) * T], table("ones"), squares[:, k, :], k in (0, 3),
                           k in (2, 4))
                    for tt in range(2):
                        for k in (3, 4):
                            last = mm(bank(6)[:, tt:tt + 1], squares[:, k, tt * P:(tt + 1) * P],
                                      table("ones")[:, 0:1], k == 3, k == 4)
                    last.then_inc(sem("latent_summed"), 1)
            slot, _, g = place(START["mla_kv"])
            pe.wait_ge(lo_split, g + 1)
            operands(2)
            for m in range(8):
                if m in (0, 4):
                    pe.wait_ge(sem("mla_taken"), 1 + m // 4)
                for k in range(2):
                    last = block_product(bank(m // 2)[:, m % 2 * T:(m % 2 + 1) * T], slot, 2 * m + k,
                                         XH[:, 11 + k, :], XL[:, 11 + k, :], k == 0, k == 1)
            last.then_inc(multiplied, 1)

            def head_sums(side):
                o = bank(7)[0:8, side * T:(side + 1) * T]
                for h in range(8):
                    mm(o, table("middle")[:, HD - h:HD - h + 8], msq[:, h, :], h == 0, False)
                if side == 0:
                    for f in range(4):
                        last = mm(o, table("pair_middle")[:, HD - 2 * f:HD - 2 * f + 8], msq[:, 8 + f, :], False, f == 3)
                else:
                    last = mm(o, table("first_half")[:, 0:8], msq[:, 8, :], False, True)
                last.then_inc(sem("mla_sums"), 1)

            def head_factors(side, first):
                r = head_rs[:, side * T:(side + 1) * T]
                for f in range(4):
                    mm(tiles_of(first, 4)[:, f, :], pick_pair[:, f, :], r)
                for h in range(8):
                    last = mm(tiles_of(4, 8)[:, h, :], pick_head[:, h, :], r)
                last.then_inc(sem("mla_factors"), 1)

            pe.wait_ge(sem("mla_squares"), 1)
            pe.wait_ge(sem("latent_roots"), 1)
            head_sums(0)
            slot, _, g = place(START["mla_kv"] + 1)
            pe.wait_ge(lo_split, g + 1)
            pe.wait_ge(sem("mla_taken"), 3)
            for tt in range(2):
                tok = slice(tt * P, (tt + 1) * P)
                for n in range(2):
                    o = bank((4, 5, 6, 0)[2 * tt + n])
                    if (tt, n) == (1, 1):
                        pe.wait_ge(sem("mla_taken"), 4)
                    for k in range(2):
                        w = slice(k * D + n * 512, k * D + (n + 1) * 512)
                        mm(o, XH[:, 11 + k, tok], ring_hi[:, slot, w], k == 0, False)
                        mm(o, XL[:, 11 + k, tok], ring_hi[:, slot, w], False, False)
                        last = mm(o, XH[:, 11 + k, tok], ring_lo[:, slot, w], False, k == 1)
            last.then_inc(multiplied, 1)
            pe.wait_ge(sem("mla_rope_in"), 1)
            for n in range(2):
                last = mm(bank(1 + n), table("swap"), flat(MQ[:, 8:12])[:, 512 * n:512 * (n + 1)])
            last.then_inc(sem("mla_swapped"), 1)
            mm(bank(3)[:, 0:T], table("swap"), MI[:, 0, :]).then_inc(sem("mla_swapped"), 1)
            pe.wait_ge(sem("mla_squares"), 2)
            head_sums(1)
            pe.wait_ge(sem("mla_taken"), 5)
            pe.wait_ge(sem("mla_rotated"), 1)
            pe.wait_ge(sem("head_rs"), 2)
            head_factors(0, 0)
            pe.wait_ge(sem("mla_q_scaled"), 1)
            head_factors(1, 2)
            pe.wait_ge(sem("mla_qk"), 1)
            for h in range(8):
                o = bank(h // 4)[:, h % 4 * P:(h % 4 + 1) * P]
                mm(o, MQ[:, h, 0:P], MK[:, h, 0:P], True, False)
                mm(o, MQ[:, 8 + h // 2, 0:P], KRP[:, h, 0:P], False, True)
                o = bank(2 + h // 2)[:, h % 2 * T:(h % 2 + 1) * T]
                mm(o, MQ[:, h, P:T], MK[:, h, :], True, False)
                last = mm(o, MQ[:, 8 + h // 2, P:T], KRP[:, h, :], False, True)
                if h in (3, 7):
                    last.then_inc(sem("mla_scores"), 1)
            for h in range(8):
                if h in (0, 4):
                    pe.wait_ge(sem("mla_probs"), 1 + h // 4)
                if h == 0:
                    pe.wait_ge(sem("mla_max"), 2)
                o = bank(h // 2)[:, h % 2 * T:(h % 2 + 1) * T]
                nc.tensor.transpose(o[:, 0:P], S0[:, h, :], table("identity"))
                nc.tensor.transpose(o[:, P:T], S1[:, h, 0:P], table("identity"))
                last = nc.tensor.transpose(bank(4 + h // 4)[:, h % 4 * P:(h % 4 + 1) * P], S1[:, h, P:T],
                                           table("identity"))
                if h in (3, 7):
                    last.then_inc(sem("mla_turned"), 1)
            for h in range(8):
                if h in (0, 4):
                    pe.wait_ge(sem("mla_turned_taken"), 1 + h // 4)
                o, c = bank(h // 2)[:, h % 2 * T:(h % 2 + 1) * T], slice(h * P, (h + 1) * P)
                mm(o, MV[:, 0, c], PT0[:, h, :], True, False)
                last = mm(o[:, P:T], MV[:, 1, c], PT1[:, h, :], False, True)
                if h % 2:
                    last.then_inc(sem("mla_out"), 1)
            residual_project("mla_out", 8, (0, 2, 4, 6))

            feed_forward("ffn_3")
            per_layer("ple_1", 1)

        @block.scalar
        def _(act):
            taken = [0]
            splits = [0]
            steps = [0]

            def run(out, in_, func=ACT.Copy, **kw):
                return nc.scalar.activation(out, in_, func, **kw)

            def step(ins_):
                steps[0] += 1
                ins_.then_inc(sem("act_step"), 1)
                act.wait_ge(sem("act_step"), steps[0])

            def split_slab(g0, i=0, by=3):
                if g0 >= N_SLABS:
                    return
                slot, use, g = place(g0, i, by)
                act.wait_ge(landed[slot], (use + 1) * 16)
                if g0 >= 3:
                    act.wait_ge(multiplied, g - 2)
                run(ring_hi[:, slot, :], ring_raw[:, slot, :]).then_inc(hi_split, 1)

            def operand(out, in_, **kw):
                splits[0] += 1
                return run(out, in_, **kw).then_inc(sem("operand_hi"), 1)

            def operand_tiles(tiles, src, gain, x0):
                for k in tiles:
                    operand(XH[:, x0 + k, :], src[:, k, :], scale=col(gain[0], gain[1] + k))

            def chunks(stage, gain, x0=0):
                for c in range(4):
                    act.wait_ge(sem("residual_ready"), chunks_until(stage, c + 1))
                    operand_tiles((2 * c, 2 * c + 1), H, gain, x0)
                run(flat(squares), flat(H[:]), ACT.Square).then_inc(sem("norm_squared"), 1)

            norms = [0]

            def norm_root(by_token=False):
                norms[0] += 1
                w = T + 2 if by_token else T
                act.wait_ge(sem("norm_summed"), norms[0])
                run(root[:, 0:w], bank(7)[:, 0:w], ACT.Sqrt, bias=eps_col(EPS), scale=1.0 / D)\
                    .then_inc(sem("norm_root"), 1)

            def eps_col(value):
                return small[:, {EPS: 32, GN_EPS: 33, 1.0: 34, 0.0: 35}[value]:][:, 0:1]

            ffns = [0]

            def feed_forward(name, conv=False):
                g0, n = START[name], ffns[0]
                up_taken, gate_scaled = sem("up_taken"), sem("gate_scaled")

                def gate(pair, i=0, split=None):
                    if conv:
                        if split is not None:
                            split_slab(split, i, 6)
                        act.wait_ge(sem("conv_done"), pair + 1)
                        run(silu_out, flat(conv_acc), ACT.Silu).then_inc(sem("gate_active"), 1)
                    else:
                        act.wait_ge(gate_scaled, pair + (n * FP + 2))
                        run(silu_out, silu_out, ACT.Silu).then_inc(sem("gate_active"), 1)
                        if split is not None:
                            split_slab(split, i, 6)

                def up(pair, odd, before=None):
                    act.wait_ge(up_taken, pair + (n * FP + 2))
                    if before is not None:
                        act.wait_ge(multiplied, before)
                    run(flat(HH[:, odd]), hidden).then_inc(sem("hidden_hi"), 1)

                split_slab(g0 + 2)
                split_slab(g0 + 3)
                norm_root()
                gate(0)
                up(0, 0)
                with act.Fori(0, FP // 2) as i:
                    split_slab(g0 + 4, i, 6)
                    gate(i * 2 + 1, i, g0 + 5)
                    up(i * 2 + 1, 1, i * 6 + (g0 + 2))
                    split_slab(g0 + 6, i, 6)
                    split_slab(g0 + 7, i, 6)
                    gate(i * 2 + 2, i, g0 + 8)
                    up(i * 2 + 2, 0, i * 6 + (g0 + 5))
                    split_slab(g0 + 9, i, 6)
                ffns[0] += 1

            def down_chunks(name, gain=None, x0=0):
                if gain is not None:
                    chunks(name, gain, x0)
                split_slab(START[name] + 34)

            def inverse_root(out, in_, eps, scale, done):
                step(run(out, in_, ACT.Ln, bias=eps_col(eps), scale=scale))
                run(out, out, ACT.Exp, scale=-0.5).then_inc(sem(done), 1)

            def elsewhere(name, n, ahead=2):
                for j in range(n):
                    split_slab(START[name] + j + ahead)

            def taken_in(name, j, ahead=3):
                if ahead:
                    split_slab(START[name] + j + ahead)
                taken[0] += 1
                act.wait_ge(sem("output_taken"), taken[0])

            x_in = ins["x_t"].rearrange("(k p) t -> p k t", p=P)
            act.dma_start(prm[:], ins["params"]).then_inc(sem("params_landed"), 16)
            for c in range(4):
                act.dma_start(H[:, 2 * c:2 * c + 2, :], x_in[:, 2 * c:2 * c + 2, :]).then_inc(sem(f"x_landed{c}"), 16)
            act.wait_ge(sem("small_ready"), 1)
            act.wait_ge(sem("params_landed"), 16)
            for c in range(4):
                act.wait_ge(sem(f"x_landed{c}"), 16)
                operand_tiles((2 * c, 2 * c + 1), H, ("norm_mix", 0), 0)
                if c == 0:
                    split_slab(0)
            run(flat(squares), flat(H[:]), ACT.Square).then_inc(sem("norm_squared"), 1)
            split_slab(1)

            split_slab(START["conv"] + 2)
            for j in range(6):
                split_slab(START["conv"] + j + 3)
                if j == 0:
                    norm_root(True)
            elsewhere("sb_qk", 4, 3)
            elsewhere("sb_v", 2, 3)
            taken[0] += 12
            act.wait_ge(sem("conv_y"), 1)
            operand(flat(XH[:, 8:12]), flat(conv_y))
            for q in range(2):
                act.wait_ge(sem("sb_z"), q + 1)
                z, w = sb_z[q], sb_w[q]
                run(z, bank(0, 3), scale=HD ** -0.5).then_inc(sem("sb_z_taken"), 1)
                act.wait_ge(sem("sb_z_taken"), q + 1)
                step(run(w, z, ACT.Abs))
                step(run(w, w, ACT.Exp, scale=-1.0))
                run(w, w, ACT.Ln, bias=eps_col(1.0)).then_inc(sem("sb_softplus"), 1)
            for q in range(2):
                act.wait_ge(sem("sb_logw"), q + 1)
                run(sb_w[q], sb_w[q], ACT.Exp).then_inc(sem("sb_exp"), 1)
            act.wait_ge(sem("sb_y"), 1)
            operand(flat(XH[:, 12:16]), bank(6, 2))

            for j in range(7):
                taken_in("rwkv", j)
                for m in range(2):
                    t = 2 * j + m
                    last = run(rp[:, t, :], shift_in[j % 2][:, m, :], scale=one_minus_mu[:, t:t + 1])
                last.then_inc(sem("rk_scaled"), 1)
            act.wait_ge(sem("rk_shifted"), 7)
            run(LORA[0:HD, 0, :], LORA[0:HD, 0, :], ACT.Tanh)
            run(LORA[:, 1, :], LORA[:, 1, :], ACT.Sigmoid).then_inc(sem("rk_lora_in"), 1)
            act.wait_ge(sem("rk_lora_out"), 1)
            for f in range(4):
                run(LW[:, f, :], tiles_of(0, 4)[:, f, :], ACT.Sigmoid, bias=col("w0", f))
                run(A_[:, f, :], tiles_of(2, 4)[:, f, :], ACT.Sigmoid, bias=col("a0", f))
            run(flat(G_), bank(4, 2)).then_inc(sem("rk_gates"), 1)
            act.wait_ge(sem("rk_guarded"), 1)
            inverse_root(flat(TM), flat(TM), 0.0, 1.0, "rk_kk_root")
            act.wait_ge(sem("rk_decays"), 1)
            run(flat(EP), flat(LC), ACT.Exp)
            run(flat(LW), flat(LW), ACT.Exp)
            step(run(flat(LC), flat(LC), ACT.Exp, scale=-1.0))
            run(chunk_decay, EP[:, :, CH - 1:T:CH]).then_inc(sem("rk_exps"), 1)
            for tt in range(2):
                act.wait_ge(sem("rk_turned"), tt + 1)
                if tt == 0:
                    act.wait_ge(sem("rk_prep"), 1)
                run(Vt[:, 0, :], bank(0))
                run(ZP[:, :, 0:HD], bank(1).rearrange("p (h k) -> p h k", k=HD)).then_inc(sem("rk_turned_act"), 1)
                act.wait_ge(sem("rk_p"), tt + 1)
                run(ZP[:, :, HD:P], bank(0).rearrange("p (h k) -> p h k", k=HD)).then_inc(sem("rk_p_taken"), 1)
                for n in range(12 * tt, 12 * (tt + 1)):
                    act.wait_ge(sem("rk_f"), n + 1)
                    q = n % 2
                    run(flat(Fm[:, 4 * q:4 * q + 4]), bank(1 + q)).then_inc(sem("rk_f_taken"), 1)
                act.wait_ge(sem("rk_wu"), tt + 1)
                for q in range(2):
                    last = run(flat(Xb[:, 4 * q:4 * q + 4]), bank(3 + q))
                last.then_inc(sem("rk_wu_taken"), 1)
                act.wait_ge(sem("rk_inner"), tt + 1)
                run(KK[:, :, tt * P:(tt + 1) * P], bank(3).rearrange("p (f t) -> p f t", f=4))\
                    .then_inc(sem("rk_inner_copied"), 1)
                act.wait_ge(sem("rk_transition"), tt + 1)
                run(flat(MT), bank(0)[:, 0:4 * HD]).then_inc(sem("rk_transition_taken"), 1)
            act.wait_ge(sem("rk_var"), 1)
            inverse_root(flat(TM), bank(2, 2), GN_EPS, 1.0 / HD, "rk_root")
            act.wait_ge(sem("rk_y_out"), 1)
            operand(flat(XH[:, 16:20]), flat(KK))

            with act.Fori(0, 4) as i:
                for j in range(3):
                    split_slab(START["gates"] + j + 3, i)
                    act.wait_ge(sem("output_taken"), i * 3 + (taken[0] + j + 1))
                    for m in range(2):
                        t = i * 6 + (2 * j + m)
                        g_ = gates[:, bass.ds(t, 1), :].squeeze(1)
                        last = run(g_, g_, ACT.Sigmoid, bias=prm[:, bass.ds(t + COL["gate_b"], 1)])
                    last.then_inc(sem("gates_active"), 1)
            taken[0] += 12
            act.wait_ge(sem("mem_landed"), 16)
            run(flat(squares), flat(mem), ACT.Square).then_inc(sem("norm_squared"), 1)
            split_slab(START["branch"] + 3)
            split_slab(START["branch"] + 4)
            norm_root()
            for j in range(3, 6):
                split_slab(START["branch"] + j + 2)
            for half in range(2):
                act.wait_ge(sem("branch_taken"), 5 + half)
                operand(flat(XH[:, 4 * half:4 * half + 4]), flat(merged[:, 4 * half:4 * half + 4]))
            act.wait_ge(sem("mem_scaled"), 1)
            operand_tiles(range(KT), squares, ("norm_mem", 0), 8)
            elsewhere("mix_out", 4)

            act.wait_ge(sem("operand_lo"), splits[0])
            act.wait_ge(multiplied, START["mix_out"] + 4)
            chunks("mix_out", ("norm_ca", 0))
            elsewhere("ca_k", 4)
            elsewhere("ca_v", 4)
            taken[0] += 8
            norm_root()
            elsewhere("ca_q", 4)
            taken[0] += 4
            for tt in range(2):
                act.wait_ge(sem("ca_max"), tt + 1)
                for i in range(4 * tt, 4 * tt + 4):
                    last = run(probs[:, i, :], tiles_of(0, 8)[:, i, :], ACT.Exp, scale=1.0 / 16,
                               bias=small[:, 8 + i:9 + i], accum_out=small[:, 16 + i:17 + i])
                last.then_inc(sem("ca_exp"), 1)
            act.wait_ge(sem("ca_turned"), 1)
            run(flat(probs_t), bank(4, 4)).then_inc(sem("ca_turned_taken"), 1)
            for h in range(4):
                act.wait_ge(sem("ca_out"), h + 1)
                operand(flat(XH[:, 8 + 2 * h:10 + 2 * h]), bank(h))
            elsewhere("ca_o", 4)

            chunks("ca_o", ("norm_ffn", 0))
            feed_forward("ffn_c", conv=True)
            for c in range(4):
                act.wait_ge(sem("residual_ready"), chunks_until("ffn_c", c + 1))
            run(flat(squares), flat(H[:]), ACT.Square).then_inc(sem("norm_squared"), 1)
            split_slab(START["ffn_c"] + 34)
            norm_root()
            chunks("final", ("norm_gains", 0))
            feed_forward("ffn_0")
            down_chunks("ffn_0", ("norm_gains", 8))

            funcs = [ACT.Gelu_apprx_tanh, ACT.Copy, ACT.Sigmoid, ACT.Silu]
            split_slab(START["even_in"] + 2)
            split_slab(START["even_in"] + 3)
            norm_root(True)
            for j in range(8):
                taken_in("even_in", j, 3 if j else None)
                e = flat(ev[:, 2 * j:2 * j + 2])
                if funcs[j // 2] != ACT.Copy:
                    last = run(e, e, funcs[j // 2])
            for j in range(4):
                taken_in("even_v", j, 3)
                dst = [AV, BI][j // 2][:, :, j % 2 * T:(j % 2 + 1) * T]
                if j < 2:
                    last = run(dst, dst, ACT.Gelu_apprx_tanh)
            last.then_inc(sem("even_active"), 1)
            act.wait_ge(sem("av_sums"), 1)
            run(small[:, 16:32], small[:, 0:16], ACT.Sqrt, bias=eps_col(EPS), scale=1.0 / HD).then_inc(sem("av_root"), 1)
            act.wait_ge(sem("av_sums"), 2)
            run(small[:, 44:48], small[:, 40:44], ACT.Exp).then_inc(sem("av_root"), 1)
            act.wait_ge(sem("gl_forget"), 1)
            run(flat(BF), flat(BF), ACT.Ln, bias=eps_col(0.0)).then_inc(sem("gl_log"), 1)
            act.wait_ge(sem("mixed_gated"), 1)
            operand(flat(XH[:, 8:12]), flat(AU))
            for li in range(1, 9):
                act.wait_ge(sem("gl_diff"), li)
                d = flat(DIF[li % 2])
                step(run(d, d, ACT.Abs))
                run(d, d, ACT.Exp, scale=-1.0).then_inc(sem("gl_exp"), 1)
            act.wait_ge(sem("gl_out"), 1)
            run(flat(BC), bank(6, 2)).then_inc(sem("gl_copied"), 1)
            act.wait_ge(sem("gl_copied"), 1)
            run(flat(KB), flat(BC), ACT.Square).then_inc(sem("gl_squares"), 1)
            act.wait_ge(sem("gl_norms"), 1)
            inverse_root(flat(DIF[0]), bank(2, 2), EPS, 1.0 / P, "gl_root")
            act.wait_ge(sem("gl_y"), 1)
            operand(flat(XH[:, 12:16]), flat(BC))
            for j in range(1, 4):
                split_slab(START["even_out"] + j + 2)

            def per_layer(name, n):
                g0 = START[name]
                split_slab(g0 + 2)
                act.wait_ge(multiplied, g0 + 1)
                run(flat(ple_p[:, 0:6]), bank(0, 3))
                run(flat(ple_p[:, 6:8]), bank(7)).then_inc(sem("ple_copied"), 1)
                split_slab(g0 + 3)
                norm_root()
                for c in range(4):
                    act.wait_ge(sem("ple_gate_scaled"), 4 * n + c + 1)
                    s_ = slice(2 * c, 2 * c + 2)
                    run(flat(ple_g[:, s_]), flat(ple_g[:, s_]), ACT.Sigmoid).then_inc(sem("ple_gated"), 1)
                    if c < 3:
                        split_slab(g0 + 4 + c)
                    act.wait_ge(sem("ple_product"), 4 * n + c + 1)
                    run(flat(squares[:, s_]), flat(ple_p[:, s_]), ACT.Square).then_inc(sem("ple_squared"), 1)
                act.wait_ge(sem("ple_summed"), n + 1)
                run(root[:, 0:T], bank(0)[:, 0:T], ACT.Sqrt, bias=eps_col(EPS), scale=1.0 / D)\
                    .then_inc(sem("ple_root"), 1)
                for k in range(KT):
                    last = run(ple_add[:, k, :], ple_p[:, k, :], scale=col("norm_gains", (5 * n + 4) * 8 + k))
                    if k % 2:
                        last.then_inc(sem("ple_gained"), 1)

            def embedding(n):
                act.wait_ge(sem("ple_landed"), 16 * (n + 1))
                operand(flat(XH[:, 8:10]), flat(ple_in))

            chunks("even_out", ("norm_gains", 16))
            embedding(0)
            feed_forward("ffn_1")
            down_chunks("ffn_1", ("norm_gains", 24))
            per_layer("ple_0", 0)
            chunks("ple_0", ("norm_gains", 40))
            feed_forward("ffn_2")
            down_chunks("ffn_2", ("norm_gains", 48))

            act.wait_ge(sem("angles"), 1)
            run(flat(sines), flat(sines), ACT.Sin, bias=eps_col(0.0))
            run(flat(cosines), flat(cosines), ACT.Sin, bias=eps_col(0.0)).then_inc(sem("angles_done"), 1)
            split_slab(START["mla_in"] + 2)
            split_slab(START["mla_in"] + 3)
            norm_root()
            taken_in("mla_in", 0, None)
            operand_tiles((0, 1), MI, ("q_a_norm", 0), 8)
            taken_in("mla_in", 1, 3)
            operand_tiles((2,), MI, ("q_a_norm", 0), 8)
            taken_in("mla_in", 2, 3)
            operand_tiles((0, 1), MI[:, 3:5], ("kv_a_norm", 0), 11)
            run(flat(squares[:, 0:5]), flat(MI[:, 0:5]), ACT.Square).then_inc(sem("latent_squared"), 1)
            act.wait_ge(sem("latent_summed"), 1)
            run(latent_rs[:, 0, :], bank(7)[:, 0:T], ACT.Sqrt, bias=eps_col(EPS), scale=1.0 / 384)
            run(latent_rs[:, 1, :], bank(7)[:, T:2 * T], ACT.Sqrt, bias=eps_col(EPS), scale=1.0 / 256)
            run(small[:, 36:38], bank(6)[:, 0:2], ACT.Sqrt, bias=eps_col(EPS), scale=1.0 / 256)\
                .then_inc(sem("latent_roots"), 1)
            split_slab(START["mla_q"] + 3)
            for j in range(3):
                act.wait_ge(sem("mla_taken"), j + 1)
                last = run(flat(msq[:, 4 * j:4 * j + 4]), flat(MQ[:, 4 * j:4 * j + 4]), ACT.Square)
                if j == 0:
                    split_slab(START["mla_q"] + 4)
            last.then_inc(sem("mla_squares"), 1)
            split_slab(START["mla_kv"] + 2)
            act.wait_ge(sem("mla_sums"), 1)
            run(head_rs[:, 0:T], bank(7)[0:8, 0:T], ACT.Sqrt, bias=small[0:8, 32:33], scale=1.0 / 192)\
                .then_inc(sem("head_roots"), 1)
            act.wait_ge(sem("mla_taken"), 4)
            run(flat(msq[:, 0:8]), flat(MK), ACT.Square)
            run(msq[:, 8, :], MI[:, 5, :], ACT.Square).then_inc(sem("mla_squares"), 1)
            act.wait_ge(multiplied, START["mla_kv"] + 2)
            for n, b in enumerate((4, 5, 6, 0)):
                tt, half = divmod(n, 2)
                last = run(MV[:, tt, half * 512:(half + 1) * 512], bank(b), scale=small[:, 38 + tt:39 + tt])
            last.then_inc(sem("mla_taken"), 1)
            act.wait_ge(sem("mla_sums"), 2)
            run(head_rs[:, T:2 * T], bank(7)[0:8, T:2 * T], ACT.Sqrt, bias=small[0:8, 32:33], scale=1.0 / 192)\
                .then_inc(sem("head_roots"), 1)
            split_slab(START["mla_kv"] + 3)
            for e in range(2):
                act.wait_ge(sem("mla_max"), e + 1)
                for h in range(4 * e, 4 * e + 4):
                    run(S0[:, h, :], S0[:, h, :], ACT.Exp, scale=192 ** -0.5, bias=small[:, h:h + 1],
                        accum_out=small[:, 16 + h:17 + h])
                    last = run(S1[:, h, :], S1[:, h, :], ACT.Exp, scale=192 ** -0.5, bias=small[:, 8 + h:9 + h],
                               accum_out=small[:, 24 + h:25 + h])
                last.then_inc(sem("mla_exp"), 1)
            for e in range(2):
                act.wait_ge(sem("mla_turned"), e + 1)
                run(flat(PT0[:, 4 * e:4 * e + 4]), bank(2 * e, 2))
                run(flat(PT1[:, 4 * e:4 * e + 4]), bank(4 + e)).then_inc(sem("mla_turned_taken"), 1)
            for f in range(4):
                act.wait_ge(sem("mla_out"), f + 1)
                operand(flat(XH[:, 8 + 2 * f:10 + 2 * f]), bank(f))
            elsewhere("mla_out", 4)

            chunks("mla_out", ("norm_gains", 56))
            embedding(1)
            feed_forward("ffn_3")
            down_chunks("ffn_3", ("norm_gains", 64))
            per_layer("ple_1", 1)

        @block.vector
        def _(dve):
            v = nc.vector
            taken = [0]
            splits = [0]
            steps = [0]

            def step(ins_):
                steps[0] += 1
                ins_.then_inc(sem("dve_step"), 1)
                dve.wait_ge(sem("dve_step"), steps[0])

            def tt_(out, a, b, op):
                return v.tensor_tensor(out, a, b, op)

            def mul(out, a, b):
                return v.tensor_tensor(out, a, b, ALU.mult)

            def over(ap, n):
                return ap.unsqueeze(1).to_broadcast([P, n, ap.shape[-1]])

            def split_slab(g0, i=0, by=3):
                if g0 >= N_SLABS:
                    return
                slot, _, g = place(g0, i, by)
                dve.wait_ge(hi_split, g + 1)
                tt_(ring_lo[:, slot, :], ring_raw[:, slot, :], ring_hi[:, slot, :].bitcast(F32), ALU.subtract)\
                    .then_inc(lo_split, 1)

            def take(name, j, out, scaled=True):
                dve.wait_ge(multiplied, START[name] + j + 1)
                b = taken[0] % 3
                taken[0] += 1
                last_ = mul(out, tiles_of(b, 2), over(inv[:, 0:T], 2)) if scaled else v.tensor_copy(out, tiles_of(b, 2))
                last_.then_inc(sem("output_taken"), 1)

            def take_by_token(name, j, out):
                dve.wait_ge(multiplied, START[name] + j + 1)
                b = taken[0] % 3
                taken[0] += 1
                for tt in range(2):
                    last_ = v.tensor_scalar(out[:, tt, :], tiles_of(b, 2)[:, tt, :], inv[:, T + tt:T + tt + 1], None,
                                            ALU.mult)
                last_.then_inc(sem("output_taken"), 1)

            def operand(out, in_, hi):
                splits[0] += 1
                dve.wait_ge(sem("operand_hi"), splits[0])
                return tt_(out, in_, hi.bitcast(F32), ALU.subtract).then_inc(sem("operand_lo"), 1)

            norms = [0]

            def norm_factor(by_token=False):
                norms[0] += 1
                w = T + 2 if by_token else T
                dve.wait_ge(sem("norm_root"), norms[0])
                step(v.reciprocal(inv[:, 0:w], root[:, 0:w]))

            def operand_tiles(tiles, src, gain, x0):
                for k in tiles:
                    splits[0] += 1
                    dve.wait_ge(sem("operand_hi"), splits[0])
                    v.scalar_tensor_tensor(out=XL[:, x0 + k, :], in0=src[:, k, :], scalar=col(gain[0], gain[1] + k),
                                           in1=XH[:, x0 + k, :].bitcast(F32), op0=ALU.mult, op1=ALU.subtract)\
                     .then_inc(sem("operand_lo"), 1)

            def chunk(c):
                return flat(H[:, 2 * c:2 * c + 2])

            def chunks(add, stage, gain, behind=1):
                for c in range(4):
                    add(c)
                    if c >= behind:
                        lower(c - behind, stage, gain)
                for c in range(4 - behind, 4):
                    lower(c, stage, gain)

            def lower(c, stage, gain):
                if gain is not None:
                    dve.wait_ge(sem("residual_ready"), chunks_until(stage, c + 1))
                    operand_tiles((2 * c, 2 * c + 1), H, gain, 0)

            def residual(name, gain, behind=1, ahead=2):
                def add(c):
                    if ahead == 2 or c:
                        split_slab(START[name] + c + 2)
                    dve.wait_ge(multiplied, START[name] + c + 1)
                    tt_(chunk(c), chunk(c), bank((6, 7, 4, 5)[c]), ALU.add).then_inc(sem("residual_ready"), 1)
                chunks(add, name, gain, behind)

            def down(name, gain, scale=0.5):
                def add(c):
                    if c < 3:
                        dve.wait_ge(sem("down_bank"), 3 * (ffns[0] - 1) + c + 1)
                    else:
                        dve.wait_ge(multiplied, START[name] + 33)
                    v.scalar_tensor_tensor(out=chunk(c), in0=bank(3 + c), scalar=scale, in1=chunk(c), op0=ALU.mult,
                                           op1=ALU.add).then_inc(sem("residual_ready"), 1)
                chunks(add, name, gain)
                split_slab(START[name] + 34)

            ffns = [0]

            def feed_forward(name, conv=False):
                g0, n = START[name], ffns[0]
                gate_scaled, gate_active, up_taken = sem("gate_scaled"), sem("gate_active"), sem("up_taken")

                def factor():
                    return over(inv[:, 0:T], 2)

                def tiled(x):
                    return x.rearrange("p (n t) -> p n t", t=T)

                def gate(at, i, pair, b, split=None):
                    dve.wait_ge(multiplied, place(at, i, 6)[2] + 1)
                    dve.wait_ge(up_taken, pair + (n * FP + 1))
                    if conv:
                        mul(conv_x[0], tiles_of(b, 2), factor()).then_inc(gate_scaled, 1)
                    else:
                        mul(tiled(silu_out), tiles_of(b, 2), factor()).then_inc(gate_scaled, 1)
                    if split is not None:
                        split_slab(split, i, 6)
                    if conv:
                        dve.wait_ge(gate_scaled, pair + 2)
                        taps(conv_acc, conv_x[0], pair * 2, pair * 11, sem("conv_done"))
                    else:
                        dve.wait_ge(gate_active, pair + (n * FP + 1))
                        mul(tiled(silu_out), tiled(silu_out), factor()).then_inc(sem("gate_rescaled"), 1)

                def taps(acc, x, tile_, before, done):
                    for m in range(2):
                        w2 = prm[:, bass.ds(tile_ + (m + COL["ffn_conv_w"] + 2 * 4 * FP), 1)]
                        b = prm[:, bass.ds(tile_ + (m + COL["ffn_conv_b"]), 1)]
                        v.tensor_scalar(acc[:, m, :], x[:, m, :], w2, b, ALU.mult, ALU.add)\
                         .then_inc(sem("conv_tap"), 1)
                    dve.wait_ge(sem("conv_tap"), before + 2)
                    for m in range(2):
                        w1 = prm[:, bass.ds(tile_ + (m + COL["ffn_conv_w"] + 4 * FP), 1)]
                        v.scalar_tensor_tensor(out=acc[:, m, 1:T], in0=x[:, m, 0:T - 1], scalar=w1,
                                               in1=acc[:, m, 1:T], op0=ALU.mult, op1=ALU.add)\
                         .then_inc(sem("conv_tap"), 1)
                    dve.wait_ge(sem("conv_tap"), before + 4)
                    for m in range(2):
                        w0 = prm[:, bass.ds(tile_ + (m + COL["ffn_conv_w"]), 1)]
                        v.scalar_tensor_tensor(out=acc[:, m, 2:T], in0=x[:, m, 0:T - 2], scalar=w0,
                                               in1=acc[:, m, 2:T], op0=ALU.mult, op1=ALU.add)\
                         .then_inc(done if m == 1 else sem("conv_tap"), 1)

                def up(at, i, pair, odd, b):
                    dve.wait_ge(multiplied, place(at, i, 6)[2] + 1)
                    dve.wait_ge(sem("hidden_lo"), pair + n * FP)
                    if conv:
                        mul(conv_x[1], tiles_of(b, 2), factor()).then_inc(sem("conv_up_scaled"), 1)
                        dve.wait_ge(sem("conv_up_scaled"), pair + 1)
                        taps(conv_acc2, conv_x[1], pair * 2 + 2 * FP, pair * 11 + 5, sem("conv_tap"))
                        dve.wait_ge(sem("conv_tap"), pair * 11 + 11)
                        dve.wait_ge(gate_active, pair + 1)
                        mul(hidden, silu_out, flat(conv_acc2)).then_inc(up_taken, 1)
                    else:
                        dve.wait_ge(sem("gate_rescaled"), pair + ((n - 1) * FP + 1))
                        mul(hidden, silu_out, bank(b)).then_inc(up_taken, 1)
                    dve.wait_ge(sem("hidden_hi"), pair + (n * FP + 1))
                    tt_(flat(HL[:, odd]), hidden, flat(HH[:, odd]).bitcast(F32), ALU.subtract)\
                        .then_inc(sem("hidden_lo"), 1)

                split_slab(g0 + 2)
                split_slab(g0 + 3)
                norm_factor()
                gate(g0, 0, 0, 0)
                up(g0 + 1, 0, 0, 0, 1)
                with dve.Fori(0, FP // 2) as i:
                    split_slab(g0 + 4, i, 6)
                    gate(g0 + 2, i, i * 2 + 1, 2, g0 + 5)
                    up(g0 + 3, i, i * 2 + 1, 1, 7)
                    split_slab(g0 + 6, i, 6)
                    split_slab(g0 + 7, i, 6)
                    gate(g0 + 5, i, i * 2 + 2, 0, g0 + 8)
                    up(g0 + 6, i, i * 2 + 2, 0, 1)
                    split_slab(g0 + 9, i, 6)
                ffns[0] += 1

            for value, c in ((EPS, 32), (GN_EPS, 33), (1.0, 34), (0.0, 35)):
                last = v.memset(small[:, c:c + 1], value)
            last.then_inc(sem("small_ready"), 1)
            for c, free in ((59, "gate_scaled"), (58, "up_taken")):
                v.memset(small[:, c:c + 1], 0.0).then_inc(sem(free), 1)
            dve.wait_ge(sem("params_landed"), 16)
            step(v.tensor_scalar(one_minus_mu[:], col("mu", 0, 14), -1.0, 1.0, ALU.mult, ALU.add))
            for c in range(4):
                operand_tiles((2 * c, 2 * c + 1), H, ("norm_mix", 0), 0)
                if c == 0:
                    split_slab(0)
            split_slab(1)

            split_slab(START["conv"] + 2)
            split_slab(START["conv"] + 3)
            norm_factor(True)
            for j in range(6):
                take("conv", j, conv_in[:, 2 * j:2 * j + 2])
                if j:
                    split_slab(START["conv"] + j + 3)
            for j in range(4):
                take("sb_qk", j, sbq[:, 2 * j:2 * j + 2])
                split_slab(START["sb_qk"] + j + 3)
            for j in range(2):
                take_by_token("sb_v", j, sbv[:, :, j * T:(j + 1) * T])
                split_slab(START["sb_v"] + j + 3)
            dve.wait_ge(sem("output_taken"), 6)
            step(mul(conv_u, conv_in[:, 4:8], conv_in[:, 8:12]))
            for f in range(4):
                last = v.tensor_scalar(conv_y[:, f, :], conv_u[:, f, :], col("conv_w", 8 + f), None, ALU.mult)
            step(last)
            for back in (1, 2):
                for f in range(4):
                    last = v.scalar_tensor_tensor(out=conv_y[:, f, back:T], in0=conv_u[:, f, 0:T - back],
                                                  scalar=col("conv_w", 4 * (2 - back) + f), in1=conv_y[:, f, back:T],
                                                  op0=ALU.mult, op1=ALU.add)
                step(last)
            mul(conv_y, conv_y, conv_in[:, 0:4]).then_inc(sem("conv_y"), 1)
            dve.wait_ge(sem("conv_y"), 1)
            operand(flat(XL[:, 8:12]), flat(conv_y), flat(XH[:, 8:12]))

            def masked(q, buf):
                for b in (0, 2):
                    blk = buf[:, b * 512:(b + 1) * 512].rearrange("p (f t) -> p f t", f=4)
                    last_ = mul(blk, blk, per_head("before"))
                return last_

            for q in range(2):
                dve.wait_ge(sem("sb_softplus"), q + 1)
                z, w = sb_z[q], sb_w[q]
                step(v.scalar_tensor_tensor(out=w, in0=z, scalar=0.0, in1=w, op0=ALU.min, op1=ALU.subtract))
                step(tt_(z, w, z, ALU.subtract))
                masked(q, z).then_inc(sem("sb_log"), 1)
            for q in range(2):
                dve.wait_ge(sem("sb_suffix"), q + 1)
                tt_(sb_w[q], sb_w[q], bank(3, 3), ALU.add).then_inc(sem("sb_logw"), 1)
                dve.wait_ge(sem("sb_exp"), q + 1)
                masked(q, sb_w[q]).then_inc(sem("sb_att"), 1)
            dve.wait_ge(sem("sb_y"), 1)
            operand(flat(XL[:, 12:16]), bank(6, 2), flat(XH[:, 12:16]))

            def shift(j):
                dve.wait_ge(sem("rk_scaled"), j + 1)
                for m in range(2):
                    t = 2 * j + m
                    last_ = v.scalar_tensor_tensor(out=rp[:, t, 1:T], in0=shift_in[j % 2][:, m, 0:T - 1],
                                                   scalar=col("mu", t), in1=rp[:, t, 1:T], op0=ALU.mult, op1=ALU.add)
                last_.then_inc(sem("rk_shifted"), 1)

            for j in range(7):
                if j == 0:
                    dve.wait_ge(sem("operand_lo"), KT + 2)
                if j >= 2:
                    dve.wait_ge(sem("rk_shifted"), j - 1)
                take("rwkv", j, shift_in[j % 2])
                split_slab(START["rwkv"] + j + 3)
                if j:
                    shift(j - 1)
            shift(6)
            dve.wait_ge(sem("rk_shifted"), 7)
            for f in range(4):
                last = v.tensor_scalar(KK[:, f, :], K_[:, f, :], col("k_k", f), None, ALU.mult)
            step(last)
            mul(TM, KK, KK).then_inc(sem("rk_squares"), 1)
            dve.wait_ge(sem("rk_norms"), 1)
            v.tensor_scalar(flat(TM), bank(6, 2), 1e-24, None, ALU.max).then_inc(sem("rk_guarded"), 1)
            dve.wait_ge(sem("rk_gates"), 1)
            step(v.tensor_scalar(flat(LW), flat(LW), -DECAY_SCALE, None, ALU.mult))
            for f in range(4):
                for c in range(4):
                    t = slice(c * CH, (c + 1) * CH)
                    last = v.tensor_tensor_scan(LC[:, f, t], table("ones")[:, 0:CH], LW[:, f, t], 0.0, ALU.mult, ALU.add)
            step(last)
            tt_(flat(LW), flat(LC), flat(LW), ALU.subtract).then_inc(sem("rk_decays"), 1)
            dve.wait_ge(sem("rk_kk_root"), 1)
            step(mul(KK, KK, TM))
            for f in range(4):
                last = v.tensor_scalar(TM[:, f, :], A_[:, f, :], -1.0, col("k_a", f), ALU.add, ALU.mult)
            step(last)
            step(v.scalar_tensor_tensor(out=flat(K_), in0=flat(TM), scalar=1.0, in1=flat(K_), op0=ALU.add, op1=ALU.mult))
            step(v.scalar_tensor_tensor(out=flat(A_), in0=flat(KK), scalar=-1.0, in1=flat(A_), op0=ALU.mult,
                                        op1=ALU.mult))
            for f in range(4):
                last = v.scalar_tensor_tensor(out=BN[:, f, :], in0=R_[:, f, :], scalar=col("r_k", f), in1=K_[:, f, :],
                                              op0=ALU.mult, op1=ALU.mult)
            last.then_inc(sem("rk_bonus_in"), 1)
            dve.wait_ge(sem("rk_exps"), 1)
            dve.wait_ge(sem("rk_bonus_in"), 1)
            mul(R_, R_, EP)
            mul(KK, KK, LW)
            mul(K_, K_, LC)
            step(mul(A_, A_, LC))
            dve.wait_ge(sem("rk_bonus_sums"), 1)
            mul(flat(BN), flat(V_), bank(6, 2)).then_inc(sem("rk_prep"), 1)
            for tt in range(2):
                tok = slice(tt * P, (tt + 1) * P)
                dve.wait_ge(sem("rk_turned"), tt + 1)
                v.tensor_copy(Kt[:, 0, :], bank(2))
                v.tensor_copy(Bt[:, 0, :], bank(3))
                dve.wait_ge(sem("rk_pairs"), tt + 1)
                for q in range(2):
                    e = slice(4 * q, 4 * q + 4)
                    mul(Fm[:, e, :], bank(4 + q).rearrange("p (f t) -> p f t", f=4), per_head("before_chunk"))
                    last = mul(Xm[:, e, :], bank(6 + q).rearrange("p (f t) -> p f t", f=4), per_head("before_chunk"))
                last.then_inc(sem("rk_masked"), 1)
                dve.wait_ge(sem("rk_masked"), tt + 1)
                for li in range(6):
                    for q in range(2):
                        n = (tt * 6 + li) * 2 + q
                        e = slice(4 * q, 4 * q + 4)
                        if li:
                            dve.wait_ge(sem("rk_f"), n - 1)
                        mul(Xb[:, e, :], Xm[:, e, :], per_head(f"level{LEVELS[li]}")).then_inc(sem("rk_x"), 1)
                    for q in range(2):
                        n = (tt * 6 + li) * 2 + q
                        e = slice(4 * q, 4 * q + 4)
                        dve.wait_ge(sem("rk_dy"), n + 1)
                        if li:
                            dve.wait_ge(sem("rk_y"), n - 1)
                        if li < 5:
                            y = Yt[:, e, :] if li else per_head("identity")
                            tt_(Yt[:, e, :], y, bank(5 + q).rearrange("p (f t) -> p f t", f=4), ALU.add)
                        y = Ym[:, e, :] if li else per_head("identity")
                        tt_(Ym[:, e, :], y, bank(3 + q).rearrange("p (f t) -> p f t", f=4), ALU.add)\
                            .then_inc(sem("rk_y"), 1)
                dve.wait_ge(sem("rk_out_pairs"), tt + 1)
                for q in range(2):
                    e = slice(4 * q, 4 * q + 4)
                    mul(Yt[:, e, :], bank(5 + q).rearrange("p (f t) -> p f t", f=4), per_head("upto_chunk"))
                    last = mul(Fm[:, e, :], bank(1 + q).rearrange("p (f t) -> p f t", f=4), per_head("upto_chunk"))
                last.then_inc(sem("rk_out_masked"), 1)
                dve.wait_ge(sem("rk_inner"), tt + 1)
                tt_(R_[:, :, tok], R_[:, :, tok], bank(7).rearrange("p (f t) -> p f t", f=4), ALU.add)\
                    .then_inc(sem("rk_inner_taken"), 1)
                dve.wait_ge(sem("rk_inner_copied"), tt + 1)
                for c in range(2):
                    gc = 2 * tt + c
                    if gc in (1, 3):
                        dve.wait_ge(sem("rk_carried"), 1 + tt)
                        t = slice(gc * CH, (gc + 1) * CH) if gc == 1 else tok
                        o = slice(CH, P) if gc == 1 else slice(0, P)
                        for q in range(2):
                            rows = slice(HD * q, HD * (q + 1))
                            part = bank(6 + q)[rows, :].rearrange("p (f t) -> p f t", f=4)[:, :, o]
                            last = tt_(KK[rows, :, t], KK[rows, :, t], part, ALU.add)
                        if gc == 3:
                            last.then_inc(sem("rk_out"), 1)
                            continue
                    dve.wait_ge(sem("rk_update"), gc + 1)
                    g_ = chunk_decay[:, :, gc:gc + 1].to_broadcast([P, 4, HD])
                    new = bank(5)[:, 0:4 * HD].rearrange("p (f v) -> p f v", f=4)
                    if gc:
                        step(tt_(state, state, new, ALU.add))
                        for q in range(2):
                            rows = slice(HD * q, HD * (q + 1))
                            old = bank(1 + q)[rows, 0:4 * HD].rearrange("p (f v) -> p f v", f=4)
                            last = tt_(state[rows], state[rows], old, ALU.add)
                        step(last)
                        if gc == 1:
                            step(mul(state, state, g_))
                            v.memset(small[:, 62:63], 0.0).then_inc(sem("rk_state"), 1)
                        else:
                            mul(state, state, g_).then_inc(sem("rk_state"), 1)
                    else:
                        mul(state, new, g_).then_inc(sem("rk_state"), 1)
                        dve.wait_ge(sem("rk_state"), 1)
                    if gc == 1:
                        v.memset(small[:, 61:62], 0.0).then_inc(sem("rk_tile_done"), 1)
            dve.wait_ge(sem("rk_mean"), 1)
            step(v.scalar_tensor_tensor(out=flat(KK), in0=bank(0, 2), scalar=-1.0 / HD, in1=flat(KK), op0=ALU.mult,
                                        op1=ALU.add))
            mul(TM, KK, KK).then_inc(sem("rk_centred"), 1)
            dve.wait_ge(sem("rk_root"), 1)
            step(mul(KK, KK, TM))
            for f in range(4):
                last = v.tensor_scalar(KK[:, f, :], KK[:, f, :], col("lnx_w", f), col("lnx_b", f), ALU.mult, ALU.add)
            step(last)
            step(tt_(KK, KK, BN, ALU.add))
            mul(KK, KK, G_).then_inc(sem("rk_y_out"), 1)
            dve.wait_ge(sem("rk_y_out"), 1)
            operand(flat(XL[:, 16:20]), flat(KK), flat(XH[:, 16:20]))

            dve.wait_ge(sem("operand_lo"), KT + 3)
            with dve.Fori(0, 4) as i:
                for j in range(3):
                    dve.wait_ge(multiplied, place(START["gates"] + j, i)[2] + 1)
                    mul(gates[:, bass.ds(i * 6 + 2 * j, 2), :], tiles_of((taken[0] + j) % 3, 2), over(inv[:, 0:T], 2))\
                        .then_inc(sem("output_taken"), 1)
                    split_slab(START["gates"] + j + 3, i)
            taken[0] += 12
            dve.wait_ge(sem("gates_active"), 12)
            for j in range(6):
                if j:
                    split_slab(START["branch"] + j + 2)
                if j == 4:
                    norm_factor()
                    mul(squares, mem, over(inv[:, 0:T], KT)).then_inc(sem("mem_scaled"), 1)
                if j == 5:
                    operand(flat(XL[:, 0:4]), flat(merged[:, 0:4]), flat(XH[:, 0:4]))
                dve.wait_ge(multiplied, START["branch"] + j + 1)
                n, half = divmod(j, 2)
                out = merged[:, 4 * half:4 * half + 4]
                g_ = gates[:, 8 * n + 4 * half:8 * n + 4 * half + 4]
                src = bank(2 * (j % 3), 2).rearrange("p (m t) -> p m t", t=T)
                if n == 0:
                    mul(out, src, g_).then_inc(sem("branch_taken"), 1)
                    dve.wait_ge(sem("branch_taken"), j + 1)
                else:
                    step(mul(gated, src, g_))
                    tt_(out, out, gated, ALU.add).then_inc(sem("branch_taken"), 1)
                    dve.wait_ge(sem("branch_taken"), j + 1)
            operand(flat(XL[:, 4:8]), flat(merged[:, 4:8]), flat(XH[:, 4:8]))
            dve.wait_ge(sem("mem_scaled"), 1)
            operand_tiles(range(KT), squares, ("norm_mem", 0), 8)
            residual("mix_out", ("norm_ca", 0), 4)

            for j in range(4):
                split_slab(START["ca_k"] + j + 2)
                take("ca_k", j, ca_k[:, 2 * j:2 * j + 2], False)
            for j in range(4):
                split_slab(START["ca_v"] + j + 2)
                take("ca_v", j, ca_v[:, :, j * T:(j + 1) * T], False)
            for j in range(4):
                split_slab(START["ca_q"] + j + 2)
                if j == 0:
                    norm_factor()
                take("ca_q", j, ca_q[:, 2 * j:2 * j + 2])
            for tt in range(2):
                i = slice(4 * tt, 4 * tt + 4)
                dve.wait_ge(sem("ca_scores"), tt + 1)
                step(v.tensor_reduce(small[:, i], tiles_of(0, 8)[:, i, :], AX.X, ALU.max))
                v.tensor_scalar(small[:, 8 + 4 * tt:12 + 4 * tt], small[:, i], -1.0 / 16, None, ALU.mult)\
                 .then_inc(sem("ca_max"), 1)
            for tt in range(2):
                dve.wait_ge(sem("ca_exp"), tt + 1)
                r = small[:, 24 + 4 * tt:28 + 4 * tt]
                step(v.reciprocal(r, small[:, 16 + 4 * tt:20 + 4 * tt]))
                p_ = probs[:, 4 * tt:4 * tt + 4]
                mul(p_, p_, r.unsqueeze(2).to_broadcast([P, 4, T])).then_inc(sem("ca_probs"), 1)
            for h in range(4):
                dve.wait_ge(sem("ca_out"), h + 1)
                operand(flat(XL[:, 8 + 2 * h:10 + 2 * h]), bank(h), flat(XH[:, 8 + 2 * h:10 + 2 * h]))
            residual("ca_o", ("norm_ffn", 0))

            feed_forward("ffn_c", conv=True)
            down("ffn_c", None, scale=1.0)
            norm_factor()
            def final(c):
                s_ = squares[:, 2 * c:2 * c + 2]
                step(mul(s_, H[:, 2 * c:2 * c + 2], over(inv[:, 0:T], 2)))
                for k in (2 * c, 2 * c + 1):
                    last_ = v.tensor_scalar(H[:, k, :], squares[:, k, :], col("norm_final", k), None, ALU.mult)
                last_.then_inc(sem("residual_ready"), 1)
            chunks(final, "final", ("norm_gains", 0))

            feed_forward("ffn_0")
            down("ffn_0", ("norm_gains", 8))

            split_slab(START["even_in"] + 2)
            split_slab(START["even_in"] + 3)
            norm_factor(True)
            for j in range(8):
                take("even_in", j, ev[:, 2 * j:2 * j + 2])
                if j:
                    split_slab(START["even_in"] + j + 3)
            for j in range(4):
                take_by_token("even_v", j, [AV, BI][j // 2][:, :, j % 2 * T:(j % 2 + 1) * T])
                split_slab(START["even_v"] + j + 3)
            dve.wait_ge(sem("even_active"), 1)
            avf = AV.rearrange("p a b -> p (a b)")
            sqv = flat(BC)
            step(mul(sqv, avf, avf))
            v.tensor_reduce(small[:, 0:16], sqv.rearrange("p (n d) -> p n d", d=HD), AX.X, ALU.add)\
             .then_inc(sem("av_sums"), 1)
            dve.wait_ge(sem("av_sums"), 1)
            tt_(small[:, 40:44], col("hgrn_lb", 0, 4), col("hgrn_lb", 0, 4), ALU.subtract).then_inc(sem("av_sums"), 1)
            dve.wait_ge(sem("spatial_landed"), 48)
            mul(spatial_w, spatial_w, per_head("upto", 8))
            dve.wait_ge(sem("av_root"), 1)
            step(v.reciprocal(small[:, 0:16], small[:, 16:32]))
            avh = avf.rearrange("p (n d) -> p n d", d=HD)
            step(mul(avh, avh, small[:, 0:16].unsqueeze(2).to_broadcast([P, 16, HD])))
            mul(AV, AV, v_gain[:, 0, :].unsqueeze(1).to_broadcast([P, 2, W])).then_inc(sem("spatial_ready"), 1)
            dve.wait_ge(sem("av_root"), 2)
            step(v.reciprocal(small[:, 48:52], small[:, 44:48]))
            step(mul(small[:, 52:56], small[:, 44:48], small[:, 48:52]))
            step(tt_(small[:, 40:44], small[:, 52:56], small[:, 52:56], ALU.subtract))
            step(v.tensor_scalar(small[:, 40:44], small[:, 40:44], 0.0, 0.999, ALU.max, ALU.min))
            step(v.tensor_scalar(small[:, 44:48], small[:, 40:44], -1.0, 1.0, ALU.mult, ALU.add))
            for h in range(4):
                last = v.tensor_scalar(BF[:, h, :], BF[:, h, :], small[:, 44 + h:45 + h], small[:, 40 + h:41 + h],
                                       ALU.mult, ALU.add)
            step(last)
            dve.wait_ge(sem("spatial_mixed"), 1)
            mul(flat(AU), flat(AU), bank(0, 2)).then_inc(sem("mixed_gated"), 1)
            step(v.tensor_scalar(flat(KB), flat(BF), -1.0, 1.0, ALU.mult, ALU.add))
            v.tensor_scalar(flat(BF), flat(BF), 1e-6, None, ALU.max).then_inc(sem("gl_forget"), 1)
            dve.wait_ge(sem("mixed_gated"), 1)
            operand(flat(XL[:, 8:12]), flat(AU), flat(XH[:, 8:12]))
            dve.wait_ge(sem("gl_log"), 1)
            for h in range(4):
                for tt in range(2):
                    t = slice(tt * P, (tt + 1) * P)
                    last = v.tensor_tensor_scan(BC[:, h, t], table("ones"), BF[:, h, t], 0.0, ALU.mult, ALU.add)
            last.then_inc(sem("gl_factors"), 1)
            dve.wait_ge(sem("gl_factors"), 1)

            def gl_mask(li):
                dve.wait_ge(sem("gl_pairs"), li + 1)
                if li == 8:
                    v.tensor_copy(AC, bank(2).rearrange("p (h t) -> p h t", h=4)).then_inc(sem("gl_added"), 1)
                    return
                name = f"level{LEVELS[li - 1]}" if li else "identity"
                for tt in range(2):
                    src = bank(2 + 2 * (li % 2) + tt).rearrange("p (h t) -> p h t", h=4)
                    a = AT[:, 4 * tt:4 * tt + 4, :]
                    if li == 0:
                        last_ = mul(a, src, per_head(name))
                    else:
                        step(mul(AM, src, per_head(name)))
                        last_ = tt_(a, a, AM, ALU.add)
                        if tt == 0:
                            step(last_)
                last_.then_inc(sem("gl_added"), 1)
                dve.wait_ge(sem("gl_added"), li + 1)

            def gl_diff(li):
                d = DIF[li % 2]
                if li < 8:
                    b = LEVELS[li - 1]
                    bc = flat(BC).rearrange("p (n c) -> p n c", c=2 * b)
                    ref = bc[:, :, b - 1:b].to_broadcast([P, 4 * T // (2 * b), 2 * b])
                    tt_(flat(d).rearrange("p (n c) -> p n c", c=2 * b), bc, ref, ALU.subtract)\
                        .then_inc(sem("gl_diff"), 1)
                else:
                    v.tensor_copy(d[:, :, P:T], BC[:, :, P:T])
                    tt_(d[:, :, 0:P], BC[:, :, 0:P], BC[:, :, P - 1:P].to_broadcast([P, 4, P]), ALU.subtract)\
                        .then_inc(sem("gl_diff"), 1)

            def gl_factor(li):
                b = LEVELS[li - 1] if li < 8 else P
                dve.wait_ge(sem("gl_exp"), li)
                if li >= 2:
                    dve.wait_ge(sem("gl_pairs"), li - 1)
                blocks = [flat(a).rearrange("p (n c) -> p n c", c=2 * b) for a in (XM[li % 2], DIF[li % 2], KB, BQ)]
                x, e, k, q = blocks
                mul(x[:, :, 0:b], e[:, :, 0:b], k[:, :, 0:b])
                mul(x[:, :, b:2 * b], e[:, :, b:2 * b], q[:, :, b:2 * b]).then_inc(sem("gl_factors"), 1)

            gl_diff(1)
            for li in range(1, 9):
                if li < 8:
                    if li > 1:
                        dve.wait_ge(sem("gl_factors"), li)
                    gl_diff(li + 1)
                gl_factor(li)
                gl_mask(li - 1)
            gl_mask(8)
            dve.wait_ge(sem("gl_root"), 1)
            step(v.scalar_tensor_tensor(out=flat(BC), in0=flat(BC), scalar=col("hgrn_out_norm"), in1=flat(DIF[0]),
                                        op0=ALU.mult, op1=ALU.mult))
            mul(BC, BC, BG).then_inc(sem("gl_y"), 1)
            dve.wait_ge(sem("gl_y"), 1)
            operand(flat(XL[:, 12:16]), flat(BC), flat(XH[:, 12:16]))
            residual("even_out", ("norm_gains", 16), ahead=3)

            def embedding(n):
                dve.wait_ge(sem("ple_landed"), 16 * (n + 1))
                operand(flat(XL[:, 8:10]), flat(ple_in), flat(XH[:, 8:10]))

            def per_layer(name, n, gain):
                g0 = START[name]
                split_slab(g0 + 2)
                split_slab(g0 + 3)
                norm_factor()
                dve.wait_ge(sem("ple_copied"), n + 1)
                for c in range(4):
                    s_ = slice(2 * c, 2 * c + 2)
                    dve.wait_ge(multiplied, g0 + 2 + c)
                    mul(ple_g[:, s_], tiles_of(3 + c, 2), over(inv[:, 0:T], 2)).then_inc(sem("ple_gate_scaled"), 1)
                    if c < 3:
                        split_slab(g0 + 4 + c)
                    dve.wait_ge(sem("ple_gated"), 4 * n + c + 1)
                    mul(ple_p[:, s_], ple_p[:, s_], ple_g[:, s_]).then_inc(sem("ple_product"), 1)
                dve.wait_ge(sem("ple_root"), n + 1)
                step(v.reciprocal(inv[:, 0:T], root[:, 0:T]))

                def add(c):
                    s_ = ple_add[:, 2 * c:2 * c + 2]
                    dve.wait_ge(sem("ple_gained"), 4 * n + c + 1)
                    step(mul(s_, s_, over(inv[:, 0:T], 2)))
                    tt_(chunk(c), chunk(c), flat(s_), ALU.add).then_inc(sem("residual_ready"), 1)
                chunks(add, name, gain)

            embedding(0)
            feed_forward("ffn_1")
            down("ffn_1", ("norm_gains", 24))
            per_layer("ple_0", 0, ("norm_gains", 40))
            feed_forward("ffn_2")
            down("ffn_2", ("norm_gains", 48))

            dve.wait_ge(sem("positions_landed"), 16)
            two_pi = 2 * np.pi
            magic = 1.5 * 2.0 ** 23
            c1 = 6.28125
            c2 = float(np.float32(two_pi - c1))
            c2 = float(np.round(c2 * 2 ** 20) / 2 ** 20)
            c3 = float(two_pi - c1 - c2)
            a_, n_ = flat(ang), flat(turns)
            step(v.tensor_copy(a_, cosines.bitcast(I32)[:, 0, :]))
            step(v.tensor_scalar(a_, a_, col("inv_freq"), None, ALU.mult))
            step(v.tensor_scalar(n_, a_, 1 / two_pi, None, ALU.mult))
            step(v.tensor_scalar(n_, n_, magic, None, ALU.add))
            step(v.tensor_scalar(n_, n_, -magic, None, ALU.add))
            for c in (c1, c2, c3):
                step(v.scalar_tensor_tensor(out=a_, in0=n_, scalar=-c, in1=a_, op0=ALU.mult, op1=ALU.add))
            limit = 3.1415925
            v.tensor_scalar(flat(sines), a_, limit, -limit, ALU.min, ALU.max)
            step(v.tensor_scalar(a_, a_, np.pi / 2, None, ALU.add))
            step(v.tensor_scalar(n_, a_, np.pi, -two_pi, ALU.is_gt, ALU.mult))
            step(tt_(a_, a_, n_, ALU.add))
            v.tensor_scalar(flat(cosines), a_, limit, -limit, ALU.min, ALU.max).then_inc(sem("angles"), 1)
            for pick in (pick_head, pick_pair):
                flat_pick = pick.rearrange("p h c -> p (h c)").rearrange("p (h c) -> p h c", h=8)
                last = v.tensor_copy(flat_pick, table("identity")[0:8, 0:8].unsqueeze(2)
                                     .to_broadcast([8, 8, flat_pick.shape[-1]]))
            split_slab(START["mla_in"] + 2)
            split_slab(START["mla_in"] + 3)
            norm_factor()
            take("mla_in", 0, MI[:, 0:2])
            dve.wait_ge(sem("output_taken"), taken[0])
            operand_tiles((0, 1), MI, ("q_a_norm", 0), 8)
            split_slab(START["mla_in"] + 4)
            take("mla_in", 1, MI[:, 2:4])
            dve.wait_ge(sem("output_taken"), taken[0])
            operand_tiles((2,), MI, ("q_a_norm", 0), 8)
            split_slab(START["mla_in"] + 5)
            take("mla_in", 2, MI[:, 4:6])
            dve.wait_ge(sem("output_taken"), taken[0])
            operand_tiles((0, 1), MI[:, 3:5], ("kv_a_norm", 0), 11)
            dve.wait_ge(sem("latent_roots"), 1)
            step(v.reciprocal(latent_rs[:, 0, :], latent_rs[:, 0, :]))

            def take_q(j):
                dve.wait_ge(multiplied, START["mla_q"] + j + 1)
                mul(MQ[:, 4 * j:4 * j + 4], tiles_of(2 * j, 4), over(latent_rs[:, 0, :], 4))\
                    .then_inc(sem("mla_taken"), 1)

            take_q(0)
            split_slab(START["mla_q"] + 3)
            take_q(1)
            step(v.reciprocal(latent_rs[:, 1, :], latent_rs[:, 1, :]))
            step(v.reciprocal(small[:, 38:40], small[:, 36:38]))
            split_slab(START["mla_q"] + 4)
            take_q(2)
            split_slab(START["mla_kv"] + 2)
            dve.wait_ge(multiplied, START["mla_kv"] + 1)
            mul(MK, tiles_of(0, 8), over(latent_rs[:, 1, :], 8)).then_inc(sem("mla_taken"), 1)
            qr, kr = MQ[:, 8:12], MI[:, 0:1]
            dve.wait_ge(sem("mla_squares"), 1)
            v.tensor_scalar(flat(qr), flat(qr), col("q_rope"), None, ALU.mult)
            v.tensor_scalar(flat(kr), flat(MI[:, 5:6]), col("k_rope"), None, ALU.mult).then_inc(sem("mla_rope_in"), 1)
            dve.wait_ge(sem("head_roots"), 1)
            v.reciprocal(head_rs[:, 0:T], head_rs[:, 0:T]).then_inc(sem("head_rs"), 1)
            dve.wait_ge(sem("angles_done"), 1)
            dve.wait_ge(sem("mla_swapped"), 2)
            rot = KRP[:, 0:5]
            mul(rot[:, 0:4], tiles_of(1, 4), over(sines[:, 0, :], 4))
            mul(rot[:, 4:5], tiles_of(3, 1), sines).then_inc(sem("mla_rotated"), 1)
            mul(qr, qr, over(cosines[:, 0, :], 4))
            step(mul(kr, kr, cosines))
            tt_(qr, qr, rot[:, 0:4], ALU.add)
            step(tt_(kr, kr, rot[:, 4:5], ALU.add))
            dve.wait_ge(sem("head_roots"), 2)
            v.reciprocal(head_rs[:, T:2 * T], head_rs[:, T:2 * T]).then_inc(sem("head_rs"), 1)
            split_slab(START["mla_kv"] + 3)
            dve.wait_ge(sem("mla_taken"), 5)
            step(v.memset(flat(KRP), 0.0))
            dve.wait_ge(sem("mla_factors"), 1)
            mul(qr, qr, tiles_of(0, 4))
            v.scalar_tensor_tensor(out=flat(MQ[:, 0:8]), in0=flat(MQ[:, 0:8]), scalar=col("q_nope"), in1=bank(4, 4),
                                   op0=ALU.mult, op1=ALU.mult).then_inc(sem("mla_q_scaled"), 1)
            dve.wait_ge(sem("mla_factors"), 2)
            v.scalar_tensor_tensor(out=flat(MK), in0=flat(MK), scalar=col("k_nope"), in1=bank(4, 4),
                                   op0=ALU.mult, op1=ALU.mult)
            for q in range(2):
                rows = slice(HD * q, HD * (q + 1))
                last = mul(KRP[rows, q:8:2, :], tiles_of(2, 4)[rows], kr[rows, 0, :].unsqueeze(1).to_broadcast([HD, 4, T]))
            last.then_inc(sem("mla_qk"), 1)
            for e in range(2):
                h_ = slice(4 * e, 4 * e + 4)
                late = tiles_of(2 + 2 * e, 4)
                dve.wait_ge(sem("mla_scores"), e + 1)
                v.tensor_copy(S1[:, h_, 0:P], late[:, :, 0:P])
                tt_(S1[:, h_, P:T], late[:, :, P:T], per_head("future_penalty"), ALU.add)
                step(tt_(S0[:, h_], bank(e).rearrange("p (h s) -> p h s", s=P), per_head("future_penalty"), ALU.add))
                v.tensor_reduce(small[:, 4 * e:4 * e + 4], S0[:, h_], AX.X, ALU.max)
                step(v.tensor_reduce(small[:, 8 + 4 * e:12 + 4 * e], S1[:, h_], AX.X, ALU.max))
                for m in (4 * e, 8 + 4 * e):
                    last = v.tensor_scalar(small[:, m:m + 4], small[:, m:m + 4], -(192 ** -0.5), None, ALU.mult)
                last.then_inc(sem("mla_max"), 1)
            for e in range(2):
                h_ = slice(4 * e, 4 * e + 4)
                dve.wait_ge(sem("mla_exp"), e + 1)
                sums = [small[:, m + 4 * e:m + 4 + 4 * e] for m in (16, 24)]
                for m in sums:
                    last = v.reciprocal(m, m)
                step(last)
                mul(S0[:, h_], S0[:, h_], sums[0].unsqueeze(2).to_broadcast([P, 4, P]))
                mul(S1[:, h_], S1[:, h_], sums[1].unsqueeze(2).to_broadcast([P, 4, T])).then_inc(sem("mla_probs"), 1)
            for f in range(4):
                dve.wait_ge(sem("mla_out"), f + 1)
                operand(flat(XL[:, 8 + 2 * f:10 + 2 * f]), bank(f), flat(XH[:, 8 + 2 * f:10 + 2 * f]))
            residual("mla_out", ("norm_gains", 56))

            embedding(1)
            feed_forward("ffn_3")
            down("ffn_3", ("norm_gains", 64))
            per_layer("ple_1", 1, None)


def by_output(w):
    n = w.shape[1] // (2 * P)
    return w.reshape(KT, P, n, 2, P).transpose(2, 1, 3, 0, 4).reshape(n, P, SLAB)


def by_token(w):
    n = w.shape[1] // (2 * P)
    return w.reshape(KT, P, n, 2 * P).transpose(2, 1, 0, 3).reshape(n, P, SLAB)


def by_input(w):
    n = w.shape[0] // (2 * P)
    return w.reshape(n, 2, P, D).transpose(0, 2, 1, 3).reshape(n, P, SLAB)


def feed_forward(first, second, down):
    a, b, c = by_output(first), by_output(second), by_input(down)
    out = [a[0], b[0]]
    for i in range(1, FP):
        out += [a[i], b[i], c[i - 1]]
    return np.stack(out + [c[FP - 1]])


def kernel(**inputs):
    import concourse.bacc as _bacc
    from concourse.bass_utils import run_bass_kernel_spmd as _run

    a = {n: np.asarray(v) for n, v in inputs.items()}
    wc = a["w_comb"][0]
    conv_end, sb_end, gate_end = 3 * W, 6 * W, 6 * W + 3 * D
    ew = a["even_w_in_2"][0]
    mi = a["mla_w_in_2"][0]
    qb = a["mla_w_q_b_2"][0].reshape(3, P, HEADS, 192)
    kvb = a["mla_w_kv_b_2"][0].reshape(2, P, HEADS, 256)
    q_tiles = np.concatenate([
        qb[:, :, :, :P].transpose(0, 1, 2, 3),
        qb[:, :, :, P:].reshape(3, P, 4, P)], axis=2)
    q_slabs = q_tiles.reshape(3, P, 3, 4, P).transpose(2, 1, 3, 0, 4).reshape(3, P, 12 * P)
    q_slabs = np.concatenate([q_slabs, q_slabs[:, :, :4 * P]], axis=2)
    k_slab = kvb[:, :, :, :P].transpose(1, 2, 0, 3).reshape(1, P, SLAB)
    v_slab = kvb[:, :, :, P:].reshape(2, P, 1024).transpose(1, 0, 2).reshape(1, P, SLAB)
    ffw = [feed_forward(a["ffn_w_gate_2"][i, j], a["ffn_w_up_2"][i, j], a["ffn_w_down_2"][i, j])
           for i in range(2) for j in range(2)]
    parts = {
        "conv": by_output(wc[:, :conv_end]),
        "sb_qk": by_output(wc[:, conv_end:conv_end + 2 * W]),
        "sb_v": by_token(wc[:, conv_end + 2 * W:sb_end]),
        "gates": by_output(wc[:, sb_end:gate_end]),
        "rwkv": by_output(wc[:, gate_end:]),
        "branch": a["branch_proj"][0].reshape(3, 4, P, 2, 4, P).transpose(0, 3, 2, 4, 1, 5).reshape(6, P, SLAB),
        "mix_out": by_output(a["w_mix_out"][0]),
        "ca_k": by_output(a["ca_wkv"][0][:, :D]),
        "ca_v": by_token(a["ca_wkv"][0][:, D:]),
        "ca_q": by_output(a["ca_wq"][0]),
        "ca_o": by_output(a["ca_wo"][0]),
        "ffn_c": feed_forward(a["ffn_up"][0][:, :F], a["ffn_up"][0][:, F:], a["ffn_down"][0]),
        "ffn_0": ffw[0], "ffn_1": ffw[1], "ffn_2": ffw[2], "ffn_3": ffw[3],
        "even_in": by_output(np.concatenate([ew[:, :W], ew[:, 2 * W:4 * W], ew[:, 5 * W:]], axis=1)),
        "even_v": by_token(np.concatenate([ew[:, W:2 * W], ew[:, 4 * W:5 * W]], axis=1)),
        "even_out": by_output(a["even_w_out_2"][0]),
        "ple_0": np.concatenate([by_input(a["ple_w_proj_2"][0]), by_output(a["ple_w_gate_2"][0])]),
        "ple_1": np.concatenate([by_input(a["ple_w_proj_2"][1]), by_output(a["ple_w_gate_2"][1])]),
        "mla_in": by_output(np.concatenate([mi, mi[:, -HD:]], axis=1)),
        "mla_q": q_slabs,
        "mla_kv": np.concatenate([k_slab, v_slab]),
        "mla_out": by_output(a["mla_w_out_2"][0]),
    }
    for name, n in STREAM:
        assert parts[name].shape == (n, P, SLAB), name

    def cols(v):
        return np.ascontiguousarray(v).reshape(-1, P).T

    inv_freq = ROPE_THETA ** (-np.arange(0, HD, 2, dtype=np.float32) / np.float32(HD))
    qn, kn = a["mla_q_norm_2"][0], a["mla_k_norm_2"][0]
    tables = {
        "norm_mix": a["norm_mix"], "conv_w": a["conv_w"], "mu": a["mu_rwkv"], "w0": a["w0"], "a0": a["a0"],
        "k_k": a["k_k"], "k_a": a["k_a"], "r_k": a["r_k"], "lnx_w": a["lnx_w"], "lnx_b": a["lnx_b"],
        "gate_b": a["gate_b"], "norm_ca": a["norm_ca"], "norm_mem": a["norm_mem"], "norm_ffn": a["norm_ffn"],
        "ffn_conv_w": a["ffn_conv_w"], "ffn_conv_b": a["ffn_conv_b"], "norm_final": a["norm_final"],
        "norm_gains": a["norm_gains_2"], "hgrn_lb": a["hgrn_lb_raw_2"], "hgrn_out_norm": a["hgrn_out_norm_2"],
        "q_a_norm": a["mla_q_a_norm_2"], "kv_a_norm": a["mla_kv_a_norm_2"],
        "q_nope": qn[:P], "q_rope": np.concatenate([qn[P:], qn[P:]]),
        "k_nope": kn[:P], "k_rope": np.concatenate([kn[P:], kn[P:]]),
        "inv_freq": np.tile(inv_freq.astype(np.float32), 4),
    }
    arrays = {
        "w_stream": np.concatenate([parts[n] for n, _ in STREAM]),
        "x_t": a["x"][0].T,
        "mem_t": a["mem"][0].T,
        "ple_t": a["p_2"][:, 0].transpose(0, 2, 1),
        "params": np.concatenate([cols(tables[n]) for n, _ in COLUMNS], axis=1),
        "tables": constant_tables(),
        "wa_lora": np.concatenate([a["w_lora"][0], a["a_lora"][0]]),
        "g_lora": a["g_lora"][0],
        "spatial_t": a["gmlp_w_s_2"][0].transpose(2, 0, 1),
        "spatial_b": a["gmlp_b_s_2"].reshape(1, HEADS * P),
        "v_gain": a["gmlp_v_norm_2"].reshape(1, W),
        "positions": a["positions_2"].reshape(1, T),
    }
    nc = _bacc.Bacc("TRN2", target_bir_lowering=False, num_devices=1)
    ins, given = {}, {}
    for name, v in arrays.items():
        v = np.ascontiguousarray(v)
        given[f"in_{name}"] = v
        ins[name] = nc.dram_tensor(f"in_{name}", v.shape, mybir.dt.from_np(v.dtype), kind="ExternalInput").ap()
    out = nc.dram_tensor("out_t", (D, T), F32, kind="ExternalOutput").ap()
    program(nc, ins, out)
    r = _run(nc, [given], core_ids=[0])
    return np.ascontiguousarray(r.results[0]["out_t"].T)[None]
```

```python
from contextlib import ExitStack

import numpy as np
import concourse.bass as bass
from concourse import mybir

F32 = mybir.dt.float32
F32R = mybir.dt.float32r
I32 = mybir.dt.int32
ALU = mybir.AluOpType
ACT = mybir.ActivationFunctionType
AX = mybir.AxisListType

P = 128
T = 256
D = 1024
KT = D // P
W = 512
WT = W // P
HEADS = 8
HD = 64
F = 2816
FP = F // (2 * P)
SLAB = 16 * P
CH = 64
EPS = 1e-6
GN_EPS = 64e-5
DECAY_SCALE = float(np.exp(-0.5))
ROPE_THETA = 10000.0
NEG_BIG = -1e30

STREAM = [
    ("conv", 6), ("sb_qk", 4), ("sb_v", 2), ("rwkv", 7), ("gates", 12), ("branch", 6), ("mix_out", 4),
    ("ca_k", 4), ("ca_v", 4), ("ca_q", 4), ("ca_o", 4), ("ffn_c", 33),
    ("ffn_0", 33), ("even_in", 8), ("even_v", 4), ("even_out", 4), ("ffn_1", 33), ("ple_0", 5),
    ("ffn_2", 33), ("mla_in", 3), ("mla_q", 3), ("mla_kv", 2), ("mla_out", 4), ("ffn_3", 33), ("ple_1", 5),
]
START = {}
N_SLABS = 0
for _name, _n in STREAM:
    START[_name] = N_SLABS
    N_SLABS += _n

STAGES = ["mix_out", "ca_o", "ffn_c", "final", "ffn_0", "even_out", "ffn_1", "ple_0", "ffn_2", "mla_out", "ffn_3",
          "ple_1"]

COLUMNS = [
    ("norm_mix", 8), ("conv_w", 12), ("mu", 14), ("w0", 4), ("a0", 4), ("k_k", 4), ("k_a", 4), ("r_k", 4),
    ("lnx_w", 4), ("lnx_b", 4), ("gate_b", 24), ("norm_ca", 8), ("norm_mem", 8), ("norm_ffn", 8),
    ("ffn_conv_w", 132), ("ffn_conv_b", 44), ("norm_final", 8), ("norm_gains", 80), ("hgrn_lb", 4),
    ("hgrn_out_norm", 1), ("q_a_norm", 3), ("kv_a_norm", 2), ("q_nope", 1), ("q_rope", 1), ("k_nope", 1),
    ("k_rope", 1), ("inv_freq", 1),
]
COL = {}
N_COLS = 0
for _name, _n in COLUMNS:
    COL[_name] = N_COLS
    N_COLS += _n

LEVELS = [1, 2, 4, 8, 16, 32, 64]
TABLES = ["identity", "ones", "head_ones", "before", "before_chunk", "upto_chunk", "upto", "past", "future_penalty",
          "after", "first_half", "middle", "pair_middle", "swap"] + \
    [f"level{b}" for b in LEVELS]


def constant_tables():
    s, t = np.meshgrid(np.arange(P), np.arange(P), indexing="ij")
    tab = {
        "identity": s == t,
        "ones": np.ones((P, P)),
        "head_ones": s // HD == t // HD,
        "before": s < t,
        "before_chunk": (s < t) & (s // CH == t // CH),
        "upto_chunk": (s <= t) & (s // CH == t // CH),
        "upto": s <= t,
        "past": s >= t,
        "future_penalty": np.where(s >= t, 0.0, NEG_BIG),
        "first_half": s < HD,
        "middle": t == HD,
        "pair_middle": t == HD + s // HD,
        "after": s > t,
    }
    half = HD // 2
    swap = np.zeros((P, P))
    for base in (0, HD):
        for j in range(half):
            swap[base + half + j, base + j] = -1.0
            swap[base + j, base + half + j] = 1.0
    tab["swap"] = swap
    for b in LEVELS:
        tab[f"level{b}"] = (s // (2 * b) == t // (2 * b)) & (s % (2 * b) < b) & (t % (2 * b) >= b)
    return np.ascontiguousarray(np.stack([tab[n].astype(np.float32) for n in TABLES], axis=1))


def program(nc, ins, out_t):
    ctx = ExitStack()
    with ctx:
        def sb(name, shape, dt=F32):
            return ctx.enter_context(nc.sbuf_tensor(name, shape, dt))

        sems = {}

        def sem(name):
            if name not in sems:
                sems[name] = ctx.enter_context(nc.semaphore(name))
            return sems[name]

        ring_raw = sb("ring_raw", [P, 3, SLAB])
        ring_hi = sb("ring_hi", [P, 3, SLAB], F32R)
        ring_lo = sb("ring_lo", [P, 3, SLAB], F32R)
        XH = sb("operand_hi", [P, 20, T], F32R)
        XL = sb("operand_lo", [P, 20, T], F32R)
        HH = sb("hidden_hi", [P, 2, 2, T], F32R)
        HL = sb("hidden_lo", [P, 2, 2, T], F32R)
        zeros = sb("zeros", [P, T], F32R)
        H = sb("residual", [P, KT, T])
        prm = sb("params", [P, N_COLS])
        tab = sb("tables", [P, len(TABLES), P])
        root = sb("root", [P, T + 2])
        inv = sb("inv", [P, T + 2])
        one_minus_mu = sb("one_minus_mu", [P, 14])
        small = sb("small", [P, 64])
        U = 1024
        arena = sb("arena", [P, 16 * U])
        PS = ctx.enter_context(nc.psum_tensor("PS", [P, 8, 512], F32))

        def area(start, tiles, width=T):
            a = int(start * U)
            return arena[:, a:a + tiles * width].rearrange("p (n t) -> p n t", t=width)

        def col(name, i=0, n=1):
            return prm[:, COL[name] + i:COL[name] + i + n]

        def table(name):
            return tab[:, TABLES.index(name), :]

        def per_head(name, n=4):
            return table(name).unsqueeze(1).to_broadcast([P, n, P])

        def bank(b, n=1):
            return PS[:, b:b + n, :].rearrange("p b c -> p (b c)")

        def tiles_of(b, n):
            return bank(b, (n + 1) // 2).rearrange("p (n t) -> p n t", t=T)[:, 0:n, :]

        def flat(ap):
            return ap.rearrange("p n t -> p (n t)")

        squares = area(12, 8)
        silu_out, hidden = flat(area(14, 2)), flat(area(14.5, 2))
        conv_x = [area(0, 2), area(0.5, 2)]
        conv_acc = area(15, 2)
        conv_acc2 = area(15.5, 2)
        conv_in = area(0, 12)
        conv_u, conv_y = area(3, 4), area(4, 4)
        sbq = area(5, 8)
        sbv = area(7, 2, W)
        sb_z = [flat(area(8 + 1.5 * q, 6)) for q in range(2)]
        sb_w = [flat(area(11 + 1.5 * q, 6)) for q in range(2)]
        rp = area(0, 14)
        shift_in = [area(14, 2), area(14.5, 2)]
        R_, K_, V_, LORA = rp[:, 0:4], rp[:, 4:8], rp[:, 8:12], rp[:, 12:14]
        A_, G_, KK, BN = (area(3.5 + i, 4) for i in range(4))
        LW, LC, EP, TM = (area(7.5 + i, 4) for i in range(4))
        lora_w = area(11.5, 2, W)
        Vt, Kt, Bt = area(7.5, 1, W), area(8, 1, W), area(8.5, 1, W)
        ZP = area(9, 8, P)
        Xm, Ym, Yt, Fm, Xb = (area(10 + i, 8, P) for i in range(5))
        MT = area(15, 4, HD)
        state = area(15.25, 4, HD)
        chunk_decay = small[:, 0:16].rearrange("p (f c) -> p f c", c=4)
        gate_stage = [area(15.5, 2), area(3, 2)]
        gates = [area(0, 12), area(7.5, 12)]
        merged, gated = area(3, 8), area(10.5, 4)
        mem = area(14, 8)
        ca_k, ca_v, ca_q = area(2, 8), area(4, 2, D), area(6, 8)
        probs, probs_t = area(8, 8), area(10, 8)
        ev = area(0, 16)
        AU, BQ, BF, BG = ev[:, 0:4], ev[:, 4:8], ev[:, 8:12], ev[:, 12:16]
        AV, BI = area(4, 2, W), area(5, 2, W)
        spatial_b = arena[0:1, 10 * U:11 * U]
        KB, BC = area(6, 4), area(7, 4)
        DIF = [area(8, 4), area(9, 4)]
        XM = [area(10, 4), area(11, 4)]
        AT = area(12, 8, P)
        AC = area(13, 4, P)
        spatial_w = AM = area(14, 8, P)
        v_gain = area(15, 1, W)
        ple_in = area(4, 2)
        ple_p, ple_g, ple_add = area(0, 8), area(2, 8), area(6, 8)
        MI, MQ, MK, MV = area(0, 6), area(1.5, 12), area(4.5, 8), area(6.5, 2, D)
        KRP = area(12.5, 8)
        msq = area(9.5, 12)
        cosines, sines = area(15.5, 1), area(15.75, 1)
        ang, turns = area(9, 1), area(9.25, 1)
        latent_rs = area(14, 2)
        head_rs = arena[0:8, int(9 * U):int(9.5 * U)]
        pick_head = arena[0:8, int(14.5 * U):int(15.5 * U)].rearrange("p (h c) -> p h c", c=P)
        pick_pair = arena[0:8, int(8.5 * U):int(9 * U)].rearrange("p (h c) -> p h c", c=P)
        S0, S1 = area(8.5, 8, P), area(9.5, 8)
        PT0, PT1 = area(11.5, 8), area(13.5, 8, P)

        landed = [sem(f"landed{s}") for s in range(3)]
        hi_split, lo_split = sem("hi_split"), sem("lo_split")
        multiplied = sem("multiplied")

        def chunks_until(stage, chunks=4):
            return 4 * STAGES.index(stage) + chunks

        def place(g0, i=0, by=3):
            return g0 % 3, i * (by // 3) + g0 // 3, i * by + g0

        def gate_slab_at(tile, level):
            n = 2 + 5 * tile + level
            return n if 1 <= level <= 5 and n < 12 else None

        def gate_bank(n):
            return (7, 6, 0)[n] if n < 3 else (0, 7)[n % 2]

        block = ctx.enter_context(nc.Block())

        @block.sync
        def _(sp):
            stream = ins["w_stream"]
            for g in range(3):
                if g == 1:
                    sp.wait_ge(sem("x_landed1"), 16)
                sp.dma_start(ring_raw[:, g, :], stream[g]).then_inc(landed[g], 16)
            turns_ = (N_SLABS - 3) // 3
            with sp.Fori(0, turns_) as i:
                for j in range(3):
                    sp.wait_ge(lo_split, i * 3 + (j + 1))
                    sp.dma_start(ring_raw[:, j, :], stream[bass.ds(i * 3 + (j + 3), 1)].squeeze(0))\
                        .then_inc(landed[j], 16)
            for g in range(3 + 3 * turns_, N_SLABS):
                sp.wait_ge(lo_split, g - 2)
                sp.dma_start(ring_raw[:, g % 3, :], stream[g]).then_inc(landed[g % 3], 16)
            sp.wait_ge(sem("residual_ready"), chunks_until("ple_1"))
            sp.dma_start(out_t.rearrange("(k p) t -> p k t", p=P), H[:]).then_inc(sem("stored"), 16)
            sp.wait_ge(sem("stored"), 16)

        @block.gpsimd
        def _(pool):
            adds = [0]

            def add(out, a, b):
                return nc.gpsimd.tensor_tensor(out, a, b, ALU.add)

            def step(ins_):
                adds[0] += 1
                ins_.then_inc(sem("pool_step"), 1)
                pool.wait_ge(sem("pool_step"), adds[0])

            norms = [0]

            def norm_fold():
                norms[0] += 1
                pool.wait_ge(sem("norm_squared"), norms[0])
                step(add(squares[:, 0:4], squares[:, 0:4], squares[:, 4:8]))
                step(add(squares[:, 0:2], squares[:, 0:2], squares[:, 2:4]))
                add(squares[:, 0], squares[:, 0], squares[:, 1]).then_inc(sem("norm_folded"), 1)

            def ple_fold(n):
                pool.wait_ge(sem("chunk_squared"), 4 * n + 7)
                step(add(squares[:, 0:2], squares[:, 0:2], squares[:, 2:4]))
                add(squares[:, 0:2], squares[:, 0:2], squares[:, 4:6]).then_inc(sem("ple_folded"), 1)

            def gl_diff(li):
                if li > 2:
                    pool.wait_ge(sem("gl_factors"), li - 1)
                d = DIF[li % 2]
                if li < 8:
                    b = LEVELS[li - 1]
                    bc = flat(BC).rearrange("p (n c) -> p n c", c=2 * b)
                    ref = bc[:, :, b - 1:b].to_broadcast([P, 4 * T // (2 * b), 2 * b])
                    nc.gpsimd.tensor_tensor(flat(d).rearrange("p (n c) -> p n c", c=2 * b), bc, ref, ALU.subtract)\
                        .then_inc(sem("gl_diff"), 1)
                else:
                    nc.gpsimd.tensor_copy(d[:, :, P:T], BC[:, :, P:T])
                    nc.gpsimd.tensor_tensor(d[:, :, 0:P], BC[:, :, 0:P], BC[:, :, P - 1:P].to_broadcast([P, 4, P]),
                                            ALU.subtract).then_inc(sem("gl_diff"), 1)

            nc.gpsimd.memset(zeros[:].bitcast(F32), 0.0)
            for c in range(4):
                pool.wait_ge(sem(f"x_landed{c}"), 16)
            pool.dma_start(tab[:], ins["tables"]).then_inc(sem("tables_landed"), 16)
            norm_fold()
            pool.wait_ge(sem("operand_lo"), KT + 2)
            pool.dma_start(lora_w[:, 0, :], ins["wa_lora"]).then_inc(sem("lora_landed"), 16)
            pool.dma_start(lora_w[:, 1, :], ins["g_lora"]).then_inc(sem("lora_landed"), 16)
            for n in range(12):
                pool.wait_ge(sem("gates_active"), n + 1)
                if n:
                    pool.wait_ge(sem("gates_moved"), 16 * n)
                pool.dma_start(ins["spilled_gates"][n], flat(gate_stage[n % 2])).then_inc(sem("gates_moved"), 16)
            pool.wait_ge(sem("gates_moved"), 12 * 16)
            pool.wait_ge(sem("rk_out"), 1)
            for half in range(2):
                pool.dma_start(gates[half].rearrange("p (n m) t -> p n (m t)", m=2),
                               ins["spilled_gates"][6 * half:6 * half + 6].rearrange("n p c -> p n c"))\
                    .then_inc(sem("gates_moved"), 16)
            pool.dma_start(mem, ins["mem_t"].rearrange("(k p) t -> p k t", p=P)).then_inc(sem("mem_landed"), 16)
            norm_fold()
            pool.wait_ge(sem("mem_factor"), 1)
            nc.gpsimd.tensor_tensor(squares, mem, inv[:, 0:T].unsqueeze(1).to_broadcast([P, KT, T]), ALU.mult)\
                .then_inc(sem("mem_scaled"), 1)
            for _ in range(3):
                norm_fold()
            pool.wait_ge(sem("residual_ready"), chunks_until("ffn_0"))
            pool.dma_start(spatial_w, ins["spatial_t"]).then_inc(sem("spatial_landed"), 16)
            pool.dma_start(spatial_b, ins["spatial_b"]).then_inc(sem("spatial_landed"), 16)
            pool.dma_start(v_gain[:, 0, :], ins["v_gain"].to_broadcast([P, W])).then_inc(sem("spatial_landed"), 16)
            norm_fold()
            pool.wait_ge(sem("gl_factors"), 1)
            pool.wait_ge(sem("spatial_ready"), 1)
            for li in range(1, 9):
                gl_diff(li)
            for n, (before, folds_) in enumerate((("even_out", 2), ("mla_out", 2))):
                pool.wait_ge(sem("residual_ready"), chunks_until(before))
                if n == 0:
                    pool.dma_start(cosines.bitcast(I32)[:, 0, :], ins["positions"].to_broadcast([P, T]))\
                        .then_inc(sem("positions_landed"), 16)
                pool.dma_start(ple_in, ins["ple_t"][n].rearrange("(k p) t -> p k t", p=P))\
                    .then_inc(sem("ple_landed"), 16)
                for _ in range(folds_):
                    norm_fold()
                ple_fold(n)
                if n == 0:
                    norm_fold()
                    norm_fold()

        @block.tensor
        def _(pe):
            taken = [0]
            split_tiles = [0]

            def mm(out, lhs, rhs, start=True, stop=True):
                return nc.tensor.matmul(out, lhs, rhs, start=start, stop=stop, skip_group_check=True)

            def block_product(out, slot, b, xh, xl, start, stop):
                w = slice(b * P, (b + 1) * P)
                mm(out, ring_hi[:, slot, w], xh, start, False)
                mm(out, ring_hi[:, slot, w], xl, False, False)
                return mm(out, ring_lo[:, slot, w], xh, False, stop)

            def output_slab(g0, x0, out, i=0, by=3, fresh=(), between=None):
                slot, _, g = place(g0, i, by)
                pe.wait_ge(lo_split, g + 1)
                for m in range(2):
                    if m and between is not None:
                        between()
                    for k in range(KT):
                        if m == 0 and k in fresh:
                            operands(1)
                        last = block_product(out[:, m * T:(m + 1) * T], slot, m * KT + k,
                                             XH[:, x0 + k, :], XL[:, x0 + k, :], k == 0, k == KT - 1)
                last.then_inc(multiplied, 1)

            def operands(n):
                split_tiles[0] += n
                pe.wait_ge(sem("operand_lo"), split_tiles[0])

            def free_bank(i=0):
                if taken[0] >= 3:
                    pe.wait_ge(sem("output_taken"), taken[0] - 2)
                b = taken[0] % 3
                taken[0] += 1
                return b

            def project(name, x0, n, fresh=(), norm=False, by_token=False):
                for j in range(n):
                    output_slab(START[name] + j, x0, bank(free_bank()), fresh=fresh if j == 0 else (),
                                between=(lambda: norm_sum(by_token)) if norm and j == 1 else None)

            def project_by_token(name, x0, n):
                for j in range(n):
                    out = bank(free_bank())
                    slot, _, g = place(START[name] + j)
                    pe.wait_ge(lo_split, g + 1)
                    for tt in range(2):
                        tok = slice(tt * P, (tt + 1) * P)
                        for k in range(KT):
                            w = slice(k * T, (k + 1) * T)
                            o = out[:, tt * T:(tt + 1) * T]
                            mm(o, XH[:, x0 + k, tok], ring_hi[:, slot, w], k == 0, False)
                            mm(o, XL[:, x0 + k, tok], ring_hi[:, slot, w], False, False)
                            last = mm(o, XH[:, x0 + k, tok], ring_lo[:, slot, w], False, k == KT - 1)
                    last.then_inc(multiplied, 1)

            norms = [0]
            folds = [0]

            def norm_sum(by_token=False, b=7):
                norms[0] += 1
                folds[0] += 1
                pe.wait_ge(sem("norm_folded"), folds[0])
                last = mm(bank(b)[:, 0:T], table("ones"), squares[:, 0, :])
                if by_token:
                    for tt in range(2):
                        last = mm(bank(b)[:, T + tt:T + tt + 1], squares[:, 0, tt * P:(tt + 1) * P],
                                  table("ones")[:, 0:1])
                last.then_inc(sem("norm_summed"), 1)

            def chunk_sums(b, k, start, stop):
                mm(bank(b)[:, 0:T], table("ones"), squares[:, k, :], start, False)
                return mm(bank(b)[:, 0:T], table("ones"), squares[:, k + 1, :], False, stop)

            ffns = [0]
            EVERY = tuple(range(KT))

            def feed_forward(name):
                g0, n = START[name], ffns[0]
                split, gate_scaled, up_taken = sem("hidden_lo"), sem("gate_scaled"), sem("up_taken")

                def down(at, odd, i, pairs):
                    slot, _, g = place(at, i, 6)
                    pe.wait_ge(lo_split, g + 1)
                    pe.wait_ge(split, pairs)
                    for k in range(2):
                        for m in range(KT):
                            last = block_product(bank(3 + m // 2)[:, m % 2 * T:(m % 2 + 1) * T], slot, k * KT + m,
                                                 HH[:, odd, k, :], HL[:, odd, k, :], False, False)
                    last.then_inc(multiplied, 1)

                output_slab(g0, 0, bank(0), fresh=EVERY)
                output_slab(g0 + 1, 0, bank(1), between=norm_sum)
                for b in range(3, 7):
                    for m in range(2):
                        mm(bank(b)[:, m * T:(m + 1) * T], zeros[:, 0:P], zeros[:], True, False)
                with pe.Fori(0, FP // 2) as i:
                    pe.wait_ge(gate_scaled, i * 2 + (n * FP + 1))
                    output_slab(g0 + 2, 0, bank(2), i, 6)
                    pe.wait_ge(sem("norm_root"), norms[0])
                    pe.wait_ge(up_taken, i * 2 + (n * FP + 1))
                    output_slab(g0 + 3, 0, bank(7), i, 6)
                    down(g0 + 4, 0, i, i * 2 + (n * FP + 1))
                    pe.wait_ge(gate_scaled, i * 2 + (n * FP + 2))
                    output_slab(g0 + 5, 0, bank(0), i, 6)
                    pe.wait_ge(up_taken, i * 2 + (n * FP + 2))
                    output_slab(g0 + 6, 0, bank(1), i, 6)
                    down(g0 + 7, 1, i, i * 2 + (n * FP + 2))
                slot, _, g = place(g0 + 32)
                pe.wait_ge(lo_split, g + 1)
                pe.wait_ge(split, (n + 1) * FP)
                for m in range(KT):
                    for k in range(2):
                        last = block_product(bank(3 + m // 2)[:, m % 2 * T:(m % 2 + 1) * T], slot, k * KT + m,
                                             HH[:, 0, k, :], HL[:, 0, k, :], False, k == 1)
                    if m % 2 and m < KT - 1:
                        last.then_inc(sem("down_bank"), 1)
                last.then_inc(multiplied, 1)
                ffns[0] += 1

            def residual_project(name, x0, fresh):
                for j in range(4):
                    output_slab(START[name] + j, x0, bank((6, 7, 4, 5)[j]), fresh=fresh if j == 0 else ())

            def first_norm():
                pe.wait_ge(sem("tables_landed"), 16)
                norm_sum(True)

            for j in range(6):
                output_slab(START["conv"] + j, 0, bank(free_bank()), fresh=EVERY if j == 0 else (),
                            between=first_norm if j == 1 else None)
            project("sb_qk", 0, 4)
            project_by_token("sb_v", 0, 2)

            before_rwkv = taken[0]

            def rwkv_slab(j):
                if j >= 2:
                    pe.wait_ge(sem("output_taken"), before_rwkv + j - 1)
                output_slab(START["rwkv"] + j, 0, bank(6 + j % 2))
                taken[0] += 1

            def sb_scores(q):
                if q:
                    pe.wait_ge(sem("sb_z_taken"), q)
                rows = slice(HD * q, HD * (q + 1))
                for f in range(4):
                    qt, kt = sbq[rows, f, :], sbq[rows, 4 + f, :]
                    o = slice(f * P, (f + 1) * P)
                    mm(bank(0)[:, o], kt[:, 0:P], qt[:, 0:P])
                    mm(bank(1)[:, o], kt[:, 0:P], qt[:, P:T])
                    last_ = mm(bank(2)[:, o], kt[:, P:T], qt[:, P:T])
                last_.then_inc(sem("sb_z"), 1)

            def sb_suffix(q):
                pe.wait_ge(sem("sb_log"), q + 1)
                if q:
                    pe.wait_ge(sem("sb_logw"), q)
                z = sb_z[q]
                mm(bank(3), table("after"), z[:, 0:512])
                mm(bank(4), table("after"), z[:, 512:1024], True, False)
                mm(bank(4), table("ones"), z[:, 1024:1536], False, True)
                mm(bank(5), table("after"), z[:, 1024:1536]).then_inc(sem("sb_suffix"), 1)

            def sb_values(q):
                pe.wait_ge(sem("sb_z_taken"), 2)
                pe.wait_ge(sem("sb_att"), q + 1)
                w = sb_w[q].rearrange("p (b f t) -> p b f t", b=3, f=4)
                for f in range(4):
                    o = bank(f // 2)[HD * q:HD * (q + 1), f % 2 * T:(f % 2 + 1) * T]
                    h = slice((2 * f + q) * HD, (2 * f + q + 1) * HD)
                    mm(o[:, 0:P], sbv[:, 0, h], w[:, 0, f, :])
                    mm(o[:, P:T], sbv[:, 0, h], w[:, 1, f, :], True, False)
                    last_ = mm(o[:, P:T], sbv[:, 1, h], w[:, 2, f, :], False, True)
                if q:
                    last_.then_inc(sem("sb_y"), 1)

            pe.wait_ge(sem("output_taken"), taken[0])
            for j, (part, q) in enumerate(((sb_scores, 0), (sb_scores, 1), (sb_suffix, 0), (sb_suffix, 1),
                                           (sb_values, 0), (sb_values, 1))):
                part(q)
                rwkv_slab(j)
            rwkv_slab(6)

            before_gates = taken[0]

            def gate_slab(n):
                if n >= 3:
                    pe.wait_ge(sem("output_taken"), before_gates + n - 1)
                output_slab(START["gates"] + n, 0, bank(gate_bank(n)))
                taken[0] += 1

            pe.wait_ge(sem("output_taken"), before_gates - 1)
            gate_slab(0)
            pe.wait_ge(sem("lora_landed"), 32)
            pe.wait_ge(sem("rk_lora_in"), 1)
            pe.wait_ge(sem("operand_lo"), KT + 2)
            for f in range(4):
                c = slice(f * P, (f + 1) * P)
                o = slice(f % 2 * T, (f % 2 + 1) * T)
                mm(bank(0 + f // 2)[:, o], lora_w[0:HD, 0, c], LORA[0:HD, 0, :])
                mm(bank(2 + f // 2)[:, o], lora_w[HD:P, 0, c], LORA[HD:P, 0, :])
                last = mm(bank(4 + f // 2)[:, o], lora_w[:, 1, c], LORA[:, 1, :])
            last.then_inc(sem("rk_lora_out"), 1)
            pe.wait_ge(sem("output_taken"), before_gates)
            gate_slab(1)
            pe.wait_ge(sem("output_taken"), before_gates + 2)
            pe.wait_ge(sem("rk_squares"), 1)
            for h in range(2):
                last = mm(bank(6 + h), table("head_ones"), flat(TM)[:, 512 * h:512 * (h + 1)])
            last.then_inc(sem("rk_norms"), 1)
            pe.wait_ge(sem("rk_gates"), 1)
            gate_slab(2)
            pe.wait_ge(sem("rk_bonus_in"), 1)
            for h in range(2):
                last = mm(bank(6 + h), table("head_ones"), flat(BN)[:, 512 * h:512 * (h + 1)])
            last.then_inc(sem("rk_bonus_sums"), 1)
            pe.wait_ge(sem("rk_prep"), 1)
            pe.wait_ge(sem("output_taken"), before_gates + 3)

            def heads(q):
                return [(f, 2 * f + q) for f in range(4)]

            for tt in range(2):
                tok = slice(tt * P, (tt + 1) * P)
                if tt:
                    pe.wait_ge(sem("rk_tile_done"), 1)
                for f in range(4):
                    c = slice(f * P, (f + 1) * P)
                    nc.tensor.transpose(bank(0)[:, c], V_[:, f, tok], table("identity"))
                    nc.tensor.transpose(bank(1)[:, c], KK[:, f, tok], table("identity"))
                    nc.tensor.transpose(bank(2)[:, c], K_[:, f, tok], table("identity"))
                    last = nc.tensor.transpose(bank(3)[:, c], A_[:, f, tok], table("identity"))
                last.then_inc(sem("rk_turned"), 1)
                for q in range(2):
                    rows = slice(HD * q, HD * (q + 1))
                    for f in range(4):
                        c = slice(f * P, (f + 1) * P)
                        mm(bank(4 + q)[:, c], K_[rows, f, tok], KK[rows, f, tok])
                        last = mm(bank(6 + q)[:, c], A_[rows, f, tok], KK[rows, f, tok])
                last.then_inc(sem("rk_pairs"), 1)
                pe.wait_ge(sem("rk_masked"), tt + 1)
                pe.wait_ge(sem("rk_turned_act"), tt + 1)
                for q in range(2):
                    for f, h in heads(q):
                        last = mm(bank(0)[:, h * HD:(h + 1) * HD], Fm[:, 4 * q + f, :], Vt[:, 0, h * HD:(h + 1) * HD])
                last.then_inc(sem("rk_p"), 1)
                pe.wait_ge(sem("rk_p_taken"), tt + 1)
                for li in range(6):
                    for q in range(2):
                        n = (tt * 6 + li) * 2 + q
                        pe.wait_ge(sem("rk_x"), n + 1)
                        if li:
                            pe.wait_ge(sem("rk_y"), n - 1)
                        for f in range(4):
                            rhs = Yt[:, 4 * q + f, :] if li else table("identity")
                            last = mm(bank(1 + q)[:, f * P:(f + 1) * P], Xb[:, 4 * q + f, :], rhs)
                        last.then_inc(sem("rk_f"), 1)
                    if li == 0:
                        continue
                    for q in range(2):
                        n = (tt * 5 + li - 1) * 2 + q
                        pe.wait_ge(sem("rk_f_taken"), n + 1)
                        for f in range(4):
                            c, e = slice(f * P, (f + 1) * P), 4 * q + f
                            last = mm(bank(3 + q)[:, c], Fm[:, e, :], Ym[:, e, :])
                            if li < 5:
                                last = mm(bank(5 + q)[:, c], Ym[:, e, :], Fm[:, e, :])
                        last.then_inc(sem("rk_dy"), 1)
                    if gate_slab_at(tt, li) is not None:
                        gate_slab(gate_slab_at(tt, li))
                pe.wait_ge(sem("rk_y"), (tt + 1) * 12)
                for q in range(2):
                    for f, h in heads(q):
                        last = mm(bank(3 + q)[:, f * P:(f + 1) * P], Ym[:, 4 * q + f, :], ZP[:, h, :])
                last.then_inc(sem("rk_wu"), 1)
                for q in range(2):
                    rows = slice(HD * q, HD * (q + 1))
                    for f in range(4):
                        c = slice(f * P, (f + 1) * P)
                        mm(bank(5 + q)[:, c], K_[rows, f, tok], R_[rows, f, tok])
                        last = mm(bank(1 + q)[:, c], A_[rows, f, tok], R_[rows, f, tok])
                last.then_inc(sem("rk_out_pairs"), 1)
                pe.wait_ge(sem("rk_wu_taken"), tt + 1)
                pe.wait_ge(sem("output_taken"), taken[0])
                pe.wait_ge(sem("rk_out_masked"), tt + 1)
                for q in range(2):
                    for f, h in heads(q):
                        e = 4 * q + f
                        mm(bank(7)[HD * q:HD * (q + 1), f * P:(f + 1) * P], Xb[:, e, 0:HD], Fm[:, e, :])
                        o = bank(3)[HD * q:HD * (q + 1), f * P:(f + 1) * P]
                        mm(o, Vt[:, 0, h * HD:(h + 1) * HD], Yt[:, e, :], True, False)
                        last = mm(o, Xb[:, e, HD:P], Fm[:, e, :], False, True)
                last.then_inc(sem("rk_inner"), 1)
                cm = slice(HD, P) if tt == 0 else slice(0, HD)
                for q in range(2):
                    for f, h in heads(q):
                        last = mm(bank(0)[HD * q:HD * (q + 1), f * HD:(f + 1) * HD], Xb[cm, 4 * q + f, 0:HD],
                                  Bt[cm, 0, h * HD:(h + 1) * HD])
                last.then_inc(sem("rk_transition"), 1)
                pe.wait_ge(sem("rk_transition_taken"), tt + 1)
                pe.wait_ge(sem("rk_inner_taken"), tt + 1)
                for c in range(2):
                    gc = 2 * tt + c
                    rows_c = slice(c * CH, (c + 1) * CH)
                    if gc:
                        pe.wait_ge(sem("rk_state"), gc)
                        for q in range(2):
                            rows = slice(HD * q, HD * (q + 1))
                            for f in range(4):
                                last = mm(bank(6 + q)[rows, f * P + c * CH:f * P + (c + 1) * CH], state[rows, f, :],
                                          R_[rows, f, gc * CH:(gc + 1) * CH])
                        if gc != 2:
                            last.then_inc(sem("rk_carried"), 1)
                    if gc == 3:
                        continue
                    for q in range(2):
                        rows = slice(HD * q, HD * (q + 1))
                        for f, h in heads(q):
                            hc = slice(h * HD, (h + 1) * HD)
                            o = bank(5)[rows, f * HD:(f + 1) * HD]
                            mm(o, Kt[rows_c, 0, hc], Vt[rows_c, 0, hc], True, False)
                            last = mm(o, Bt[rows_c, 0, hc], Xb[rows_c, 4 * q + f, HD:P], False, True)
                            if gc:
                                last = mm(bank(1 + q)[rows, f * HD:(f + 1) * HD], MT[rows, f, :], state[rows, f, :])
                    last.then_inc(sem("rk_update"), 1)
            def branch_slab(j, first):
                slot, _, g = place(START["branch"] + j)
                pe.wait_ge(lo_split, g + 1)
                for m in range(4):
                    for k in range(4):
                        x = 8 + 4 * (j // 2) + k
                        last_ = block_product(tiles_of(first, 4)[:, m, :], slot, 4 * m + k, XH[:, x, :], XL[:, x, :],
                                              k == 0, k == 3)
                last_.then_inc(multiplied, 1)

            operands(2)
            pe.wait_ge(sem("rk_out"), 1)
            for h in range(2):
                last = mm(bank(h), table("head_ones"), flat(KK)[:, 512 * h:512 * (h + 1)])
            last.then_inc(sem("rk_moments"), 1)
            branch_slab(0, 4)
            pe.wait_ge(sem("rk_centred"), 1)
            for h in range(2):
                last = mm(bank(2 + h), table("head_ones"), flat(TM)[:, 512 * h:512 * (h + 1)])
            last.then_inc(sem("rk_moments"), 1)
            branch_slab(1, 6)
            branch_slab(2, 0)
            for j in range(3, 6):
                pe.wait_ge(sem("branch_taken"), j - 2)
                if j == 4:
                    operands(1)
                branch_slab(j, (4, 6, 0)[j - 3])
                if j == 3:
                    pe.wait_ge(sem("rk_root"), 1)
                    norm_sum(b=3)
            residual_project("mix_out", 0, (0, 4, 6))

            pe.wait_ge(sem("output_taken"), taken[0])
            pe.wait_ge(sem("branch_taken"), 7)
            operands(KT)
            project("ca_k", 8, 4)
            project_by_token("ca_v", 8, 4)
            norm_sum()
            project("ca_q", 0, 4, fresh=EVERY)
            pe.wait_ge(sem("output_taken"), taken[0])
            for tt in range(2):
                for h in range(4):
                    i = 4 * tt + h
                    for d in range(2):
                        last = mm(bank(i // 2)[:, i % 2 * T:(i % 2 + 1) * T], ca_q[:, 2 * h + d, tt * P:(tt + 1) * P],
                                  ca_k[:, 2 * h + d, :], d == 0, d == 1)
                last.then_inc(sem("ca_scores"), 1)
            for i in range(8):
                tt, h = divmod(i, 4)
                pe.wait_ge(sem("ca_probs"), tt + 1)
                for mt in range(2):
                    last = nc.tensor.transpose(bank(4 + h)[:, mt * T + tt * P:mt * T + (tt + 1) * P],
                                               probs[:, i, mt * P:(mt + 1) * P], table("identity"))
            last.then_inc(sem("ca_turned"), 1)
            pe.wait_ge(sem("ca_turned_taken"), 1)
            for h in range(4):
                for d in range(2):
                    for mt in range(2):
                        last = mm(bank(h)[:, d * T:(d + 1) * T], ca_v[:, mt, (2 * h + d) * P:(2 * h + d + 1) * P],
                                  probs_t[:, 2 * h + mt, :], mt == 0, mt == 1)
                last.then_inc(sem("ca_out"), 1)
            residual_project("ca_o", 8, (0, 2, 4, 6))

            feed_forward("ffn_c")
            norms[0] += 1
            for c in range(4):
                pe.wait_ge(sem("chunk_squared"), c + 1)
                last = chunk_sums(7, 2 * c, c == 0, c == 3)
            last.then_inc(sem("norm_summed"), 1)

            feed_forward("ffn_0")

            project("even_in", 0, 8, fresh=EVERY, norm=True, by_token=True)
            project_by_token("even_v", 0, 4)
            pe.wait_ge(sem("output_taken"), taken[0])
            pe.wait_ge(sem("spatial_ready"), 1)
            pe.wait_ge(sem("spatial_landed"), 48)
            for f in range(4):
                for q in range(2):
                    h = 2 * f + q
                    for tt in range(2):
                        o = bank(f // 2)[HD * q:HD * (q + 1), f % 2 * T + tt * P:f % 2 * T + (tt + 1) * P]
                        mm(o, AV[:, tt, h * HD:(h + 1) * HD], spatial_w[:, h, :], True, False)
                        last = mm(o, table("ones")[0:1, 0:HD], spatial_b[:, h * P:(h + 1) * P], False, True)
            last.then_inc(sem("spatial_mixed"), 1)
            for li in range(9):
                pe.wait_ge(sem("gl_factors"), li + 1)
                if li >= 2:
                    pe.wait_ge(sem("gl_added"), li - 1)
                if li < 8:
                    for tt in range(2):
                        tok = slice(tt * P, (tt + 1) * P)
                        for h in range(4):
                            k = KB[:, h, tok] if li == 0 else XM[li % 2][:, h, tok]
                            q = BQ[:, h, tok] if li == 0 else XM[li % 2][:, h, tok]
                            last = mm(bank(2 + 2 * (li % 2) + tt)[:, h * P:(h + 1) * P], k, q)
                else:
                    for h in range(4):
                        last = mm(bank(2)[:, h * P:(h + 1) * P], XM[0][:, h, 0:P], XM[0][:, h, P:T])
                last.then_inc(sem("gl_pairs"), 1)
            pe.wait_ge(sem("gl_added"), 9)
            for h in range(4):
                o, c = bank(6 + h // 2)[:, h % 2 * T:(h % 2 + 1) * T], slice(h * P, (h + 1) * P)
                mm(o[:, 0:P], BI[:, 0, c], AT[:, h, :])
                mm(o[:, P:T], BI[:, 1, c], AT[:, 4 + h, :], True, False)
                last = mm(o[:, P:T], BI[:, 0, c], AC[:, h, :], False, True)
                if h % 2:
                    last.then_inc(sem("gl_out"), 1)
            for h in range(2):
                pe.wait_ge(sem("gl_squares"), h + 1)
                mm(bank(2 + h), table("ones"), flat(KB)[:, 512 * h:512 * (h + 1)]).then_inc(sem("gl_norms"), 1)
            operands(1)
            residual_project("even_out", 8, (4, 6))

            def per_layer(name, n):
                g0 = START[name]

                def gate_norm():
                    pe.wait_ge(sem("ple_copied"), n + 1)
                    norm_sum()

                operands(1)
                slot, _, g = place(g0)
                pe.wait_ge(lo_split, g + 1)
                for m in range(KT):
                    for k in range(2):
                        last = block_product(bank((0, 1, 2, 7)[m // 2])[:, m % 2 * T:(m % 2 + 1) * T], slot,
                                             k * KT + m, XH[:, 8 + k, :], XL[:, 8 + k, :], k == 0, k == 1)
                last.then_inc(multiplied, 1)
                for j in range(4):
                    output_slab(g0 + 1 + j, 0, bank(3 + j), fresh=EVERY if j == 0 else (),
                                between=gate_norm if j == 0 else None)
                pe.wait_ge(sem("ple_folded"), n + 1)
                chunk_sums(0, 0, True, False)
                pe.wait_ge(sem("chunk_squared"), 4 * (n + 2))
                chunk_sums(0, 6, False, True).then_inc(sem("ple_summed"), 1)

            feed_forward("ffn_1")
            per_layer("ple_0", 0)
            feed_forward("ffn_2")

            project("mla_in", 0, 3, fresh=EVERY, norm=True)
            pe.wait_ge(sem("output_taken"), taken[0])
            for j in range(3):
                slot, _, g = place(START["mla_q"] + j)
                pe.wait_ge(lo_split, g + 1)
                out = bank(2 * j, 2)
                for m in range(4):
                    for k in range(3):
                        if j == 0 and m == 0:
                            operands(1)
                        last = block_product(out[:, m * T:(m + 1) * T], slot, 3 * m + k, XH[:, 8 + k, :],
                                             XL[:, 8 + k, :], k == 0, k == 2)
                last.then_inc(multiplied, 1)
                if j == 0:
                    pe.wait_ge(sem("latent_squared"), 1)
                    for k in range(5):
                        side = k // 3
                        mm(bank(7)[:, side * T:(side + 1) * T], table("ones"), squares[:, k, :], k in (0, 3),
                           k in (2, 4))
                    for tt in range(2):
                        for k in (3, 4):
                            last = mm(bank(6)[:, tt:tt + 1], squares[:, k, tt * P:(tt + 1) * P],
                                      table("ones")[:, 0:1], k == 3, k == 4)
                    last.then_inc(sem("latent_summed"), 1)
            slot, _, g = place(START["mla_kv"])
            pe.wait_ge(lo_split, g + 1)
            operands(2)
            for m in range(8):
                if m in (0, 4):
                    pe.wait_ge(sem("mla_taken"), 1 + m // 4)
                for k in range(2):
                    last = block_product(bank(m // 2)[:, m % 2 * T:(m % 2 + 1) * T], slot, 2 * m + k,
                                         XH[:, 11 + k, :], XL[:, 11 + k, :], k == 0, k == 1)
            last.then_inc(multiplied, 1)

            def head_sums(side):
                o = bank(7)[0:8, side * T:(side + 1) * T]
                for h in range(8):
                    mm(o, table("middle")[:, HD - h:HD - h + 8], msq[:, h, :], h == 0, False)
                if side == 0:
                    for f in range(4):
                        last = mm(o, table("pair_middle")[:, HD - 2 * f:HD - 2 * f + 8], msq[:, 8 + f, :], False, f == 3)
                else:
                    last = mm(o, table("first_half")[:, 0:8], msq[:, 8, :], False, True)
                last.then_inc(sem("mla_sums"), 1)

            def pair_factors(side, first):
                for f in range(4):
                    last = mm(tiles_of(first, 4)[:, f, :], pick_pair[:, f, :], head_rs[:, side * T:(side + 1) * T])
                last.then_inc(sem("mla_factors"), 1)

            def head_factors(side):
                for h in range(8):
                    last = mm(tiles_of(4, 8)[:, h, :], pick_head[:, h, :], head_rs[:, side * T:(side + 1) * T])
                    if h in (3, 7):
                        last.then_inc(sem("mla_factors"), 1)

            pe.wait_ge(sem("mla_squares"), 1)
            pe.wait_ge(sem("latent_roots"), 1)
            head_sums(0)
            slot, _, g = place(START["mla_kv"] + 1)
            pe.wait_ge(lo_split, g + 1)
            pe.wait_ge(sem("mla_taken"), 3)
            for tt in range(2):
                tok = slice(tt * P, (tt + 1) * P)
                for n in range(2):
                    o = bank((4, 5, 6, 0)[2 * tt + n])
                    if (tt, n) == (1, 1):
                        pe.wait_ge(sem("mla_taken"), 4)
                    for k in range(2):
                        w = slice(k * D + n * 512, k * D + (n + 1) * 512)
                        mm(o, XH[:, 11 + k, tok], ring_hi[:, slot, w], k == 0, False)
                        mm(o, XL[:, 11 + k, tok], ring_hi[:, slot, w], False, False)
                        last = mm(o, XH[:, 11 + k, tok], ring_lo[:, slot, w], False, k == 1)
            last.then_inc(multiplied, 1)
            pe.wait_ge(sem("mla_rope_in"), 1)
            for n in range(2):
                last = mm(bank(1 + n), table("swap"), flat(MQ[:, 8:12])[:, 512 * n:512 * (n + 1)])
            last.then_inc(sem("mla_swapped"), 1)
            mm(bank(3)[:, 0:T], table("swap"), MI[:, 0, :]).then_inc(sem("mla_swapped"), 1)
            pe.wait_ge(sem("mla_squares"), 2)
            head_sums(1)
            pe.wait_ge(sem("mla_taken"), 5)
            pe.wait_ge(sem("mla_rotated"), 1)
            pe.wait_ge(sem("head_rs"), 1)
            pair_factors(0, 0)
            pe.wait_ge(sem("head_rs"), 2)
            head_factors(0)
            pair_factors(1, 2)
            pe.wait_ge(sem("mla_q_scaled"), 1)
            head_factors(1)
            for h in range(8):
                if h in (0, 4):
                    pe.wait_ge(sem("mla_qk"), 1 + h // 4)
                o = bank(h // 4)[:, h % 4 * P:(h % 4 + 1) * P]
                mm(o, MQ[:, h, 0:P], MK[:, h, 0:P], True, False)
                mm(o, MQ[:, 8 + h // 2, 0:P], KRP[:, h, 0:P], False, True)
                o = bank(2 + h // 2)[:, h % 2 * T:(h % 2 + 1) * T]
                mm(o, MQ[:, h, P:T], MK[:, h, :], True, False)
                last = mm(o, MQ[:, 8 + h // 2, P:T], KRP[:, h, :], False, True)
                if h in (3, 7):
                    last.then_inc(sem("mla_scores"), 1)
            for h in range(8):
                if h in (0, 4):
                    pe.wait_ge(sem("mla_probs"), 1 + h // 4)
                if h == 0:
                    pe.wait_ge(sem("mla_max"), 2)
                o = bank(h // 2)[:, h % 2 * T:(h % 2 + 1) * T]
                nc.tensor.transpose(o[:, 0:P], S0[:, h, :], table("identity"))
                nc.tensor.transpose(o[:, P:T], S1[:, h, 0:P], table("identity"))
                last = nc.tensor.transpose(bank(4 + h // 4)[:, h % 4 * P:(h % 4 + 1) * P], S1[:, h, P:T],
                                           table("identity"))
                if h in (3, 7):
                    last.then_inc(sem("mla_turned"), 1)
            for h in range(8):
                if h in (0, 4):
                    pe.wait_ge(sem("mla_turned_taken"), 1 + h // 4)
                o, c = bank(h // 2)[:, h % 2 * T:(h % 2 + 1) * T], slice(h * P, (h + 1) * P)
                mm(o, MV[:, 0, c], PT0[:, h, :], True, False)
                last = mm(o[:, P:T], MV[:, 1, c], PT1[:, h, :], False, True)
                if h % 2:
                    last.then_inc(sem("mla_out"), 1)
            residual_project("mla_out", 8, (0, 2, 4, 6))

            feed_forward("ffn_3")
            per_layer("ple_1", 1)

        @block.scalar
        def _(act):
            taken = [0]
            splits = [0]
            steps = [0]

            def run(out, in_, func=ACT.Copy, **kw):
                return nc.scalar.activation(out, in_, func, **kw)

            def step(ins_):
                steps[0] += 1
                ins_.then_inc(sem("act_step"), 1)
                act.wait_ge(sem("act_step"), steps[0])

            def split_slab(g0, i=0, by=3):
                if g0 >= N_SLABS:
                    return
                slot, use, g = place(g0, i, by)
                act.wait_ge(landed[slot], (use + 1) * 16)
                if g0 >= 3:
                    act.wait_ge(multiplied, g - 2)
                run(ring_hi[:, slot, :], ring_raw[:, slot, :]).then_inc(hi_split, 1)

            def operand(out, in_, **kw):
                splits[0] += 1
                return run(out, in_, **kw).then_inc(sem("operand_hi"), 1)

            def operand_tiles(tiles, src, gain, x0):
                for k in tiles:
                    operand(XH[:, x0 + k, :], src[:, k, :], scale=col(gain[0], gain[1] + k))

            def chunks(stage, gain, x0=0):
                for c in range(4):
                    act.wait_ge(sem("residual_ready"), chunks_until(stage, c + 1))
                    operand_tiles((2 * c, 2 * c + 1), H, gain, x0)
                run(flat(squares), flat(H[:]), ACT.Square).then_inc(sem("norm_squared"), 1)

            norms = [0]

            def norm_root(by_token=False, b=7):
                norms[0] += 1
                w = T + 2 if by_token else T
                act.wait_ge(sem("norm_summed"), norms[0])
                run(root[:, 0:w], bank(b)[:, 0:w], ACT.Sqrt, bias=eps_col(EPS), scale=1.0 / D)\
                    .then_inc(sem("norm_root"), 1)

            def eps_col(value):
                return small[:, {EPS: 32, GN_EPS: 33, 1.0: 34, 0.0: 35}[value]:][:, 0:1]

            ffns = [0]

            def feed_forward(name, conv=False):
                g0, n = START[name], ffns[0]
                up_taken, gate_scaled = sem("up_taken"), sem("gate_scaled")

                def gate(pair, i=0, split=None):
                    if conv:
                        if split is not None:
                            split_slab(split, i, 6)
                        act.wait_ge(sem("conv_done"), pair + 1)
                        run(silu_out, flat(conv_acc), ACT.Silu).then_inc(sem("gate_active"), 1)
                    else:
                        act.wait_ge(gate_scaled, pair + (n * FP + 2))
                        run(silu_out, silu_out, ACT.Silu).then_inc(sem("gate_active"), 1)
                        if split is not None:
                            split_slab(split, i, 6)

                def up(pair, odd, before=None):
                    act.wait_ge(up_taken, pair + (n * FP + 2))
                    if before is not None:
                        act.wait_ge(multiplied, before)
                    run(flat(HH[:, odd]), hidden).then_inc(sem("hidden_hi"), 1)

                split_slab(g0 + 2)
                split_slab(g0 + 3)
                norm_root()
                gate(0)
                up(0, 0)
                with act.Fori(0, FP // 2) as i:
                    split_slab(g0 + 4, i, 6)
                    gate(i * 2 + 1, i, g0 + 5)
                    up(i * 2 + 1, 1, i * 6 + (g0 + 2))
                    split_slab(g0 + 6, i, 6)
                    split_slab(g0 + 7, i, 6)
                    gate(i * 2 + 2, i, g0 + 8)
                    up(i * 2 + 2, 0, i * 6 + (g0 + 5))
                    split_slab(g0 + 9, i, 6)
                ffns[0] += 1

            def down_chunks(name, gain, x0=0):
                split_slab(START[name] + 34)
                chunks(name, gain, x0)

            def inverse_root(out, in_, eps, scale, done):
                step(run(out, in_, ACT.Ln, bias=eps_col(eps), scale=scale))
                run(out, out, ACT.Exp, scale=-0.5).then_inc(sem(done), 1)

            def elsewhere(name, n, ahead=2):
                for j in range(n):
                    split_slab(START[name] + j + ahead)

            def taken_in(name, j, ahead=3):
                if ahead:
                    split_slab(START[name] + j + ahead)
                taken[0] += 1
                act.wait_ge(sem("output_taken"), taken[0])

            x_in = ins["x_t"].rearrange("(k p) t -> p k t", p=P)
            act.dma_start(prm[:], ins["params"]).then_inc(sem("params_landed"), 16)
            for c in range(4):
                act.dma_start(H[:, 2 * c:2 * c + 2, :], x_in[:, 2 * c:2 * c + 2, :]).then_inc(sem(f"x_landed{c}"), 16)
            split_slab(0)
            act.wait_ge(sem("small_ready"), 1)
            act.wait_ge(sem("params_landed"), 16)
            for c in range(4):
                act.wait_ge(sem(f"x_landed{c}"), 16)
                operand_tiles((2 * c, 2 * c + 1), H, ("norm_mix", 0), 0)
            run(flat(squares), flat(H[:]), ACT.Square).then_inc(sem("norm_squared"), 1)
            split_slab(1)

            split_slab(START["conv"] + 2)
            for j in range(6):
                split_slab(START["conv"] + j + 3)
                if j == 0:
                    norm_root(True)
            elsewhere("sb_qk", 3, 3)
            act.wait_ge(sem("conv_y"), 1)
            operand(flat(XH[:, 8:12]), flat(conv_y))
            split_slab(START["sb_qk"] + 6)
            elsewhere("sb_v", 2, 3)
            taken[0] += 12

            def softplus(q):
                act.wait_ge(sem("sb_z"), q + 1)
                z, w = sb_z[q], sb_w[q]
                run(z, bank(0, 3), scale=HD ** -0.5).then_inc(sem("sb_z_taken"), 1)
                act.wait_ge(sem("sb_z_taken"), q + 1)
                step(run(w, z, ACT.Abs))
                step(run(w, w, ACT.Exp, scale=-1.0))
                run(w, w, ACT.Ln, bias=eps_col(1.0)).then_inc(sem("sb_softplus"), 1)

            def attention(q):
                act.wait_ge(sem("sb_logw"), q + 1)
                run(sb_w[q], sb_w[q], ACT.Exp).then_inc(sem("sb_exp"), 1)

            def shift(j):
                taken[0] += 1
                act.wait_ge(sem("output_taken"), taken[0])
                for m in range(2):
                    t = 2 * j + m
                    last_ = run(rp[:, t, :], shift_in[j % 2][:, m, :], scale=one_minus_mu[:, t:t + 1])
                last_.then_inc(sem("rk_scaled"), 1)

            softplus(0)
            split_slab(START["rwkv"] + 3)
            softplus(1)
            act.wait_ge(sem("operand_lo"), KT + 1)
            shift(0)
            split_slab(START["rwkv"] + 4)
            attention(0)
            shift(1)
            split_slab(START["rwkv"] + 5)
            attention(1)
            for j in range(2, 7):
                shift(j)
                if j < 6:
                    split_slab(START["rwkv"] + j + 4)
                if j == 4:
                    act.wait_ge(sem("sb_y"), 1)
                    operand(flat(XH[:, 12:16]), bank(0, 2))
            def activate_gates(n):
                taken[0] += 1
                act.wait_ge(sem("output_taken"), taken[0])
                for m in range(2):
                    g_ = gate_stage[n % 2][:, m, :]
                    last_ = run(g_, g_, ACT.Sigmoid, bias=col("gate_b", 2 * n + m))
                last_.then_inc(sem("gates_active"), 1)

            act.wait_ge(sem("rk_shifted"), 7)
            run(LORA[0:HD, 0, :], LORA[0:HD, 0, :], ACT.Tanh)
            run(LORA[:, 1, :], LORA[:, 1, :], ACT.Sigmoid).then_inc(sem("rk_lora_in"), 1)
            activate_gates(0)
            split_slab(START["gates"] + 3)
            act.wait_ge(sem("rk_lora_out"), 1)
            for f in range(4):
                run(LW[:, f, :], tiles_of(0, 4)[:, f, :], ACT.Sigmoid, bias=col("w0", f))
                run(A_[:, f, :], tiles_of(2, 4)[:, f, :], ACT.Sigmoid, bias=col("a0", f))
            run(flat(G_), bank(4, 2)).then_inc(sem("rk_gates"), 1)
            activate_gates(1)
            act.wait_ge(sem("rk_guarded"), 1)
            inverse_root(flat(TM), flat(TM), 0.0, 1.0, "rk_kk_root")
            act.wait_ge(sem("rk_decays"), 1)
            run(flat(EP), flat(LC), ACT.Exp)
            run(flat(LW), flat(LW), ACT.Exp)
            step(run(flat(LC), flat(LC), ACT.Exp, scale=-1.0))
            run(chunk_decay, EP[:, :, CH - 1:T:CH]).then_inc(sem("rk_exps"), 1)
            split_slab(START["gates"] + 4)
            activate_gates(2)
            split_slab(START["gates"] + 5)
            for tt in range(2):
                act.wait_ge(sem("rk_turned"), tt + 1)
                if tt == 0:
                    act.wait_ge(sem("rk_prep"), 1)
                run(Vt[:, 0, :], bank(0))
                run(ZP[:, :, 0:HD], bank(1).rearrange("p (h k) -> p h k", k=HD)).then_inc(sem("rk_turned_act"), 1)
                act.wait_ge(sem("rk_p"), tt + 1)
                run(ZP[:, :, HD:P], bank(0).rearrange("p (h k) -> p h k", k=HD)).then_inc(sem("rk_p_taken"), 1)
                for li in range(1, 6):
                    for q in range(2):
                        act.wait_ge(sem("rk_f"), (tt * 6 + li) * 2 + q + 1)
                        run(flat(Fm[:, 4 * q:4 * q + 4]), bank(1 + q)).then_inc(sem("rk_f_taken"), 1)
                    n = gate_slab_at(tt, li - 1)
                    if n is not None:
                        activate_gates(n)
                        split_slab(START["gates"] + n + 3)
                n = gate_slab_at(tt, 5)
                if n is not None:
                    activate_gates(n)
                    split_slab(START["gates"] + n + 3)
                act.wait_ge(sem("rk_wu"), tt + 1)
                for q in range(2):
                    last = run(flat(Xb[:, 4 * q:4 * q + 4]), bank(3 + q))
                last.then_inc(sem("rk_wu_taken"), 1)
                act.wait_ge(sem("rk_inner"), tt + 1)
                run(KK[:, :, tt * P:(tt + 1) * P], bank(3).rearrange("p (f t) -> p f t", f=4))\
                    .then_inc(sem("rk_inner_copied"), 1)
                act.wait_ge(sem("rk_transition"), tt + 1)
                run(flat(MT), bank(0)[:, 0:4 * HD]).then_inc(sem("rk_transition_taken"), 1)
            split_slab(START["branch"] + 3)
            act.wait_ge(sem("mem_landed"), 16)
            run(flat(squares), flat(mem), ACT.Square).then_inc(sem("norm_squared"), 1)
            act.wait_ge(sem("rk_moments"), 2)
            inverse_root(flat(TM), bank(2, 2), GN_EPS, 1.0 / HD, "rk_root")
            act.wait_ge(sem("rk_y_out"), 1)
            operand(flat(XH[:, 16:20]), flat(KK))
            split_slab(START["branch"] + 4)
            split_slab(START["branch"] + 5)
            norm_root(b=3)
            split_slab(START["branch"] + 6)
            split_slab(START["branch"] + 7)
            for i, (a, b) in enumerate(((0, 4), (4, 6), (6, 8))):
                act.wait_ge(sem("branch_taken"), 5 + i)
                operand(flat(XH[:, a:b]), flat(merged[:, a:b]))
            elsewhere("mix_out", 2)
            act.wait_ge(sem("mem_scaled"), 1)
            operand_tiles(range(KT), squares, ("norm_mem", 0), 8)
            elsewhere("mix_out", 2, 4)

            act.wait_ge(sem("operand_lo"), splits[0])
            act.wait_ge(multiplied, START["mix_out"] + 4)
            chunks("mix_out", ("norm_ca", 0))
            elsewhere("ca_k", 4)
            elsewhere("ca_v", 4)
            taken[0] += 8
            norm_root()
            elsewhere("ca_q", 4)
            taken[0] += 4
            for tt in range(2):
                act.wait_ge(sem("ca_max"), tt + 1)
                for i in range(4 * tt, 4 * tt + 4):
                    last = run(probs[:, i, :], tiles_of(0, 8)[:, i, :], ACT.Exp, scale=1.0 / 16,
                               bias=small[:, 8 + i:9 + i], accum_out=small[:, 16 + i:17 + i])
                last.then_inc(sem("ca_exp"), 1)
            act.wait_ge(sem("ca_turned"), 1)
            run(flat(probs_t), bank(4, 4)).then_inc(sem("ca_turned_taken"), 1)
            for h in range(4):
                act.wait_ge(sem("ca_out"), h + 1)
                operand(flat(XH[:, 8 + 2 * h:10 + 2 * h]), bank(h))
            elsewhere("ca_o", 4)

            chunks("ca_o", ("norm_ffn", 0))
            feed_forward("ffn_c", conv=True)
            split_slab(START["ffn_c"] + 34)
            for c in range(4):
                act.wait_ge(sem("residual_ready"), chunks_until("ffn_c", c + 1))
                run(flat(squares[:, 2 * c:2 * c + 2]), flat(H[:, 2 * c:2 * c + 2]), ACT.Square)\
                    .then_inc(sem("chunk_squared"), 1)
            norm_root()
            chunks("final", ("norm_gains", 0))
            feed_forward("ffn_0")
            down_chunks("ffn_0", ("norm_gains", 8))

            funcs = [ACT.Gelu_apprx_tanh, ACT.Copy, ACT.Sigmoid, ACT.Silu]
            split_slab(START["even_in"] + 2)
            split_slab(START["even_in"] + 3)
            norm_root(True)
            act.wait_ge(sem("av_sums"), 1)
            run(small[:, 44:48], small[:, 40:44], ACT.Exp).then_inc(sem("av_root"), 1)
            for j in range(8):
                taken_in("even_in", j, 3 if j else None)
                e = flat(ev[:, 2 * j:2 * j + 2])
                if funcs[j // 2] != ACT.Copy:
                    last = run(e, e, funcs[j // 2])
                if j in (5, 7):
                    last.then_inc(sem("even_active"), 1)
            act.wait_ge(sem("gl_forget"), 1)
            run(flat(BF), flat(BF), ACT.Ln, bias=eps_col(0.0)).then_inc(sem("gl_log"), 1)
            for j in range(2):
                taken_in("even_v", j, 3)
                v_ = AV[:, :, j * T:(j + 1) * T]
                last = run(v_, v_, ACT.Gelu_apprx_tanh)
            last.then_inc(sem("even_active"), 1)
            taken_in("even_v", 2, 3)
            act.wait_ge(sem("av_sums"), 2)
            run(small[:, 16:32], small[:, 0:16], ACT.Sqrt, bias=eps_col(EPS), scale=1.0 / HD).then_inc(sem("av_root"), 1)
            taken_in("even_v", 3, 3)
            for li in range(1, 9):
                act.wait_ge(sem("gl_diff"), li)
                d = flat(DIF[li % 2])
                step(run(d, d, ACT.Abs))
                run(d, d, ACT.Exp, scale=-1.0).then_inc(sem("gl_exp"), 1)
                if li == 1:
                    act.wait_ge(sem("mixed_gated"), 1)
                    operand(flat(XH[:, 8:12]), flat(AU))
            for h in range(2):
                act.wait_ge(sem("gl_out"), h + 1)
                run(flat(BC[:, 2 * h:2 * h + 2]), bank(6 + h)).then_inc(sem("gl_copied"), 1)
                act.wait_ge(sem("gl_copied"), h + 1)
                run(flat(KB[:, 2 * h:2 * h + 2]), flat(BC[:, 2 * h:2 * h + 2]), ACT.Square)\
                    .then_inc(sem("gl_squares"), 1)
            roots = [flat(DIF[0][:, 2 * h:2 * h + 2]) for h in range(2)]
            for h in range(2):
                act.wait_ge(sem("gl_norms"), h + 1)
                last = run(roots[h], bank(2 + h), ACT.Ln, bias=eps_col(EPS), scale=1.0 / P)
            step(last)
            for h in range(2):
                run(roots[h], roots[h], ACT.Exp, scale=-0.5).then_inc(sem("gl_root"), 1)
            for h in range(2):
                act.wait_ge(sem("gl_y"), h + 1)
                operand(flat(XH[:, 12 + 2 * h:14 + 2 * h]), flat(BC[:, 2 * h:2 * h + 2]))
            for j in range(1, 4):
                split_slab(START["even_out"] + j + 2)

            def per_layer(name, n):
                g0 = START[name]
                split_slab(g0 + 2)
                act.wait_ge(multiplied, g0 + 1)
                run(flat(ple_p[:, 0:6]), bank(0, 3))
                run(flat(ple_p[:, 6:8]), bank(7)).then_inc(sem("ple_copied"), 1)
                split_slab(g0 + 3)
                norm_root()
                def gained(c):
                    for k in (2 * c, 2 * c + 1):
                        last_ = run(ple_add[:, k, :], ple_p[:, k, :], scale=col("norm_gains", (5 * n + 4) * 8 + k))
                    last_.then_inc(sem("ple_gained"), 1)

                for c in range(4):
                    if c < 2:
                        split_slab(g0 + 4 + c)
                    act.wait_ge(sem("ple_gate_scaled"), 4 * n + c + 1)
                    s_ = slice(2 * c, 2 * c + 2)
                    run(flat(ple_g[:, s_]), flat(ple_g[:, s_]), ACT.Sigmoid).then_inc(sem("ple_gated"), 1)
                    act.wait_ge(sem("ple_product"), 4 * n + c + 1)
                    run(flat(squares[:, s_]), flat(ple_p[:, s_]), ACT.Square).then_inc(sem("chunk_squared"), 1)
                    if c < 3:
                        gained(c)
                split_slab(g0 + 6)
                act.wait_ge(sem("ple_summed"), n + 1)
                run(root[:, 0:T], bank(0)[:, 0:T], ACT.Sqrt, bias=eps_col(EPS), scale=1.0 / D)\
                    .then_inc(sem("ple_root"), 1)
                gained(3)

            def embedding(n):
                act.wait_ge(sem("ple_landed"), 16 * (n + 1))
                operand(flat(XH[:, 8:10]), flat(ple_in))

            chunks("even_out", ("norm_gains", 16))
            embedding(0)
            feed_forward("ffn_1")
            down_chunks("ffn_1", ("norm_gains", 24))
            per_layer("ple_0", 0)
            chunks("ple_0", ("norm_gains", 40))
            feed_forward("ffn_2")
            down_chunks("ffn_2", ("norm_gains", 48))

            split_slab(START["mla_in"] + 2)
            split_slab(START["mla_in"] + 3)
            norm_root()
            taken_in("mla_in", 0, None)
            operand_tiles((0, 1), MI, ("q_a_norm", 0), 8)
            taken_in("mla_in", 1, None)
            operand_tiles((2,), MI, ("q_a_norm", 0), 8)
            split_slab(START["mla_in"] + 4)
            taken_in("mla_in", 2, None)
            operand_tiles((0, 1), MI[:, 3:5], ("kv_a_norm", 0), 11)
            split_slab(START["mla_in"] + 5)
            run(flat(squares[:, 0:5]), flat(MI[:, 0:5]), ACT.Square).then_inc(sem("latent_squared"), 1)
            act.wait_ge(sem("latent_summed"), 1)
            run(latent_rs[:, 0, :], bank(7)[:, 0:T], ACT.Sqrt, bias=eps_col(EPS), scale=1.0 / 384)
            run(latent_rs[:, 1, :], bank(7)[:, T:2 * T], ACT.Sqrt, bias=eps_col(EPS), scale=1.0 / 256)
            run(small[:, 36:38], bank(6)[:, 0:2], ACT.Sqrt, bias=eps_col(EPS), scale=1.0 / 256)\
                .then_inc(sem("latent_roots"), 1)
            split_slab(START["mla_q"] + 3)
            act.wait_ge(sem("angles"), 1)
            run(flat(sines), flat(sines), ACT.Sin, bias=eps_col(0.0))
            run(flat(cosines), flat(cosines), ACT.Sin, bias=eps_col(0.0)).then_inc(sem("angles_done"), 1)
            for j in range(3):
                act.wait_ge(sem("mla_taken"), j + 1)
                last = run(flat(msq[:, 4 * j:4 * j + 4]), flat(MQ[:, 4 * j:4 * j + 4]), ACT.Square)
                if j == 0:
                    split_slab(START["mla_q"] + 4)
            last.then_inc(sem("mla_squares"), 1)
            split_slab(START["mla_kv"] + 2)
            act.wait_ge(sem("mla_sums"), 1)
            run(head_rs[:, 0:T], bank(7)[0:8, 0:T], ACT.Sqrt, bias=small[0:8, 32:33], scale=1.0 / 192)\
                .then_inc(sem("head_roots"), 1)
            act.wait_ge(sem("mla_taken"), 4)
            run(flat(msq[:, 0:8]), flat(MK), ACT.Square)
            run(msq[:, 8, :], MI[:, 5, :], ACT.Square).then_inc(sem("mla_squares"), 1)
            act.wait_ge(multiplied, START["mla_kv"] + 2)
            for n, b in enumerate((4, 5, 6, 0)):
                tt, half = divmod(n, 2)
                last = run(MV[:, tt, half * 512:(half + 1) * 512], bank(b), scale=small[:, 38 + tt:39 + tt])
            last.then_inc(sem("mla_taken"), 1)
            act.wait_ge(sem("mla_sums"), 2)
            run(head_rs[:, T:2 * T], bank(7)[0:8, T:2 * T], ACT.Sqrt, bias=small[0:8, 32:33], scale=1.0 / 192)\
                .then_inc(sem("head_roots"), 1)
            split_slab(START["mla_kv"] + 3)
            for e in range(2):
                act.wait_ge(sem("mla_max"), e + 1)
                for h in range(4 * e, 4 * e + 4):
                    run(S0[:, h, :], S0[:, h, :], ACT.Exp, scale=192 ** -0.5, bias=small[:, h:h + 1],
                        accum_out=small[:, 16 + h:17 + h])
                    last = run(S1[:, h, :], S1[:, h, :], ACT.Exp, scale=192 ** -0.5, bias=small[:, 8 + h:9 + h],
                               accum_out=small[:, 24 + h:25 + h])
                last.then_inc(sem("mla_exp"), 1)
            for e in range(2):
                act.wait_ge(sem("mla_turned"), e + 1)
                run(flat(PT0[:, 4 * e:4 * e + 4]), bank(2 * e, 2))
                run(flat(PT1[:, 4 * e:4 * e + 4]), bank(4 + e)).then_inc(sem("mla_turned_taken"), 1)
            for f in range(4):
                act.wait_ge(sem("mla_out"), f + 1)
                operand(flat(XH[:, 8 + 2 * f:10 + 2 * f]), bank(f))
            elsewhere("mla_out", 4)

            chunks("mla_out", ("norm_gains", 56))
            embedding(1)
            feed_forward("ffn_3")
            down_chunks("ffn_3", ("norm_gains", 64))
            per_layer("ple_1", 1)

        @block.vector
        def _(dve):
            v = nc.vector
            taken = [0]
            splits = [0]
            steps = [0]

            def step(ins_):
                steps[0] += 1
                ins_.then_inc(sem("dve_step"), 1)
                dve.wait_ge(sem("dve_step"), steps[0])

            def tt_(out, a, b, op):
                return v.tensor_tensor(out, a, b, op)

            def mul(out, a, b):
                return v.tensor_tensor(out, a, b, ALU.mult)

            def over(ap, n):
                return ap.unsqueeze(1).to_broadcast([P, n, ap.shape[-1]])

            def split_slab(g0, i=0, by=3):
                if g0 >= N_SLABS:
                    return
                slot, _, g = place(g0, i, by)
                dve.wait_ge(hi_split, g + 1)
                tt_(ring_lo[:, slot, :], ring_raw[:, slot, :], ring_hi[:, slot, :].bitcast(F32), ALU.subtract)\
                    .then_inc(lo_split, 1)

            def take(name, j, out, scaled=True):
                dve.wait_ge(multiplied, START[name] + j + 1)
                b = taken[0] % 3
                taken[0] += 1
                last_ = mul(out, tiles_of(b, 2), over(inv[:, 0:T], 2)) if scaled else v.tensor_copy(out, tiles_of(b, 2))
                last_.then_inc(sem("output_taken"), 1)

            def take_by_token(name, j, out):
                dve.wait_ge(multiplied, START[name] + j + 1)
                b = taken[0] % 3
                taken[0] += 1
                for tt in range(2):
                    last_ = v.tensor_scalar(out[:, tt, :], tiles_of(b, 2)[:, tt, :], inv[:, T + tt:T + tt + 1], None,
                                            ALU.mult)
                last_.then_inc(sem("output_taken"), 1)

            def operand(out, in_, hi):
                splits[0] += 1
                dve.wait_ge(sem("operand_hi"), splits[0])
                return tt_(out, in_, hi.bitcast(F32), ALU.subtract).then_inc(sem("operand_lo"), 1)

            norms = [0]

            def norm_factor(by_token=False):
                norms[0] += 1
                w = T + 2 if by_token else T
                dve.wait_ge(sem("norm_root"), norms[0])
                step(v.reciprocal(inv[:, 0:w], root[:, 0:w]))

            def operand_tiles(tiles, src, gain, x0):
                for k in tiles:
                    splits[0] += 1
                    dve.wait_ge(sem("operand_hi"), splits[0])
                    v.scalar_tensor_tensor(out=XL[:, x0 + k, :], in0=src[:, k, :], scalar=col(gain[0], gain[1] + k),
                                           in1=XH[:, x0 + k, :].bitcast(F32), op0=ALU.mult, op1=ALU.subtract)\
                     .then_inc(sem("operand_lo"), 1)

            def chunk(c):
                return flat(H[:, 2 * c:2 * c + 2])

            def chunks(add, stage, gain, behind=1):
                for c in range(4):
                    add(c)
                    if c >= behind:
                        lower(c - behind, stage, gain)
                for c in range(4 - behind, 4):
                    lower(c, stage, gain)

            def lower(c, stage, gain):
                if gain is not None:
                    dve.wait_ge(sem("residual_ready"), chunks_until(stage, c + 1))
                    operand_tiles((2 * c, 2 * c + 1), H, gain, 0)

            def residual(name, gain, behind=1, ahead=2, before={}):
                def add(c):
                    if c in before:
                        before[c]()
                    if ahead == 2 or c:
                        split_slab(START[name] + c + 2)
                    dve.wait_ge(multiplied, START[name] + c + 1)
                    tt_(chunk(c), chunk(c), bank((6, 7, 4, 5)[c]), ALU.add).then_inc(sem("residual_ready"), 1)
                chunks(add, name, gain, behind)

            def down(name, gain, scale=0.5):
                def add(c):
                    if c < 3:
                        dve.wait_ge(sem("down_bank"), 3 * (ffns[0] - 1) + c + 1)
                    else:
                        dve.wait_ge(multiplied, START[name] + 33)
                    v.scalar_tensor_tensor(out=chunk(c), in0=bank(3 + c), scalar=scale, in1=chunk(c), op0=ALU.mult,
                                           op1=ALU.add).then_inc(sem("residual_ready"), 1)
                chunks(add, name, gain)
                split_slab(START[name] + 34)

            ffns = [0]

            def feed_forward(name, conv=False):
                g0, n = START[name], ffns[0]
                gate_scaled, gate_active, up_taken = sem("gate_scaled"), sem("gate_active"), sem("up_taken")

                def factor():
                    return over(inv[:, 0:T], 2)

                def tiled(x):
                    return x.rearrange("p (n t) -> p n t", t=T)

                def gate(at, i, pair, b, split=None):
                    dve.wait_ge(multiplied, place(at, i, 6)[2] + 1)
                    dve.wait_ge(up_taken, pair + (n * FP + 1))
                    if conv:
                        mul(conv_x[0], tiles_of(b, 2), factor()).then_inc(gate_scaled, 1)
                    else:
                        mul(tiled(silu_out), tiles_of(b, 2), factor()).then_inc(gate_scaled, 1)
                    if split is not None:
                        split_slab(split, i, 6)
                    if conv:
                        dve.wait_ge(gate_scaled, pair + 2)
                        taps(conv_acc, conv_x[0], pair * 2, pair * 11, sem("conv_done"))
                    else:
                        dve.wait_ge(gate_active, pair + (n * FP + 1))
                        mul(tiled(silu_out), tiled(silu_out), factor()).then_inc(sem("gate_rescaled"), 1)

                def taps(acc, x, tile_, before, done):
                    for m in range(2):
                        w2 = prm[:, bass.ds(tile_ + (m + COL["ffn_conv_w"] + 2 * 4 * FP), 1)]
                        b = prm[:, bass.ds(tile_ + (m + COL["ffn_conv_b"]), 1)]
                        v.tensor_scalar(acc[:, m, :], x[:, m, :], w2, b, ALU.mult, ALU.add)\
                         .then_inc(sem("conv_tap"), 1)
                    dve.wait_ge(sem("conv_tap"), before + 2)
                    for m in range(2):
                        w1 = prm[:, bass.ds(tile_ + (m + COL["ffn_conv_w"] + 4 * FP), 1)]
                        v.scalar_tensor_tensor(out=acc[:, m, 1:T], in0=x[:, m, 0:T - 1], scalar=w1,
                                               in1=acc[:, m, 1:T], op0=ALU.mult, op1=ALU.add)\
                         .then_inc(sem("conv_tap"), 1)
                    dve.wait_ge(sem("conv_tap"), before + 4)
                    for m in range(2):
                        w0 = prm[:, bass.ds(tile_ + (m + COL["ffn_conv_w"]), 1)]
                        v.scalar_tensor_tensor(out=acc[:, m, 2:T], in0=x[:, m, 0:T - 2], scalar=w0,
                                               in1=acc[:, m, 2:T], op0=ALU.mult, op1=ALU.add)\
                         .then_inc(done if m == 1 else sem("conv_tap"), 1)

                def up(at, i, pair, odd, b):
                    dve.wait_ge(multiplied, place(at, i, 6)[2] + 1)
                    dve.wait_ge(sem("hidden_lo"), pair + n * FP)
                    if conv:
                        mul(conv_x[1], tiles_of(b, 2), factor()).then_inc(sem("conv_up_scaled"), 1)
                        dve.wait_ge(sem("conv_up_scaled"), pair + 1)
                        taps(conv_acc2, conv_x[1], pair * 2 + 2 * FP, pair * 11 + 5, sem("conv_tap"))
                        dve.wait_ge(sem("conv_tap"), pair * 11 + 11)
                        dve.wait_ge(gate_active, pair + 1)
                        mul(hidden, silu_out, flat(conv_acc2)).then_inc(up_taken, 1)
                    else:
                        dve.wait_ge(sem("gate_rescaled"), pair + ((n - 1) * FP + 1))
                        mul(hidden, silu_out, bank(b)).then_inc(up_taken, 1)
                    dve.wait_ge(sem("hidden_hi"), pair + (n * FP + 1))
                    tt_(flat(HL[:, odd]), hidden, flat(HH[:, odd]).bitcast(F32), ALU.subtract)\
                        .then_inc(sem("hidden_lo"), 1)

                split_slab(g0 + 2)
                split_slab(g0 + 3)
                norm_factor()
                gate(g0, 0, 0, 0)
                up(g0 + 1, 0, 0, 0, 1)
                with dve.Fori(0, FP // 2) as i:
                    split_slab(g0 + 4, i, 6)
                    gate(g0 + 2, i, i * 2 + 1, 2, g0 + 5)
                    up(g0 + 3, i, i * 2 + 1, 1, 7)
                    split_slab(g0 + 6, i, 6)
                    split_slab(g0 + 7, i, 6)
                    gate(g0 + 5, i, i * 2 + 2, 0, g0 + 8)
                    up(g0 + 6, i, i * 2 + 2, 0, 1)
                    split_slab(g0 + 9, i, 6)
                ffns[0] += 1

            for value, c in ((EPS, 32), (GN_EPS, 33), (1.0, 34), (0.0, 35)):
                last = v.memset(small[:, c:c + 1], value)
            last.then_inc(sem("small_ready"), 1)
            for c, free in ((59, "gate_scaled"), (58, "up_taken")):
                v.memset(small[:, c:c + 1], 0.0).then_inc(sem(free), 1)
            split_slab(0)
            dve.wait_ge(sem("params_landed"), 16)
            step(v.tensor_scalar(one_minus_mu[:], col("mu", 0, 14), -1.0, 1.0, ALU.mult, ALU.add))
            for c in range(4):
                operand_tiles((2 * c, 2 * c + 1), H, ("norm_mix", 0), 0)
            split_slab(1)

            split_slab(START["conv"] + 2)
            split_slab(START["conv"] + 3)
            norm_factor(True)
            for j in range(6):
                take("conv", j, conv_in[:, 2 * j:2 * j + 2])
                if j:
                    split_slab(START["conv"] + j + 3)
            def conv_taps(back):
                for f in range(4):
                    last_ = v.scalar_tensor_tensor(out=conv_y[:, f, back:T], in0=conv_u[:, f, 0:T - back],
                                                   scalar=col("conv_w", 4 * (2 - back) + f), in1=conv_y[:, f, back:T],
                                                   op0=ALU.mult, op1=ALU.add)
                step(last_)

            for j in range(4):
                take("sb_qk", j, sbq[:, 2 * j:2 * j + 2])
                split_slab(START["sb_qk"] + j + 3)
                if j == 0:
                    dve.wait_ge(sem("output_taken"), 6)
                    step(mul(conv_u, conv_in[:, 4:8], conv_in[:, 8:12]))
                    for f in range(4):
                        last = v.tensor_scalar(conv_y[:, f, :], conv_u[:, f, :], col("conv_w", 8 + f), None, ALU.mult)
                    step(last)
                elif j == 1:
                    conv_taps(1)
                elif j == 2:
                    conv_taps(2)
                    mul(conv_y, conv_y, conv_in[:, 0:4]).then_inc(sem("conv_y"), 1)
                    dve.wait_ge(sem("conv_y"), 1)
                else:
                    operand(flat(XL[:, 8:12]), flat(conv_y), flat(XH[:, 8:12]))
            for j in range(2):
                take_by_token("sb_v", j, sbv[:, :, j * T:(j + 1) * T])
                split_slab(START["sb_v"] + j + 3)

            def masked(q, buf):
                for b in (0, 2):
                    blk = buf[:, b * 512:(b + 1) * 512].rearrange("p (f t) -> p f t", f=4)
                    last_ = mul(blk, blk, per_head("before"))
                return last_

            def logs(q):
                dve.wait_ge(sem("sb_softplus"), q + 1)
                z, w = sb_z[q], sb_w[q]
                step(v.scalar_tensor_tensor(out=w, in0=z, scalar=0.0, in1=w, op0=ALU.min, op1=ALU.subtract))
                step(tt_(z, w, z, ALU.subtract))
                masked(q, z).then_inc(sem("sb_log"), 1)

            def attention(q):
                dve.wait_ge(sem("sb_suffix"), q + 1)
                tt_(sb_w[q], sb_w[q], bank(3, 3), ALU.add).then_inc(sem("sb_logw"), 1)
                dve.wait_ge(sem("sb_exp"), q + 1)
                masked(q, sb_w[q]).then_inc(sem("sb_att"), 1)

            def take_rwkv(j):
                dve.wait_ge(multiplied, START["rwkv"] + j + 1)
                if j >= 2:
                    dve.wait_ge(sem("rk_shifted"), j - 1)
                taken[0] += 1
                mul(shift_in[j % 2], tiles_of(6 + j % 2, 2), over(inv[:, 0:T], 2)).then_inc(sem("output_taken"), 1)

            def shift(j):
                dve.wait_ge(sem("rk_scaled"), j + 1)
                for m in range(2):
                    t = 2 * j + m
                    last_ = v.scalar_tensor_tensor(out=rp[:, t, 1:T], in0=shift_in[j % 2][:, m, 0:T - 1],
                                                   scalar=col("mu", t), in1=rp[:, t, 1:T], op0=ALU.mult, op1=ALU.add)
                last_.then_inc(sem("rk_shifted"), 1)

            take_rwkv(0)
            logs(0)
            split_slab(START["rwkv"] + 3)
            take_rwkv(1)
            logs(1)
            attention(0)
            shift(0)
            split_slab(START["rwkv"] + 4)
            take_rwkv(2)
            attention(1)
            shift(1)
            split_slab(START["rwkv"] + 5)
            for j in range(3, 7):
                take_rwkv(j)
                shift(j - 1)
                split_slab(START["rwkv"] + j + 3)
                if j == 5:
                    dve.wait_ge(sem("sb_y"), 1)
                    operand(flat(XL[:, 12:16]), bank(0, 2), flat(XH[:, 12:16]))
            shift(6)
            dve.wait_ge(sem("rk_shifted"), 7)
            for f in range(4):
                last = v.tensor_scalar(KK[:, f, :], K_[:, f, :], col("k_k", f), None, ALU.mult)
            step(last)
            mul(TM, KK, KK).then_inc(sem("rk_squares"), 1)

            def take_gates(n):
                dve.wait_ge(multiplied, START["gates"] + n + 1)
                if n >= 2:
                    dve.wait_ge(sem("gates_moved"), 16 * (n - 1))
                taken[0] += 1
                mul(gate_stage[n % 2], tiles_of(gate_bank(n), 2), over(inv[:, 0:T], 2))\
                    .then_inc(sem("output_taken"), 1)

            take_gates(0)
            split_slab(START["gates"] + 3)
            dve.wait_ge(sem("rk_lora_out"), 1)
            take_gates(1)
            dve.wait_ge(sem("rk_norms"), 1)
            v.tensor_scalar(flat(TM), bank(6, 2), 1e-24, None, ALU.max).then_inc(sem("rk_guarded"), 1)
            dve.wait_ge(sem("rk_gates"), 1)
            step(v.tensor_scalar(flat(LW), flat(LW), -DECAY_SCALE, None, ALU.mult))
            for f in range(4):
                for c in range(4):
                    t = slice(c * CH, (c + 1) * CH)
                    last = v.tensor_tensor_scan(LC[:, f, t], table("ones")[:, 0:CH], LW[:, f, t], 0.0, ALU.mult, ALU.add)
            step(last)
            tt_(flat(LW), flat(LC), flat(LW), ALU.subtract).then_inc(sem("rk_decays"), 1)
            dve.wait_ge(sem("rk_kk_root"), 1)
            step(mul(KK, KK, TM))
            for f in range(4):
                last = v.tensor_scalar(TM[:, f, :], A_[:, f, :], -1.0, col("k_a", f), ALU.add, ALU.mult)
            step(last)
            step(v.scalar_tensor_tensor(out=flat(K_), in0=flat(TM), scalar=1.0, in1=flat(K_), op0=ALU.add, op1=ALU.mult))
            step(v.scalar_tensor_tensor(out=flat(A_), in0=flat(KK), scalar=-1.0, in1=flat(A_), op0=ALU.mult,
                                        op1=ALU.mult))
            for f in range(4):
                last = v.scalar_tensor_tensor(out=BN[:, f, :], in0=R_[:, f, :], scalar=col("r_k", f), in1=K_[:, f, :],
                                              op0=ALU.mult, op1=ALU.mult)
            last.then_inc(sem("rk_bonus_in"), 1)
            dve.wait_ge(sem("rk_exps"), 1)
            dve.wait_ge(sem("rk_bonus_in"), 1)
            mul(R_, R_, EP)
            mul(KK, KK, LW)
            mul(K_, K_, LC)
            step(mul(A_, A_, LC))
            dve.wait_ge(sem("rk_bonus_sums"), 1)
            take_gates(2)
            mul(flat(BN), flat(V_), bank(6, 2)).then_inc(sem("rk_prep"), 1)
            split_slab(START["gates"] + 4)
            for tt in range(2):
                tok = slice(tt * P, (tt + 1) * P)
                dve.wait_ge(sem("rk_turned"), tt + 1)
                v.tensor_copy(Kt[:, 0, :], bank(2))
                v.tensor_copy(Bt[:, 0, :], bank(3))
                dve.wait_ge(sem("rk_pairs"), tt + 1)
                for q in range(2):
                    e = slice(4 * q, 4 * q + 4)
                    mul(Fm[:, e, :], bank(4 + q).rearrange("p (f t) -> p f t", f=4), per_head("before_chunk"))
                    last = mul(Xm[:, e, :], bank(6 + q).rearrange("p (f t) -> p f t", f=4), per_head("before_chunk"))
                last.then_inc(sem("rk_masked"), 1)
                if tt == 0:
                    split_slab(START["gates"] + 5)
                dve.wait_ge(sem("rk_masked"), tt + 1)
                for li in range(6):
                    for q in range(2):
                        n = (tt * 6 + li) * 2 + q
                        e = slice(4 * q, 4 * q + 4)
                        if li:
                            dve.wait_ge(sem("rk_f"), n - 1)
                        if li == 1:
                            dve.wait_ge(sem("rk_y"), n - 1)
                        mul(Xb[:, e, :], Xm[:, e, :], per_head(f"level{LEVELS[li]}")).then_inc(sem("rk_x"), 1)
                    if gate_slab_at(tt, li - 2) is not None:
                        split_slab(START["gates"] + gate_slab_at(tt, li - 2) + 3)
                    if gate_slab_at(tt, li - 1) is not None:
                        take_gates(gate_slab_at(tt, li - 1))
                    for q in range(2):
                        n = (tt * 6 + li) * 2 + q
                        e = slice(4 * q, 4 * q + 4)
                        if li == 0:
                            dve.wait_ge(sem("rk_x"), n + 1)
                            tt_(Ym[:, e, :], per_head("identity"), Xb[:, e, :], ALU.add)
                            dve.wait_ge(sem("rk_f"), n + 1)
                            tt_(Yt[:, e, :], per_head("identity"), bank(1 + q).rearrange("p (f t) -> p f t", f=4),
                                ALU.add).then_inc(sem("rk_y"), 1)
                            continue
                        dve.wait_ge(sem("rk_dy"), n - 1 - 2 * tt)
                        dve.wait_ge(sem("rk_y"), n - 1)
                        if li < 5:
                            tt_(Yt[:, e, :], Yt[:, e, :], bank(5 + q).rearrange("p (f t) -> p f t", f=4), ALU.add)
                        tt_(Ym[:, e, :], Ym[:, e, :], bank(3 + q).rearrange("p (f t) -> p f t", f=4), ALU.add)\
                            .then_inc(sem("rk_y"), 1)
                split_slab(START["gates"] + gate_slab_at(tt, 4) + 3)
                if gate_slab_at(tt, 5) is not None:
                    take_gates(gate_slab_at(tt, 5))
                dve.wait_ge(sem("rk_out_pairs"), tt + 1)
                for q in range(2):
                    e = slice(4 * q, 4 * q + 4)
                    mul(Yt[:, e, :], bank(5 + q).rearrange("p (f t) -> p f t", f=4), per_head("upto_chunk"))
                    last = mul(Fm[:, e, :], bank(1 + q).rearrange("p (f t) -> p f t", f=4), per_head("upto_chunk"))
                last.then_inc(sem("rk_out_masked"), 1)
                if gate_slab_at(tt, 5) is not None:
                    split_slab(START["gates"] + gate_slab_at(tt, 5) + 3)
                if tt:
                    for f in range(4):
                        last = v.tensor_scalar(BN[:, f, :], BN[:, f, :], col("lnx_b", f), None, ALU.add)
                    step(last)
                    step(mul(BN, BN, G_))
                    for f in range(4):
                        last = v.tensor_scalar(G_[:, f, :], G_[:, f, :], col("lnx_w", f), None, ALU.mult)
                    step(last)
                dve.wait_ge(sem("rk_inner"), tt + 1)
                tt_(R_[:, :, tok], R_[:, :, tok], bank(7).rearrange("p (f t) -> p f t", f=4), ALU.add)\
                    .then_inc(sem("rk_inner_taken"), 1)
                dve.wait_ge(sem("rk_inner_copied"), tt + 1)
                for c in range(2):
                    gc = 2 * tt + c
                    if gc in (1, 3):
                        dve.wait_ge(sem("rk_carried"), 1 + tt)
                        t = slice(gc * CH, (gc + 1) * CH) if gc == 1 else tok
                        o = slice(CH, P) if gc == 1 else slice(0, P)
                        for q in range(2):
                            rows = slice(HD * q, HD * (q + 1))
                            part = bank(6 + q)[rows, :].rearrange("p (f t) -> p f t", f=4)[:, :, o]
                            last = tt_(KK[rows, :, t], KK[rows, :, t], part, ALU.add)
                        if gc == 3:
                            last.then_inc(sem("rk_out"), 1)
                            continue
                    dve.wait_ge(sem("rk_update"), gc + 1)
                    g_ = chunk_decay[:, :, gc:gc + 1].to_broadcast([P, 4, HD])
                    new = bank(5)[:, 0:4 * HD].rearrange("p (f v) -> p f v", f=4)
                    if gc:
                        step(tt_(state, state, new, ALU.add))
                        for q in range(2):
                            rows = slice(HD * q, HD * (q + 1))
                            old = bank(1 + q)[rows, 0:4 * HD].rearrange("p (f v) -> p f v", f=4)
                            last = tt_(state[rows], state[rows], old, ALU.add)
                        step(last)
                        if gc == 1:
                            step(mul(state, state, g_))
                            v.memset(small[:, 62:63], 0.0).then_inc(sem("rk_state"), 1)
                        else:
                            mul(state, state, g_).then_inc(sem("rk_state"), 1)
                    else:
                        mul(state, new, g_).then_inc(sem("rk_state"), 1)
                        dve.wait_ge(sem("rk_state"), 1)
                    if gc == 1:
                        v.memset(small[:, 61:62], 0.0).then_inc(sem("rk_tile_done"), 1)
            dve.wait_ge(sem("rk_moments"), 1)
            step(v.scalar_tensor_tensor(out=flat(KK), in0=bank(0, 2), scalar=-1.0 / HD, in1=flat(KK), op0=ALU.mult,
                                        op1=ALU.add))
            mul(TM, KK, KK).then_inc(sem("rk_centred"), 1)
            split_slab(START["branch"] + 3)
            dve.wait_ge(sem("gates_moved"), 14 * 16)
            dve.wait_ge(multiplied, START["branch"] + 1)
            mul(merged[:, 0:4], tiles_of(4, 4), gates[0][:, 0:4]).then_inc(sem("branch_taken"), 1)
            dve.wait_ge(sem("rk_root"), 1)
            step(mul(KK, KK, TM))
            step(mul(KK, KK, G_))
            tt_(KK, KK, BN, ALU.add).then_inc(sem("rk_y_out"), 1)
            dve.wait_ge(sem("rk_y_out"), 1)
            operand(flat(XL[:, 16:20]), flat(KK), flat(XH[:, 16:20]))

            dve.wait_ge(sem("operand_lo"), KT + 3)
            split_slab(START["branch"] + 4)
            for j in range(1, 6):
                dve.wait_ge(multiplied, START["branch"] + j + 1)
                n, half = divmod(j, 2)
                for part, (a, b) in enumerate(((0, 2), (2, 4)) if j == 5 else ((0, 4),)):
                    out = merged[:, 4 * half + a:4 * half + b]
                    upper, first = divmod(4 * j, 12)
                    g_ = gates[upper][:, first + a:first + b]
                    src = tiles_of((4, 6, 0)[j % 3], 4)[:, a:b]
                    if n == 0:
                        mul(out, src, g_).then_inc(sem("branch_taken"), 1)
                    else:
                        step(mul(gated[:, a:b], src, g_))
                        tt_(out, out, gated[:, a:b], ALU.add).then_inc(sem("branch_taken"), 1)
                    dve.wait_ge(sem("branch_taken"), j + 1 + part)
                    if j == 5 and part == 0:
                        operand(flat(XL[:, 0:4]), flat(merged[:, 0:4]), flat(XH[:, 0:4]))
                if j in (1, 3):
                    split_slab(START["branch"] + {1: 5, 3: 6}[j])
            for a in (4, 6):
                operand(flat(XL[:, a:a + 2]), flat(merged[:, a:a + 2]), flat(XH[:, a:a + 2]))
            split_slab(START["branch"] + 7)
            norm_factor()
            v.memset(small[:, 57:58], 0.0).then_inc(sem("mem_factor"), 1)

            def memory_operand():
                dve.wait_ge(sem("mem_scaled"), 1)
                operand_tiles(range(KT), squares, ("norm_mem", 0), 8)

            residual("mix_out", ("norm_ca", 0), 4, before={2: memory_operand})

            for j in range(4):
                split_slab(START["ca_k"] + j + 2)
                take("ca_k", j, ca_k[:, 2 * j:2 * j + 2], False)
            for j in range(4):
                split_slab(START["ca_v"] + j + 2)
                take("ca_v", j, ca_v[:, :, j * T:(j + 1) * T], False)
            for j in range(4):
                split_slab(START["ca_q"] + j + 2)
                if j == 0:
                    norm_factor()
                take("ca_q", j, ca_q[:, 2 * j:2 * j + 2])
            for tt in range(2):
                i = slice(4 * tt, 4 * tt + 4)
                dve.wait_ge(sem("ca_scores"), tt + 1)
                step(v.tensor_reduce(small[:, i], tiles_of(0, 8)[:, i, :], AX.X, ALU.max))
                v.tensor_scalar(small[:, 8 + 4 * tt:12 + 4 * tt], small[:, i], -1.0 / 16, None, ALU.mult)\
                 .then_inc(sem("ca_max"), 1)
            for tt in range(2):
                dve.wait_ge(sem("ca_exp"), tt + 1)
                r = small[:, 24 + 4 * tt:28 + 4 * tt]
                step(v.reciprocal(r, small[:, 16 + 4 * tt:20 + 4 * tt]))
                p_ = probs[:, 4 * tt:4 * tt + 4]
                mul(p_, p_, r.unsqueeze(2).to_broadcast([P, 4, T])).then_inc(sem("ca_probs"), 1)
            for h in range(4):
                dve.wait_ge(sem("ca_out"), h + 1)
                operand(flat(XL[:, 8 + 2 * h:10 + 2 * h]), bank(h), flat(XH[:, 8 + 2 * h:10 + 2 * h]))
            residual("ca_o", ("norm_ffn", 0))

            feed_forward("ffn_c", conv=True)
            down("ffn_c", None, scale=1.0)
            norm_factor()
            def final(c):
                s_ = squares[:, 2 * c:2 * c + 2]
                step(mul(s_, H[:, 2 * c:2 * c + 2], over(inv[:, 0:T], 2)))
                for k in (2 * c, 2 * c + 1):
                    last_ = v.tensor_scalar(H[:, k, :], squares[:, k, :], col("norm_final", k), None, ALU.mult)
                last_.then_inc(sem("residual_ready"), 1)
            chunks(final, "final", ("norm_gains", 0))

            feed_forward("ffn_0")
            down("ffn_0", ("norm_gains", 8))

            split_slab(START["even_in"] + 2)
            split_slab(START["even_in"] + 3)
            norm_factor(True)
            tt_(small[:, 40:44], col("hgrn_lb", 0, 4), col("hgrn_lb", 0, 4), ALU.subtract).then_inc(sem("av_sums"), 1)
            dve.wait_ge(sem("av_root"), 1)
            step(v.reciprocal(small[:, 48:52], small[:, 44:48]))
            step(mul(small[:, 52:56], small[:, 44:48], small[:, 48:52]))
            step(tt_(small[:, 40:44], small[:, 52:56], small[:, 52:56], ALU.subtract))
            step(v.tensor_scalar(small[:, 40:44], small[:, 40:44], 0.0, 0.999, ALU.max, ALU.min))
            step(v.tensor_scalar(small[:, 44:48], small[:, 40:44], -1.0, 1.0, ALU.mult, ALU.add))
            for j in range(8):
                take("even_in", j, ev[:, 2 * j:2 * j + 2])
                if j:
                    split_slab(START["even_in"] + j + 3)
                if j == 4:
                    dve.wait_ge(sem("spatial_landed"), 48)
                    step(mul(spatial_w, spatial_w, per_head("upto", 8)))
                if j == 6:
                    dve.wait_ge(sem("even_active"), 1)
                    for h in range(4):
                        last = v.tensor_scalar(BF[:, h, :], BF[:, h, :], small[:, 44 + h:45 + h],
                                               small[:, 40 + h:41 + h], ALU.mult, ALU.add)
                    step(last)
                    step(v.tensor_scalar(flat(KB), flat(BF), -1.0, 1.0, ALU.mult, ALU.add))
                    v.tensor_scalar(flat(BF), flat(BF), 1e-6, None, ALU.max).then_inc(sem("gl_forget"), 1)
            avf = AV.rearrange("p a b -> p (a b)")
            avh = avf.rearrange("p (n d) -> p n d", d=HD)
            for j in range(4):
                take_by_token("even_v", j, [AV, BI][j // 2][:, :, j % 2 * T:(j % 2 + 1) * T])
                split_slab(START["even_v"] + j + 3)
                if j == 0:
                    dve.wait_ge(sem("gl_log"), 1)
                    for h in range(4):
                        for tt in range(2):
                            t = slice(tt * P, (tt + 1) * P)
                            last = v.tensor_tensor_scan(BC[:, h, t], table("ones"), BF[:, h, t], 0.0, ALU.mult,
                                                        ALU.add)
                    last.then_inc(sem("gl_factors"), 1)
                if j == 1:
                    dve.wait_ge(sem("even_active"), 3)
                    step(mul(flat(DIF[0]), avf, avf))
                    v.tensor_reduce(small[:, 0:16], flat(DIF[0]).rearrange("p (n d) -> p n d", d=HD), AX.X, ALU.add)\
                     .then_inc(sem("av_sums"), 1)
                if j == 2:
                    dve.wait_ge(sem("av_root"), 2)
                    step(v.reciprocal(small[:, 0:16], small[:, 16:32]))
                    step(mul(avh, avh, small[:, 0:16].unsqueeze(2).to_broadcast([P, 16, HD])))
                    mul(AV, AV, v_gain[:, 0, :].unsqueeze(1).to_broadcast([P, 2, W])).then_inc(sem("spatial_ready"), 1)
            dve.wait_ge(sem("spatial_mixed"), 1)
            mul(flat(AU), flat(AU), bank(0, 2)).then_inc(sem("mixed_gated"), 1)
            dve.wait_ge(sem("mixed_gated"), 1)

            def gl_mask(li):
                dve.wait_ge(sem("gl_pairs"), li + 1)
                if li == 8:
                    v.tensor_copy(AC, bank(2).rearrange("p (h t) -> p h t", h=4)).then_inc(sem("gl_added"), 1)
                    return
                src = bank(2 + 2 * (li % 2), 2).rearrange("p (h t) -> p h t", t=P)
                b = LEVELS[li - 1] if li else 0
                if b >= 32:
                    for r in range(0, P, 2 * b):
                        last_ = v.tensor_copy(AT[r:r + b, :, r + b:r + 2 * b], src[r:r + b, :, r + b:r + 2 * b])
                elif li == 0:
                    last_ = mul(AT, src, per_head("identity", 8))
                else:
                    step(mul(AM, src, per_head(f"level{b}", 8)))
                    last_ = tt_(AT, AT, AM, ALU.add)
                last_.then_inc(sem("gl_added"), 1)
                dve.wait_ge(sem("gl_added"), li + 1)

            def gl_factor(li):
                b = LEVELS[li - 1] if li < 8 else P
                dve.wait_ge(sem("gl_exp"), li)
                if li >= 2:
                    dve.wait_ge(sem("gl_pairs"), li - 1)
                blocks = [flat(a).rearrange("p (n c) -> p n c", c=2 * b) for a in (XM[li % 2], DIF[li % 2], KB, BQ)]
                x, e, k, q = blocks
                mul(x[:, :, 0:b], e[:, :, 0:b], k[:, :, 0:b])
                mul(x[:, :, b:2 * b], e[:, :, b:2 * b], q[:, :, b:2 * b]).then_inc(sem("gl_factors"), 1)

            for li in range(1, 9):
                gl_factor(li)
                gl_mask(li - 1)
                if li == 1:
                    operand(flat(XL[:, 8:12]), flat(AU), flat(XH[:, 8:12]))
            gl_mask(8)
            for h in range(2):
                s_ = slice(2 * h, 2 * h + 2)
                dve.wait_ge(sem("gl_root"), h + 1)
                step(v.scalar_tensor_tensor(out=flat(BC[:, s_]), in0=flat(BC[:, s_]), scalar=col("hgrn_out_norm"),
                                            in1=flat(DIF[0][:, s_]), op0=ALU.mult, op1=ALU.mult))
                mul(BC[:, s_], BC[:, s_], BG[:, s_]).then_inc(sem("gl_y"), 1)
            for h in range(2):
                s_ = slice(2 * h, 2 * h + 2)
                dve.wait_ge(sem("gl_y"), h + 1)
                operand(flat(XL[:, 12 + 2 * h:14 + 2 * h]), flat(BC[:, s_]), flat(XH[:, 12 + 2 * h:14 + 2 * h]))
            residual("even_out", ("norm_gains", 16), ahead=3)

            def embedding(n):
                dve.wait_ge(sem("ple_landed"), 16 * (n + 1))
                operand(flat(XL[:, 8:10]), flat(ple_in), flat(XH[:, 8:10]))

            def per_layer(name, n, gain):
                g0 = START[name]
                split_slab(g0 + 2)
                split_slab(g0 + 3)
                norm_factor()
                dve.wait_ge(sem("ple_copied"), n + 1)
                for c in range(4):
                    s_ = slice(2 * c, 2 * c + 2)
                    dve.wait_ge(multiplied, g0 + 2 + c)
                    mul(ple_g[:, s_], tiles_of(3 + c, 2), over(inv[:, 0:T], 2)).then_inc(sem("ple_gate_scaled"), 1)
                    if c < 2:
                        split_slab(g0 + 4 + c)
                    dve.wait_ge(sem("ple_gated"), 4 * n + c + 1)
                    mul(ple_p[:, s_], ple_p[:, s_], ple_g[:, s_]).then_inc(sem("ple_product"), 1)
                split_slab(g0 + 6)
                dve.wait_ge(sem("ple_root"), n + 1)
                step(v.reciprocal(inv[:, 0:T], root[:, 0:T]))

                def add(c):
                    s_ = ple_add[:, 2 * c:2 * c + 2]
                    dve.wait_ge(sem("ple_gained"), 4 * n + c + 1)
                    step(mul(s_, s_, over(inv[:, 0:T], 2)))
                    tt_(chunk(c), chunk(c), flat(s_), ALU.add).then_inc(sem("residual_ready"), 1)
                chunks(add, name, gain)

            embedding(0)
            feed_forward("ffn_1")
            down("ffn_1", ("norm_gains", 24))
            per_layer("ple_0", 0, ("norm_gains", 40))
            feed_forward("ffn_2")
            down("ffn_2", ("norm_gains", 48))

            split_slab(START["mla_in"] + 2)
            split_slab(START["mla_in"] + 3)
            norm_factor()
            take("mla_in", 0, MI[:, 0:2])
            take("mla_in", 1, MI[:, 2:4])
            dve.wait_ge(sem("output_taken"), taken[0])
            operand_tiles((0, 1), MI, ("q_a_norm", 0), 8)
            operand_tiles((2,), MI, ("q_a_norm", 0), 8)
            split_slab(START["mla_in"] + 4)
            take("mla_in", 2, MI[:, 4:6])
            dve.wait_ge(sem("output_taken"), taken[0])
            operand_tiles((0, 1), MI[:, 3:5], ("kv_a_norm", 0), 11)
            split_slab(START["mla_in"] + 5)
            dve.wait_ge(sem("positions_landed"), 16)
            two_pi = 2 * np.pi
            magic = 1.5 * 2.0 ** 23
            c1 = 6.28125
            c2 = float(np.float32(two_pi - c1))
            c2 = float(np.round(c2 * 2 ** 20) / 2 ** 20)
            c3 = float(two_pi - c1 - c2)
            a_, n_ = flat(ang), flat(turns)
            step(v.tensor_copy(a_, cosines.bitcast(I32)[:, 0, :]))
            step(v.tensor_scalar(a_, a_, col("inv_freq"), None, ALU.mult))
            step(v.tensor_scalar(n_, a_, 1 / two_pi, None, ALU.mult))
            step(v.tensor_scalar(n_, n_, magic, None, ALU.add))
            step(v.tensor_scalar(n_, n_, -magic, None, ALU.add))
            for c in (c1, c2, c3):
                step(v.scalar_tensor_tensor(out=a_, in0=n_, scalar=-c, in1=a_, op0=ALU.mult, op1=ALU.add))
            limit = 3.1415925
            v.tensor_scalar(flat(sines), a_, limit, -limit, ALU.min, ALU.max)
            step(v.tensor_scalar(a_, a_, np.pi / 2, None, ALU.add))
            step(v.tensor_scalar(n_, a_, np.pi, -two_pi, ALU.is_gt, ALU.mult))
            step(tt_(a_, a_, n_, ALU.add))
            v.tensor_scalar(flat(cosines), a_, limit, -limit, ALU.min, ALU.max).then_inc(sem("angles"), 1)
            for pick in (pick_head, pick_pair):
                flat_pick = pick.rearrange("p h c -> p (h c)").rearrange("p (h c) -> p h c", h=8)
                last = v.tensor_copy(flat_pick, table("identity")[0:8, 0:8].unsqueeze(2)
                                     .to_broadcast([8, 8, flat_pick.shape[-1]]))
            dve.wait_ge(sem("latent_roots"), 1)
            step(v.reciprocal(latent_rs[:, 0, :], latent_rs[:, 0, :]))

            def take_q(j):
                dve.wait_ge(multiplied, START["mla_q"] + j + 1)
                mul(MQ[:, 4 * j:4 * j + 4], tiles_of(2 * j, 4), over(latent_rs[:, 0, :], 4))\
                    .then_inc(sem("mla_taken"), 1)

            take_q(0)
            split_slab(START["mla_q"] + 3)
            take_q(1)
            step(v.reciprocal(latent_rs[:, 1, :], latent_rs[:, 1, :]))
            step(v.reciprocal(small[:, 38:40], small[:, 36:38]))
            split_slab(START["mla_q"] + 4)
            take_q(2)
            split_slab(START["mla_kv"] + 2)
            dve.wait_ge(multiplied, START["mla_kv"] + 1)
            mul(MK, tiles_of(0, 8), over(latent_rs[:, 1, :], 8)).then_inc(sem("mla_taken"), 1)
            qr, kr = MQ[:, 8:12], MI[:, 0:1]
            dve.wait_ge(sem("mla_squares"), 1)
            v.tensor_scalar(flat(qr), flat(qr), col("q_rope"), None, ALU.mult)
            v.tensor_scalar(flat(kr), flat(MI[:, 5:6]), col("k_rope"), None, ALU.mult).then_inc(sem("mla_rope_in"), 1)
            dve.wait_ge(sem("head_roots"), 1)
            v.reciprocal(head_rs[:, 0:T], head_rs[:, 0:T]).then_inc(sem("head_rs"), 1)
            dve.wait_ge(sem("angles_done"), 1)
            dve.wait_ge(sem("mla_swapped"), 2)
            rot = KRP[:, 0:5]
            mul(rot[:, 0:4], tiles_of(1, 4), over(sines[:, 0, :], 4))
            mul(rot[:, 4:5], tiles_of(3, 1), sines).then_inc(sem("mla_rotated"), 1)
            mul(qr, qr, over(cosines[:, 0, :], 4))
            step(mul(kr, kr, cosines))
            tt_(qr, qr, rot[:, 0:4], ALU.add)
            step(tt_(kr, kr, rot[:, 4:5], ALU.add))
            dve.wait_ge(sem("head_roots"), 2)
            v.reciprocal(head_rs[:, T:2 * T], head_rs[:, T:2 * T]).then_inc(sem("head_rs"), 1)
            split_slab(START["mla_kv"] + 3)
            dve.wait_ge(sem("mla_taken"), 5)
            step(v.memset(flat(KRP), 0.0))
            dve.wait_ge(sem("mla_factors"), 1)
            mul(qr, qr, tiles_of(0, 4))

            def scale_heads(x, gain, e):
                return v.scalar_tensor_tensor(out=flat(x[:, 4 * e:4 * e + 4]), in0=flat(x[:, 4 * e:4 * e + 4]),
                                              scalar=col(gain), in1=bank(4 + 2 * e, 2), op0=ALU.mult, op1=ALU.mult)

            for e in range(2):
                dve.wait_ge(sem("mla_factors"), 2 + e)
                last = scale_heads(MQ, "q_nope", e)
            last.then_inc(sem("mla_q_scaled"), 1)
            dve.wait_ge(sem("mla_factors"), 4)
            for q in range(2):
                rows = slice(HD * q, HD * (q + 1))
                mul(KRP[rows, q:8:2, :], tiles_of(2, 4)[rows], kr[rows, 0, :].unsqueeze(1).to_broadcast([HD, 4, T]))
            for e in range(2):
                dve.wait_ge(sem("mla_factors"), 5 + e)
                scale_heads(MK, "k_nope", e).then_inc(sem("mla_qk"), 1)
            for e in range(2):
                h_ = slice(4 * e, 4 * e + 4)
                late = tiles_of(2 + 2 * e, 4)
                dve.wait_ge(sem("mla_scores"), e + 1)
                v.tensor_copy(S1[:, h_, 0:P], late[:, :, 0:P])
                tt_(S1[:, h_, P:T], late[:, :, P:T], per_head("future_penalty"), ALU.add)
                step(tt_(S0[:, h_], bank(e).rearrange("p (h s) -> p h s", s=P), per_head("future_penalty"), ALU.add))
                v.tensor_reduce(small[:, 4 * e:4 * e + 4], S0[:, h_], AX.X, ALU.max)
                step(v.tensor_reduce(small[:, 8 + 4 * e:12 + 4 * e], S1[:, h_], AX.X, ALU.max))
                for m in (4 * e, 8 + 4 * e):
                    last = v.tensor_scalar(small[:, m:m + 4], small[:, m:m + 4], -(192 ** -0.5), None, ALU.mult)
                last.then_inc(sem("mla_max"), 1)
            for e in range(2):
                h_ = slice(4 * e, 4 * e + 4)
                dve.wait_ge(sem("mla_exp"), e + 1)
                sums = [small[:, m + 4 * e:m + 4 + 4 * e] for m in (16, 24)]
                for m in sums:
                    last = v.reciprocal(m, m)
                step(last)
                mul(S0[:, h_], S0[:, h_], sums[0].unsqueeze(2).to_broadcast([P, 4, P]))
                mul(S1[:, h_], S1[:, h_], sums[1].unsqueeze(2).to_broadcast([P, 4, T])).then_inc(sem("mla_probs"), 1)
            for f in range(4):
                dve.wait_ge(sem("mla_out"), f + 1)
                operand(flat(XL[:, 8 + 2 * f:10 + 2 * f]), bank(f), flat(XH[:, 8 + 2 * f:10 + 2 * f]))
            residual("mla_out", ("norm_gains", 56))

            embedding(1)
            feed_forward("ffn_3")
            down("ffn_3", ("norm_gains", 64))
            per_layer("ple_1", 1, None)


def by_output(w):
    n = w.shape[1] // (2 * P)
    return w.reshape(KT, P, n, 2, P).transpose(2, 1, 3, 0, 4).reshape(n, P, SLAB)


def by_token(w):
    n = w.shape[1] // (2 * P)
    return w.reshape(KT, P, n, 2 * P).transpose(2, 1, 0, 3).reshape(n, P, SLAB)


def by_input(w):
    n = w.shape[0] // (2 * P)
    return w.reshape(n, 2, P, D).transpose(0, 2, 1, 3).reshape(n, P, SLAB)


def feed_forward(first, second, down):
    a, b, c = by_output(first), by_output(second), by_input(down)
    out = [a[0], b[0]]
    for i in range(1, FP):
        out += [a[i], b[i], c[i - 1]]
    return np.stack(out + [c[FP - 1]])


def kernel(**inputs):
    import concourse.bacc as _bacc
    from concourse.bass_utils import run_bass_kernel_spmd as _run

    a = {n: np.asarray(v) for n, v in inputs.items()}
    wc = a["w_comb"][0]
    conv_end, sb_end, gate_end = 3 * W, 6 * W, 6 * W + 3 * D
    ew = a["even_w_in_2"][0]
    mi = a["mla_w_in_2"][0]
    qb = a["mla_w_q_b_2"][0].reshape(3, P, HEADS, 192)
    kvb = a["mla_w_kv_b_2"][0].reshape(2, P, HEADS, 256)
    q_tiles = np.concatenate([
        qb[:, :, :, :P].transpose(0, 1, 2, 3),
        qb[:, :, :, P:].reshape(3, P, 4, P)], axis=2)
    q_slabs = q_tiles.reshape(3, P, 3, 4, P).transpose(2, 1, 3, 0, 4).reshape(3, P, 12 * P)
    q_slabs = np.concatenate([q_slabs, q_slabs[:, :, :4 * P]], axis=2)
    k_slab = kvb[:, :, :, :P].transpose(1, 2, 0, 3).reshape(1, P, SLAB)
    v_slab = kvb[:, :, :, P:].reshape(2, P, 1024).transpose(1, 0, 2).reshape(1, P, SLAB)
    ffw = [feed_forward(a["ffn_w_gate_2"][i, j], a["ffn_w_up_2"][i, j], a["ffn_w_down_2"][i, j])
           for i in range(2) for j in range(2)]
    parts = {
        "conv": by_output(wc[:, :conv_end]),
        "sb_qk": by_output(wc[:, conv_end:conv_end + 2 * W]),
        "sb_v": by_token(wc[:, conv_end + 2 * W:sb_end]),
        "gates": by_output(wc[:, sb_end:gate_end]),
        "rwkv": by_output(wc[:, gate_end:]),
        "branch": a["branch_proj"][0].reshape(3, 4, P, 2, 4, P).transpose(0, 3, 2, 4, 1, 5).reshape(6, P, SLAB),
        "mix_out": by_output(a["w_mix_out"][0]),
        "ca_k": by_output(a["ca_wkv"][0][:, :D]),
        "ca_v": by_token(a["ca_wkv"][0][:, D:]),
        "ca_q": by_output(a["ca_wq"][0]),
        "ca_o": by_output(a["ca_wo"][0]),
        "ffn_c": feed_forward(a["ffn_up"][0][:, :F], a["ffn_up"][0][:, F:], a["ffn_down"][0]),
        "ffn_0": ffw[0], "ffn_1": ffw[1], "ffn_2": ffw[2], "ffn_3": ffw[3],
        "even_in": by_output(np.concatenate([ew[:, :W], ew[:, 2 * W:4 * W], ew[:, 5 * W:]], axis=1)),
        "even_v": by_token(np.concatenate([ew[:, W:2 * W], ew[:, 4 * W:5 * W]], axis=1)),
        "even_out": by_output(a["even_w_out_2"][0]),
        "ple_0": np.concatenate([by_input(a["ple_w_proj_2"][0]), by_output(a["ple_w_gate_2"][0])]),
        "ple_1": np.concatenate([by_input(a["ple_w_proj_2"][1]), by_output(a["ple_w_gate_2"][1])]),
        "mla_in": by_output(np.concatenate([mi, mi[:, -HD:]], axis=1)),
        "mla_q": q_slabs,
        "mla_kv": np.concatenate([k_slab, v_slab]),
        "mla_out": by_output(a["mla_w_out_2"][0]),
    }
    for name, n in STREAM:
        assert parts[name].shape == (n, P, SLAB), name

    def cols(v):
        return np.ascontiguousarray(v).reshape(-1, P).T

    inv_freq = ROPE_THETA ** (-np.arange(0, HD, 2, dtype=np.float32) / np.float32(HD))
    qn, kn = a["mla_q_norm_2"][0], a["mla_k_norm_2"][0]
    tables = {
        "norm_mix": a["norm_mix"], "conv_w": a["conv_w"], "mu": a["mu_rwkv"], "w0": a["w0"], "a0": a["a0"],
        "k_k": a["k_k"], "k_a": a["k_a"], "r_k": a["r_k"], "lnx_w": a["lnx_w"], "lnx_b": a["lnx_b"],
        "gate_b": a["gate_b"], "norm_ca": a["norm_ca"], "norm_mem": a["norm_mem"], "norm_ffn": a["norm_ffn"],
        "ffn_conv_w": a["ffn_conv_w"], "ffn_conv_b": a["ffn_conv_b"], "norm_final": a["norm_final"],
        "norm_gains": a["norm_gains_2"], "hgrn_lb": a["hgrn_lb_raw_2"], "hgrn_out_norm": a["hgrn_out_norm_2"],
        "q_a_norm": a["mla_q_a_norm_2"], "kv_a_norm": a["mla_kv_a_norm_2"],
        "q_nope": qn[:P], "q_rope": np.concatenate([qn[P:], qn[P:]]),
        "k_nope": kn[:P], "k_rope": np.concatenate([kn[P:], kn[P:]]),
        "inv_freq": np.tile(inv_freq.astype(np.float32), 4),
    }
    arrays = {
        "w_stream": np.concatenate([parts[n] for n, _ in STREAM]),
        "x_t": a["x"][0].T,
        "mem_t": a["mem"][0].T,
        "ple_t": a["p_2"][:, 0].transpose(0, 2, 1),
        "params": np.concatenate([cols(tables[n]) for n, _ in COLUMNS], axis=1),
        "tables": constant_tables(),
        "wa_lora": np.concatenate([a["w_lora"][0], a["a_lora"][0]]),
        "g_lora": a["g_lora"][0],
        "spatial_t": a["gmlp_w_s_2"][0].transpose(2, 0, 1),
        "spatial_b": a["gmlp_b_s_2"].reshape(1, HEADS * P),
        "v_gain": a["gmlp_v_norm_2"].reshape(1, W),
        "positions": a["positions_2"].reshape(1, T),
    }
    nc = _bacc.Bacc("TRN2", target_bir_lowering=False, num_devices=1)
    ins, given = {}, {}
    for name, v in arrays.items():
        v = np.ascontiguousarray(v)
        given[f"in_{name}"] = v
        ins[name] = nc.dram_tensor(f"in_{name}", v.shape, mybir.dt.from_np(v.dtype), kind="ExternalInput").ap()
    out = nc.dram_tensor("out_t", (D, T), F32, kind="ExternalOutput").ap()
    ins["spilled_gates"] = nc.dram_tensor("spilled_gates", (12, P, 2 * T), F32).ap()
    program(nc, ins, out)
    r = _run(nc, [given], core_ids=[0])
    return np.ascontiguousarray(r.results[0]["out_t"].T)[None]
```
